# Optimizing a Trainium2 kernel written in Bass

```python
import math
import jax, jax.numpy as jnp
from jax import lax
import numpy as np

D_MODEL = 1024
BATCH = 1
SEQ = 512
DEPTH = 2

CHUNK = 64
N_MIXERS = 2
N_A = (DEPTH + 1) // 2
N_B = DEPTH // 2

D_RNN = D_MODEL
RG_BLOCKS = 4
RG_BW = D_RNN // RG_BLOCKS
CONV_W = 4
RG_C = 8.0

SB_HEADS = 16
SB_HEAD_DIM = D_MODEL // SB_HEADS
Q_BLOCK = 128

D_FF = int(math.ceil(8 * D_MODEL / 3 / 256) * 256)

RMS_EPS = 1e-6


def _rmsnorm(x, g):
    x32 = x.astype(jnp.float32)
    y = x32 * lax.rsqrt(jnp.mean(x32 * x32, axis=-1, keepdims=True) + RMS_EPS)
    return (y * g.astype(jnp.float32)).astype(x.dtype)

def _causal_depthwise_conv(x, w, b):
    c = x.shape[-1]
    y = lax.conv_general_dilated(
        x, w.astype(x.dtype)[:, None, :], window_strides=(1,),
        padding=[(CONV_W - 1, 0)], dimension_numbers=("NWC", "WIO", "NWC"),
        feature_group_count=c)
    return y + b.astype(x.dtype)

def _linear_scan(a, u):
    def combine(l, r):
        a_l, b_l = l
        a_r, b_r = r
        return a_l * a_r, a_r * b_l + b_r
    _, h = lax.associative_scan(combine, (a, u), axis=1)
    return h

def _rglru_mixer(h, w_in, conv_w, conv_b, w_r, b_r, w_i, b_i, lam, w_out):
    bsz, s, _ = h.shape
    proj = h @ w_in.astype(h.dtype)
    gate_br, x_br = proj[..., :D_RNN], proj[..., D_RNN:]
    gate = jax.nn.gelu(gate_br, approximate=True)
    xc = _causal_depthwise_conv(x_br, conv_w, conv_b)
    xg = xc.reshape(bsz, s, RG_BLOCKS, RG_BW).astype(jnp.float32)
    r = jax.nn.sigmoid(jnp.einsum("bsnc,ncd->bsnd", xg, w_r.astype(jnp.float32)).reshape(bsz, s, D_RNN)
                       + b_r.astype(jnp.float32))
    i = jax.nn.sigmoid(jnp.einsum("bsnc,ncd->bsnd", xg, w_i.astype(jnp.float32)).reshape(bsz, s, D_RNN)
                       + b_i.astype(jnp.float32))
    log_a = RG_C * r * jax.nn.log_sigmoid(lam.astype(jnp.float32))
    a = jnp.exp(log_a)
    mult = jnp.sqrt(jnp.maximum(-jnp.expm1(2.0 * log_a), 0.0))
    u = mult * (i * xc.astype(jnp.float32))
    hs = _linear_scan(a, u)
    y = (hs * gate.astype(jnp.float32)).astype(h.dtype)
    return y @ w_out.astype(h.dtype)

def _stick_breaking_attention(q, k, v):
    bsz, nh, s, dh = q.shape
    nq = s // Q_BLOCK
    scale = 1.0 / math.sqrt(dh)
    k32 = k.astype(jnp.float32)
    v32 = v.astype(jnp.float32)
    key_pos = jnp.arange(s)
    q_blocks = q.reshape(bsz, nh, nq, Q_BLOCK, dh).transpose(2, 0, 1, 3, 4)
    starts = jnp.arange(nq) * Q_BLOCK

    def block(args):
        qb, start = args
        z = jnp.einsum("bhqd,bhkd->bhqk", qb.astype(jnp.float32), k32) * scale
        q_pos = start + jnp.arange(Q_BLOCK)
        mask = key_pos[None, :] < q_pos[:, None]
        log_beta = jax.nn.log_sigmoid(z)
        log_1m = jnp.where(mask, jax.nn.log_sigmoid(-z), 0.0)
        suffix = lax.cumsum(log_1m, axis=3, reverse=True) - log_1m
        wts = jnp.where(mask, jnp.exp(log_beta + suffix), 0.0)
        return jnp.einsum("bhqk,bhkd->bhqd", wts, v32)

    out = lax.map(block, (q_blocks, starts))
    return out.transpose(1, 2, 0, 3, 4).reshape(bsz, nh, s, dh).astype(q.dtype)

def _sb_mixer(h, w_qkv, w_out):
    bsz, s, _ = h.shape
    qkv = (h @ w_qkv.astype(h.dtype)).reshape(bsz, s, 3, SB_HEADS, SB_HEAD_DIM)
    qkv = qkv.transpose(2, 0, 3, 1, 4)
    o = _stick_breaking_attention(qkv[0], qkv[1], qkv[2])
    o = o.transpose(0, 2, 1, 3).reshape(bsz, s, D_MODEL)
    return o @ w_out.astype(h.dtype)

def _swiglu(h, w_gate, w_up, w_down):
    g = h @ w_gate.astype(h.dtype)
    u = h @ w_up.astype(h.dtype)
    return (jax.nn.silu(g) * u) @ w_down.astype(h.dtype)

def first_inputs(seed: int = 0) -> dict:
    key = jax.random.key(seed)
    ks = jax.random.split(key, 20)
    f32 = jnp.float32

    def nrm(k, shape, fan_in):
        return jax.random.normal(k, shape, f32) * (fan_in ** -0.5)

    a0 = jax.random.uniform(ks[10], (N_A, D_RNN), f32, 0.9, 0.999)
    base = a0 ** (1.0 / RG_C)
    lam = jnp.log(base) - jnp.log1p(-base)

    return {
        "x": jax.random.normal(ks[0], (BATCH, SEQ, D_MODEL), f32),
        "norm_mix_g": 1.0 + 0.02 * jax.random.normal(ks[1], (DEPTH, D_MODEL), f32),
        "norm_ffn_g": 1.0 + 0.02 * jax.random.normal(ks[2], (DEPTH, D_MODEL), f32),
        "a_w_in": nrm(ks[3], (N_A, D_MODEL, 2 * D_RNN), D_MODEL),
        "a_conv_w": nrm(ks[4], (N_A, CONV_W, D_RNN), CONV_W),
        "a_conv_b": 0.01 * jax.random.normal(ks[5], (N_A, D_RNN), f32),
        "a_w_r": nrm(ks[6], (N_A, RG_BLOCKS, RG_BW, RG_BW), RG_BW),
        "a_b_r": 0.01 * jax.random.normal(ks[7], (N_A, D_RNN), f32),
        "a_w_i": nrm(ks[8], (N_A, RG_BLOCKS, RG_BW, RG_BW), RG_BW),
        "a_b_i": 0.01 * jax.random.normal(ks[9], (N_A, D_RNN), f32),
        "a_lambda": lam,
        "a_w_out": nrm(ks[11], (N_A, D_RNN, D_MODEL), D_RNN),
        "b_w_qkv": nrm(ks[12], (N_B, D_MODEL, 3 * D_MODEL), D_MODEL),
        "b_w_out": nrm(ks[13], (N_B, D_MODEL, D_MODEL), D_MODEL),
        "ffn_w_gate": nrm(ks[14], (DEPTH, D_MODEL, D_FF), D_MODEL),
        "ffn_w_up": nrm(ks[15], (DEPTH, D_MODEL, D_FF), D_MODEL),
        "ffn_w_down": nrm(ks[16], (DEPTH, D_FF, D_MODEL), D_FF),
        "final_g": 1.0 + 0.02 * jax.random.normal(ks[17], (D_MODEL,), f32),
    }

def first_block(x, norm_mix_g, norm_ffn_g, a_w_in, a_conv_w, a_conv_b, a_w_r, a_b_r,
              a_w_i, a_b_i, a_lambda, a_w_out, b_w_qkv, b_w_out,
              ffn_w_gate, ffn_w_up, ffn_w_down, final_g):
    for layer in range(DEPTH):
        h = _rmsnorm(x, norm_mix_g[layer])
        if layer % N_MIXERS == 0:
            j = layer // N_MIXERS
            mix = _rglru_mixer(h, a_w_in[j], a_conv_w[j], a_conv_b[j], a_w_r[j], a_b_r[j],
                               a_w_i[j], a_b_i[j], a_lambda[j], a_w_out[j])
        else:
            j = layer // N_MIXERS
            mix = _sb_mixer(h, b_w_qkv[j], b_w_out[j])
        x = x + mix
        h = _rmsnorm(x, norm_ffn_g[layer])
        x = x + _swiglu(h, ffn_w_gate[layer], ffn_w_up[layer], ffn_w_down[layer])
    return _rmsnorm(x, final_g)


DEPTH_2 = 1

GRID_W = 64
HEAD_DIM = 64
NA_HEADS = 8
NA_KH_MAX = 8
NA_KW = 16
NA_QBLK = 16
NA_BAND = 2 * NA_KW
NA_W = NA_HEADS * HEAD_DIM
GQA_HEADS = 8
GQA_KV_HEADS = 2
GQA_QBLK = 128
ROPE_THETA = 10000.0
GQA_Q_W = GQA_HEADS * HEAD_DIM
GQA_KV_W = GQA_KV_HEADS * HEAD_DIM
MEM_TOKENS = 256
MEM_HEADS = 4
MEM_HEAD_DIM = 128
MEM_W = MEM_HEADS * MEM_HEAD_DIM
N_BRANCH = 3
BRANCH_WIDTH = 512
GATE_W = N_BRANCH * D_MODEL
IN_W = 3 * NA_W + GQA_Q_W + 2 * GQA_KV_W + MEM_W + GATE_W
N_EXPERTS = 16
EC_CAPACITY_FACTOR = 2
D_FF_EXPERT = 1024
LN_EPS = 1e-5
DN_ALPHA = (2 * DEPTH_2) ** 0.25
DN_BETA = (8 * DEPTH_2) ** -0.25
NEG_INF = -1e30


def _split_points():
    sizes = (NA_W, NA_W, NA_W, GQA_Q_W, GQA_KV_W, GQA_KV_W, MEM_W)
    return tuple(int(v) for v in np.cumsum(sizes))

def layer_norm(x, g, b):
    xf = x.astype(jnp.float32)
    mu = jnp.mean(xf, axis=-1, keepdims=True)
    var = jnp.mean(jnp.square(xf - mu), axis=-1, keepdims=True)
    return ((xf - mu) * lax.rsqrt(var + LN_EPS) * g.astype(jnp.float32) + b.astype(jnp.float32)).astype(x.dtype)

def rms_norm(x, g):
    xf = x.astype(jnp.float32)
    ms = jnp.mean(jnp.square(xf), axis=-1, keepdims=True)
    return (xf * lax.rsqrt(ms + RMS_EPS) * g.astype(jnp.float32)).astype(x.dtype)

def axial_rope_tables(seq_len):
    t = jnp.arange(seq_len)
    row = (t // GRID_W).astype(jnp.float32)
    col = (t % GRID_W).astype(jnp.float32)
    half = HEAD_DIM // 2
    inv = ROPE_THETA ** (-jnp.arange(0, half, 2, dtype=jnp.float32) / half)
    ang = jnp.concatenate([row[:, None] * inv, col[:, None] * inv], axis=-1)
    return jnp.cos(ang), jnp.sin(ang)

def apply_rope(x, cos, sin):
    xf = x.astype(jnp.float32)
    x1, x2 = xf[..., 0::2], xf[..., 1::2]
    c, s = cos[None, :, None, :], sin[None, :, None, :]
    out = jnp.stack([x1 * c - x2 * s, x1 * s + x2 * c], axis=-1).reshape(x.shape)
    return out.astype(x.dtype)

def neighbourhood_attention(q, k, v, rpb):
    S, H, dh = q.shape
    rows = S // GRID_W
    kh = min(NA_KH_MAX, rows)
    ncb = GRID_W // NA_QBLK
    qg = q.reshape(rows, ncb, NA_QBLK, H, dh)
    kg = k.reshape(rows, GRID_W, H, dh)
    vg = v.reshape(rows, GRID_W, H, dh)
    r = jnp.arange(rows)
    row_start = jnp.clip(r - kh // 2, 0, rows - kh)
    key_rows = row_start[:, None] + jnp.arange(kh)
    cb = jnp.arange(ncb)
    band_start = jnp.clip(cb * NA_QBLK - NA_KW // 2, 0, GRID_W - NA_BAND)
    key_cols = band_start[:, None] + jnp.arange(NA_BAND)
    ri = key_rows[:, None, :, None]
    ci = key_cols[None, :, None, :]
    k_blk = kg[ri, ci]
    v_blk = vg[ri, ci]
    qcol = cb[:, None] * NA_QBLK + jnp.arange(NA_QBLK)
    col_start = jnp.clip(qcol - NA_KW // 2, 0, GRID_W - NA_KW)
    kc = key_cols[:, None, :]
    in_win = (kc >= col_start[:, :, None]) & (kc < col_start[:, :, None] + NA_KW)
    dr = key_rows - r[:, None]
    dc = jnp.clip(kc - qcol[:, :, None] + NA_KW - 1, 0, 2 * NA_KW - 2)
    bias = rpb[:, (dr + NA_KH_MAX - 1)[:, None, None, :, None], dc[None, :, :, None, :]]
    scores = jnp.einsum('rcqhd,rckwhd->hrcqkw', qg, k_blk,
                        preferred_element_type=jnp.float32) * (1.0 / math.sqrt(dh))
    scores = jnp.where(in_win[None, None, :, :, None, :], scores + bias.astype(jnp.float32), NEG_INF)
    p = jax.nn.softmax(scores, axis=(-2, -1))
    out = jnp.einsum('hrcqkw,rckwhd->rcqhd', p.astype(v.dtype), v_blk)
    return out.reshape(S, H * dh)

def gqa_attention(q, k, v, q_gain, k_gain, cos, sin):
    q = apply_rope(rms_norm(q, q_gain), cos, sin)
    k = apply_rope(rms_norm(k, k_gain), cos, sin)
    B, S, Hq, dh = q.shape
    hkv = k.shape[2]
    grp = Hq // hkv
    nblk = S // GQA_QBLK
    qb = q.reshape(B, nblk, GQA_QBLK, hkv, grp, dh).transpose(1, 0, 3, 4, 2, 5)
    scale = 1.0 / math.sqrt(dh)

    def block(qi):
        s = jnp.einsum('bkgqd,bskd->bkgqs', qi, k, preferred_element_type=jnp.float32) * scale
        p = jax.nn.softmax(s, axis=-1)
        return jnp.einsum('bkgqs,bskd->bqkgd', p.astype(v.dtype), v)

    out = lax.map(block, qb)
    return out.transpose(1, 0, 2, 3, 4, 5).reshape(B, S, Hq * dh)

def memory_attention(q, mk, mv):
    B, S, H, dm = q.shape
    s = jnp.einsum('bshd,bmhd->bhsm', q, mk, preferred_element_type=jnp.float32) * (1.0 / math.sqrt(dm))
    p = jax.nn.softmax(s, axis=-1)
    return jnp.einsum('bhsm,bmhd->bshd', p.astype(mv.dtype), mv).reshape(B, S, H * dm)

def expert_choice_ffn(x, w_router, w_gate_up, w_down):
    B, T, D = x.shape
    cap = EC_CAPACITY_FACTOR * T // N_EXPERTS
    logits = jnp.einsum('btd,de->bte', x, w_router, preferred_element_type=jnp.float32)
    aff = jax.nn.softmax(logits, axis=-1)
    gate, idx = lax.top_k(jnp.swapaxes(aff, 1, 2), cap)
    bidx = jnp.arange(B)[:, None, None]
    xs = x[bidx, idx]
    h = jnp.einsum('becd,edf->becf', xs, w_gate_up)
    hg, hu = jnp.split(h, 2, axis=-1)
    ye = jnp.einsum('becf,efd->becd', jax.nn.silu(hg) * hu, w_down)
    ye = ye * gate[..., None].astype(ye.dtype)
    return jnp.zeros_like(x).at[bidx, idx].add(ye)

def second_inputs(seed: int = 0) -> dict:
    key = jax.random.key(seed)
    ks = jax.random.split(key, 20)

    def nrm(k, shape, scale):
        return jax.random.normal(k, shape, jnp.float32) * scale

    return {
        "x": nrm(ks[0], (BATCH, SEQ, D_MODEL), 1.0),
        "mem": nrm(ks[1], (BATCH, MEM_TOKENS, D_MODEL), 1.0),
        "w_in": nrm(ks[2], (DEPTH_2, D_MODEL, IN_W), D_MODEL ** -0.5),
        "b_gate": nrm(ks[3], (DEPTH_2, GATE_W), 0.1),
        "na_rpb": nrm(ks[4], (DEPTH_2, NA_HEADS, 2 * NA_KH_MAX - 1, 2 * NA_KW - 1), 0.05),
        "gqa_q_gain": 1.0 + nrm(ks[5], (DEPTH_2, HEAD_DIM), 0.1),
        "gqa_k_gain": 1.0 + nrm(ks[6], (DEPTH_2, HEAD_DIM), 0.1),
        "w_mem_kv": nrm(ks[7], (DEPTH_2, D_MODEL, 2 * MEM_W), D_MODEL ** -0.5),
        "w_branch": nrm(ks[8], (DEPTH_2, N_BRANCH, BRANCH_WIDTH, D_MODEL), BRANCH_WIDTH ** -0.5),
        "w_out": nrm(ks[9], (DEPTH_2, D_MODEL, D_MODEL), D_MODEL ** -0.5 * DN_BETA),
        "ln1_g": 1.0 + nrm(ks[10], (DEPTH_2, D_MODEL), 0.1),
        "ln1_b": nrm(ks[11], (DEPTH_2, D_MODEL), 0.02),
        "w_router": nrm(ks[12], (DEPTH_2, D_MODEL, N_EXPERTS), D_MODEL ** -0.5),
        "w_gate_up": nrm(ks[13], (DEPTH_2, N_EXPERTS, D_MODEL, 2 * D_FF_EXPERT), D_MODEL ** -0.5),
        "w_down": nrm(ks[14], (DEPTH_2, N_EXPERTS, D_FF_EXPERT, D_MODEL), D_FF_EXPERT ** -0.5 * DN_BETA),
        "ln2_g": 1.0 + nrm(ks[15], (DEPTH_2, D_MODEL), 0.1),
        "ln2_b": nrm(ks[16], (DEPTH_2, D_MODEL), 0.02),
    }

def second_block(x, mem, w_in, b_gate, na_rpb, gqa_q_gain, gqa_k_gain, w_mem_kv, w_branch, w_out,
              ln1_g, ln1_b, w_router, w_gate_up, w_down, ln2_g, ln2_b):
    B, S, D = x.shape
    M = mem.shape[1]
    cos, sin = axial_rope_tables(S)
    for l in range(DEPTH_2):
        z = jnp.einsum('bsd,df->bsf', x, w_in[l])
        q_na, k_na, v_na, q_g, k_g, v_g, q_m, gate_logits = jnp.split(z, _split_points(), axis=-1)
        rpb = na_rpb[l]
        y_na = lax.map(lambda qkv: neighbourhood_attention(qkv[0], qkv[1], qkv[2], rpb),
                       (q_na.reshape(B, S, NA_HEADS, HEAD_DIM),
                        k_na.reshape(B, S, NA_HEADS, HEAD_DIM),
                        v_na.reshape(B, S, NA_HEADS, HEAD_DIM)))
        y_gqa = gqa_attention(q_g.reshape(B, S, GQA_HEADS, HEAD_DIM),
                              k_g.reshape(B, S, GQA_KV_HEADS, HEAD_DIM),
                              v_g.reshape(B, S, GQA_KV_HEADS, HEAD_DIM),
                              gqa_q_gain[l], gqa_k_gain[l], cos, sin)
        mkv = jnp.einsum('bmd,df->bmf', mem, w_mem_kv[l])
        mk, mv = jnp.split(mkv, 2, axis=-1)
        y_mem = memory_attention(q_m.reshape(B, S, MEM_HEADS, MEM_HEAD_DIM),
                                 mk.reshape(B, M, MEM_HEADS, MEM_HEAD_DIM),
                                 mv.reshape(B, M, MEM_HEADS, MEM_HEAD_DIM))
        branches = jnp.stack([y_na, y_gqa, y_mem], axis=2)
        proj = jnp.einsum('bsgk,gkd->bsgd', branches, w_branch[l])
        gates = jax.nn.sigmoid(gate_logits + b_gate[l]).reshape(B, S, N_BRANCH, D)
        merged = jnp.sum(gates * proj, axis=2)
        mix = jnp.einsum('bsd,de->bse', merged, w_out[l])
        x = layer_norm(DN_ALPHA * x + mix, ln1_g[l], ln1_b[l])
        ffn = expert_choice_ffn(x, w_router[l], w_gate_up[l], w_down[l])
        x = layer_norm(DN_ALPHA * x + ffn, ln2_g[l], ln2_b[l])
    return x


def setup_inputs(seed=0):
    out = dict(first_inputs(seed))
    for name, value in second_inputs(seed + 1).items():
        if name != "x":
            out[name + "_2"] = value
    return out


def reference(
    x, norm_mix_g, norm_ffn_g, a_w_in, a_conv_w, a_conv_b, a_w_r, a_b_r, a_w_i, a_b_i, a_lambda,
    a_w_out, b_w_qkv, b_w_out, ffn_w_gate, ffn_w_up, ffn_w_down, final_g, mem_2, w_in_2,
    b_gate_2, na_rpb_2, gqa_q_gain_2, gqa_k_gain_2, w_mem_kv_2, w_branch_2, w_out_2, ln1_g_2,
    ln1_b_2, w_router_2, w_gate_up_2, w_down_2, ln2_g_2, ln2_b_2,
):
    x = first_block(
        x, norm_mix_g, norm_ffn_g, a_w_in, a_conv_w, a_conv_b, a_w_r, a_b_r, a_w_i, a_b_i,
        a_lambda, a_w_out, b_w_qkv, b_w_out, ffn_w_gate, ffn_w_up, ffn_w_down, final_g,
    )
    return second_block(
        x, mem_2, w_in_2, b_gate_2, na_rpb_2, gqa_q_gain_2, gqa_k_gain_2, w_mem_kv_2,
        w_branch_2, w_out_2, ln1_g_2, ln1_b_2, w_router_2, w_gate_up_2, w_down_2, ln2_g_2,
        ln2_b_2,
    )


_drawn_inputs = setup_inputs


def setup_inputs(seed=0):
    import zlib

    import numpy as np

    out = dict(_drawn_inputs(seed))
    spreads = {}
    factors = {'norm_mix_g': 2.92,
     'a_b_r': 8.0,
     'a_b_i': 8.0,
     'b_gate_2': 8.0,
     'na_rpb_2': 29.273,
     'gqa_q_gain_2': 8.0,
     'gqa_k_gain_2': 8.0,
     'ln2_b_2': 2.75}
    for name, (base, spread) in spreads.items():
        noise = np.random.default_rng([zlib.crc32(name.encode()), seed]).standard_normal(out[name].shape)
        drawn = base * np.exp(spread * noise) if base else spread * noise
        out[name] = __import__('jax').numpy.asarray(drawn.astype(out[name].dtype))
    for name, factor in factors.items():
        out[name] = (out[name] * factor).astype(out[name].dtype)
    return out
```

```python
import math
from contextlib import ExitStack

import numpy as np

import concourse.bass as bass
from concourse import mybir

F = mybir.dt.float32
R = mybir.dt.float32r
B16 = mybir.dt.bfloat16
ALU = mybir.AluOpType
ACT = mybir.ActivationFunctionType
AX = mybir.AxisListType

T = 512
D = 1024
DC = 8
FF = 2816
FH = 11
ALPHA = 2.0 ** 0.25
RMS_EPS = 1e-6
LN_EPS = 1e-5
NRAW = 7
NSPL = 3
AHEAD = 2
NE = 16
CAP = 64
NSLOT = 12

VEC = {}
_at = 0
for _n, _w in (("gmix", 16), ("gffn", 16), ("gfin", 8), ("cw", 32), ("cb", 8), ("br", 8), ("bi", 8),
               ("lam", 8), ("bg", 24), ("qg", 1), ("kg", 1), ("l1g", 8), ("l1b", 8), ("l2g", 8),
               ("l2b", 8), ("eps", 2)):
    VEC[_n] = _at
    _at += _w
NVEC = _at

CST = {}
_at = 0
for _n, _w in (("ident", 128), ("ones", 128), ("bones", 128), ("anti", 128), ("tri", 128), ("nmask", 128),
               ("swap", 128), ("cos", 512), ("sin", 512), ("mask", 768), ("iota", 64)):
    CST[_n] = _at
    _at += _w
NCST = _at


class Queues:

    def __init__(self, sems):
        self.sems = sems
        self.q = {e: [] for e in sems}
        self.q["sp"] = []
        self.n = {e: 0 for e in sems}
        self.seen = {}

    def wait(self, eng, *toks):
        for t in toks:
            if t is None:
                continue
            if isinstance(t, list):
                self.wait(eng, *t)
                continue
            name, sem, v = t
            if self.seen.get((eng, name), 0) >= v:
                continue
            self.seen[(eng, name)] = v
            self.q[eng].append(lambda e, s=sem, v=v: e.wait_ge(s, v))

    def do(self, eng, fn, *waits):
        self.wait(eng, *waits)
        self.n[eng] += 1
        sem = self.sems[eng]
        self.q[eng].append(lambda e: fn(e).then_inc(sem, 1))
        return (eng, sem, self.n[eng])

    def raw(self, eng, fn, *waits):
        self.wait(eng, *waits)
        self.q[eng].append(fn)

    def dma(self, eng, dst, src, ds, *waits):
        self.wait(eng, *waits)
        ds.n += 16
        self.q[eng].append(lambda e: e.dma_start(dst, src).then_inc(ds.sem, 16))
        return (ds.name, ds.sem, ds.n)

    def now(self):
        return [(e, self.sems[e], self.n[e]) for e in self.sems if self.n[e]]


class DmaSem:
    def __init__(self, name, sem):
        self.name, self.sem, self.n = name, sem, 0


class Ring:

    def __init__(self, bufs, after=None):
        self.bufs = bufs
        self.free = [list(after or []) for _ in bufs]
        self.i = 0

    def claim(self):
        j = self.i % len(self.bufs)
        self.i += 1
        w, self.free[j] = self.free[j], None
        assert w is not None, "claimed again before its release"
        return j, self.bufs[j], w

    def release(self, j, *toks):
        self.free[j] = (self.free[j] or []) + list(toks)


def program(nc, I, OUT, plan, stop=None):
    ctx = ExitStack()
    rec = []
    with ctx:
        def sb(name, shape, dt=F, cx=None):
            return (cx or ctx).enter_context(nc.sbuf_tensor(name, shape, dt))

        def sem(name):
            return ctx.enter_context(nc.semaphore(name))

        Q = Queues({e: sem("s_" + e) for e in ("pe", "act", "dve", "pool")})
        PS = ctx.enter_context(nc.psum_tensor("PS", [128, 8, 512], F))

        X = sb("X", [128, DC, T])
        V = sb("V", [128, NVEC])
        C = sb("C", [128, NCST])
        RS = sb("RS", [128, T])
        ST = sb("ST", [128, T])
        SQ = sb("SQ", [128, 2, T])
        SA = sb("SA", [128, T])
        LC = sb("LC", [128, 16])
        WRT = sb("WRT", [128, DC, NE])
        AF = sb("AF", [128, 4 * NE])
        PO = sb("PO", [128, 4 * NE])
        SM = sb("SM", [128, 16])
        dense = ExitStack()
        HH = sb("HH", [128, DC, T], R, dense)
        HL = sb("HL", [128, DC, T], R, dense)
        RAW = [sb(f"RAW{i}", [128, 1024], F, dense) for i in range(NRAW)]
        WH = [sb(f"WH{i}", [128, 1024], R, dense) for i in range(NSPL)]
        WL = [sb(f"WL{i}", [128, 1024], R, dense) for i in range(NSPL)]

        d_in = DmaSem("d_in", sem("d_in"))
        d_raw = [DmaSem(f"d_raw{i}", sem(f"d_raw{i}")) for i in range(NRAW)]
        d_misc = [DmaSem(f"d_misc{i}", sem(f"d_misc{i}")) for i in range(4)]
        d_slot = [DmaSem(f"d_slot{i}", sem(f"d_slot{i}")) for i in range(NSLOT)]
        d_out = DmaSem("d_out", sem("d_out"))

        def vec(n, i=0):
            return V[:, VEC[n] + i:VEC[n] + i + 1]

        def cst(n, a=0, w=128):
            return C[:, CST[n] + a:CST[n] + a + w]

        ident, ones, bones, anti = cst("ident"), cst("ones"), cst("bones"), cst("anti")

        t_in = Q.dma("act", V[:, :], I["vec"], d_in)
        t_in = Q.dma("act", C[:, :], I["cst"], d_in)
        t_in = Q.dma("act", WRT[:, :, :], I["wrt"], d_in)
        t_in = Q.dma("act", X[:, :, :], I["x"], d_in)

        class Banks:
            ring = Ring([PS[:, i, :] for i in range(8)])

            def claim(self):
                j, buf, w = self.ring.claim()
                return (self.ring, j), buf, w

            def release(self, b, *toks):
                b[0].release(b[1], *toks)

            def only(self, *which):
                self.ring = Ring([PS[:, i, :] for i in which], Q.now())

        banks = Banks()

        raw_at = {}
        raws = Ring(RAW)
        spls = Ring(list(zip(WH, WL)))
        ready = {}
        count = [0]

        def load_unit(i):
            name, idx, nt = plan[i]
            j, buf, w = raws.claim()
            src = I[name][idx].rearrange("p a b -> p (a b)")
            raw_at[i] = (j, buf, Q.dma("sp", buf[:, 0:nt * 128], src, d_raw[j], *w))

        def split_unit(i):
            nt = plan[i][2]
            n = nt * 128
            rj, buf, t_raw = raw_at.pop(i)
            j, (wh, wl), w = spls.claim()
            t_hi = Q.do("act", lambda e: e.activation(wh[:, 0:n], buf[:, 0:n], ACT.Copy), t_raw, w)
            t_lo = Q.do("dve", lambda e: e.tensor_tensor(wl[:, 0:n], buf[:, 0:n], wh[:, 0:n].bitcast(F), ALU.subtract),
                        t_hi, t_raw, w)
            raws.release(rj, t_lo)
            if i + NRAW < len(plan):
                load_unit(i + NRAW)
            ready[i] = (j, wh, wl, t_hi, t_lo)

        def use(name, idx, nt):
            i = count[0]
            count[0] += 1
            rec.append((name, idx, nt))
            if plan is None:
                return (0, WH[0], WL[0], None, None)
            assert plan[i] == (name, idx, nt)
            if i == 0:
                for k in range(min(NRAW, len(plan))):
                    load_unit(k)
                for k in range(AHEAD):
                    split_unit(k)
            if i + AHEAD < len(plan):
                split_unit(i + AHEAD)
            return ready.pop(i)

        def mm3(out, wh, wl, xh, xl, start, stop, waits):
            Q.wait("pe", *waits)
            Q.raw("pe", lambda e: e.matmul(out, wh, xh, start=start, stop=False))
            Q.raw("pe", lambda e: e.matmul(out, wh, xl, start=False, stop=False))
            return Q.do("pe", lambda e: e.matmul(out, wl, xh, start=False, stop=stop))

        def lin(units, rhs, n=T):
            b, bank, w = banks.claim()
            out = bank[:, 0:n]
            total = sum(u[2] for u in units)
            k = 0
            for name, idx, nt in units:
                j, wh, wl, th, tl = use(name, idx, nt)
                for t in range(nt):
                    xh, xl, tx = rhs(k)
                    tok = mm3(out, wh[:, t * 128:t * 128 + 128], wl[:, t * 128:t * 128 + 128], xh, xl,
                              k == 0, k == total - 1, [w, th, tl, tx])
                    w = []
                    k += 1
                spls.release(j, tok)
            return b, out, tok

        xt = [[t_in] for _ in range(DC)]
        xr = [[] for _ in range(DC)]
        ht = [None] * DC
        hr = [[] for _ in range(DC)]
        rs_t = [None]
        rs_r = [[]]
        sq_r = [[], []]
        sa_r = [[]]

        def norm_start(c, g, gi):
            t = Q.do("act", lambda e: e.activation(SQ[:, c % 2, :], X[:, c, :], ACT.Square), xt[c], sq_r[c % 2])
            if c == 0:
                t2 = Q.do("pool", lambda e: e.tensor_copy(SA[:, :], SQ[:, 0, :]), t, sa_r[0])
            else:
                t2 = Q.do("pool", lambda e: e.tensor_tensor(SA[:, :], SA[:, :], SQ[:, c % 2, :], ALU.add),
                          t, sa_t[0])
            sa_t[0] = t2
            sq_r[c % 2] = [t2]
            tg = Q.do("dve", lambda e: e.tensor_scalar(GX[:, c % 2, :], X[:, c, :], vec(g, gi + c), None, ALU.mult),
                      xt[c], gx_r[c % 2])
            th = Q.do("act", lambda e: e.activation(HH[:, c, :], GX[:, c % 2, :], ACT.Copy), tg, hr[c])
            tl = Q.do("dve", lambda e: e.tensor_tensor(HL[:, c, :], GX[:, c % 2, :], HH[:, c, :].bitcast(F),
                                                       ALU.subtract), th, hr[c])
            gx_r[c % 2] = [tl]
            xr[c] += [t, tg]
            hr[c] = []
            ht[c] = [th, tl]

        def norm_rest():
            b, bank, w = banks.claim()
            tp = Q.do("pe", lambda e: e.matmul(bank, ones, SA[:, :], start=True, stop=True), w, sa_t[0], t_in)
            sa_r[0] = [tp]
            ta = Q.do("act", lambda e: e.activation(ST[:, :], bank, ACT.Sqrt, bias=vec("eps", 0), scale=1.0 / D),
                      tp, rs_t[0])
            banks.release(b, ta)
            rs_t[0] = Q.do("dve", lambda e: e.reciprocal(RS[:, :], ST[:, :]), ta, rs_r[0])
            rs_r[0] = []

        sa_t = [None]
        GX = sb("GX", [128, 2, T], F, dense)
        gx_r = [[], []]

        def hrhs(k):
            return HH[:, k, :], HL[:, k, :], ht[k]

        def add_x(c, b, out, tok):
            t = Q.do("dve", lambda e: e.tensor_tensor(X[:, c, :], X[:, c, :], out, ALU.add), tok, xt[c], xr[c])
            banks.release(b, t)
            xt[c], xr[c] = [t], []

        def scaled(dst, b, out, tok, mul=1.0, free=()):
            n = out.shape[-1]
            if mul == 1.0:
                t = Q.do("dve", lambda e: e.tensor_tensor(dst, out, RS[:, 0:n], ALU.mult), tok, rs_t[0], *free)
            else:
                t = Q.do("dve", lambda e: e.scalar_tensor_tensor(out=dst, in0=out, scalar=mul, in1=RS[:, 0:n],
                                                                 op0=ALU.mult, op1=ALU.mult), tok, rs_t[0], *free)
            banks.release(b, t)
            rs_r[0] = [t]
            return t

        def halves(hi, lo, src, tok, free=()):
            th = Q.do("act", lambda e: e.activation(hi, src, ACT.Copy), tok, *free)
            tl = Q.do("dve", lambda e: e.tensor_tensor(lo, src, hi.bitcast(F), ALU.subtract), th, tok, *free)
            return [th, tl]

        def natural(dst, parts, waits, free):
            b, bank, w = banks.claim()
            Q.wait("pe", w, waits, t_in)
            n = len(parts)
            for j, src in enumerate(parts):
                tt = Q.do("pe", lambda e, j=j, src=src: e.transpose(bank[:, 128 * j:128 * j + 128], src, ident))
            tv = Q.do("dve", lambda e: e.tensor_copy(dst, bank[:, 0:128 * n]), tt, free)
            banks.release(b, tv)
            return tv

        def dump():
            t = Q.dma("sp", OUT.rearrange("c p t -> p c t"), X[:, :, :], d_out, Q.now())
            Q.wait("sp", t)

        for c in range(DC):
            norm_start(c, "gmix", 0)
        lam = V[:, VEC["lam"]:VEC["lam"] + 8]
        t = Q.do("act", lambda e: e.activation(LC[:, 8:16], lam, ACT.Abs), t_in)
        t = Q.do("act", lambda e: e.activation(LC[:, 8:16], LC[:, 8:16], ACT.Exp, scale=-1.0), t)
        t = Q.do("act", lambda e: e.activation(LC[:, 8:16], LC[:, 8:16], ACT.Ln, bias=1.0), t)
        t2 = Q.do("dve", lambda e: e.tensor_scalar(LC[:, 0:8], lam, 0.0, 8.0, ALU.min, ALU.mult), t_in)
        t_lc = Q.do("dve", lambda e: e.scalar_tensor_tensor(out=LC[:, 0:8], in0=LC[:, 8:16], scalar=-8.0,
                                                            in1=LC[:, 0:8], op0=ALU.mult, op1=ALU.add), t, t2)

        ph = ExitStack()
        YH = sb("YH", [128, DC, T], R, ph)
        YL = sb("YL", [128, DC, T], R, ph)
        XB = [sb(f"XB{i}", [128, T + 4], F, ph) for i in range(2)]
        XC = [sb(f"XC{i}", [128, T], F, ph) for i in range(4)]
        XCH = [sb(f"XCH{i}", [128, T], R, ph) for i in range(2)]
        XCL = [sb(f"XCL{i}", [128, T], R, ph) for i in range(2)]
        GG = [sb(f"GG{i}", [128, T], F, ph) for i in range(2)]
        RI = [sb(f"RI{i}", [128, 2, T], F, ph) for i in range(2)]
        TA = [sb(f"TA{i}", [128, 3, T], F, ph) for i in range(2)]
        tz = [Q.do("pool", lambda e, i=i: e.memset(XB[i][:, 0:4], 0.0)) for i in range(2)]
        xb_r, xc_r, xch_r, gg_r, ri_r, ta_r = ([[] for _ in range(4)] for _ in range(6))
        yt = [None] * DC
        late = []
        for n in range(4):
            gg_t, xc_t, xcs_t = [None, None], [None, None], [None, None]
            for p in range(2):
                c = 2 * n + p
                b, out, tok = lin([("win", (8 + c,), 8)], hrhs)
                if n == 0 and p == 0:
                    norm_rest()
                tb = scaled(XB[p][:, 4:T + 4], b, out, tok, free=[tz[p], xb_r[p]])
                xc = XC[2 * (n % 2) + p]
                xf = xc_r[2 * (n % 2) + p]
                t = Q.do("dve", lambda e, p=p, c=c, xc=xc: e.tensor_scalar(
                    xc[:, :], XB[p][:, 4:T + 4], vec("cw", 24 + c), vec("cb", c), ALU.mult, ALU.add), tb, xf, t_in)
                for j in (2, 1, 0):
                    t = Q.do("dve", lambda e, p=p, c=c, xc=xc, j=j: e.scalar_tensor_tensor(
                        out=xc[:, :], in0=XB[p][:, 1 + j:T + 1 + j], scalar=vec("cw", 8 * j + c), in1=xc[:, :],
                        op0=ALU.mult, op1=ALU.add), t)
                xb_r[p] = [t]
                xc_r[2 * (n % 2) + p] = []
                xc_t[p] = t
                xcs_t[p] = halves(XCH[p][:, :], XCL[p][:, :], xc[:, :], t, free=[xch_r[p]])
            for p in range(2):
                c = 2 * n + p
                b, out, tok = lin([("win", (c,), 8)], hrhs)
                tg = scaled(GG[p][:, :], b, out, tok, free=[gg_r[p]])
                gg_t[p] = Q.do("act", lambda e, p=p: e.activation(GG[p][:, :], GG[p][:, :], ACT.Gelu_apprx_tanh), tg)
            j, wh, wl, th, tl = use("wri", (n,), 8)
            rib = []
            for p in range(2):
                for w in range(2):
                    b, bank, wt = banks.claim()
                    for k in range(2):
                        m = (w * 2 + p) * 2 + k
                        tok = mm3(bank, wh[:, m * 128:m * 128 + 128], wl[:, m * 128:m * 128 + 128],
                                  XCH[k][:, :], XCL[k][:, :], k == 0, k == 1, [wt, th, tl, xcs_t[k]])
                    rib.append((b, bank, tok))
            spls.release(j, tok)
            xch_r[0], xch_r[1] = [tok], [tok]
            for p in range(2):
                c = 2 * n + p
                ts = []
                for w in range(2):
                    b, bank, tok = rib[2 * p + w]
                    t = Q.do("act", lambda e, p=p, w=w, c=c, bank=bank: e.activation(
                        RI[p][:, w, :], bank, ACT.Sigmoid, bias=vec(("br", "bi")[w], c)), tok, ri_r[p])
                    banks.release(b, t)
                    ts.append(t)
                rib[2 * p] = ts
            for p in range(2):
                c = 2 * n + p
                xc = XC[2 * (n % 2) + p]
                ts = rib[2 * p]
                a, tt, u = TA[p][:, 0, :], TA[p][:, 1, :], TA[p][:, 2, :]
                t_a = Q.do("act", lambda e, p=p, c=c, a=a: e.activation(a, RI[p][:, 0, :], ACT.Exp, scale=LC[:, c:c + 1]),
                           ts[0], t_lc, ta_r[p])
                t_t = Q.do("act", lambda e, p=p, c=c, tt=tt: e.activation(tt, RI[p][:, 0, :], ACT.Tanh, scale=LC[:, c:c + 1]),
                           ts[0], t_lc, ta_r[p])
                t_ix = Q.do("pool", lambda e, p=p, xc=xc: e.tensor_tensor(RI[p][:, 1, :], RI[p][:, 1, :], xc[:, :], ALU.mult),
                            ts[1], xc_t[p])
                t1 = Q.do("dve", lambda e, tt=tt, u=u: e.tensor_scalar(u, tt, -1.0, 1.0, ALU.mult, ALU.add), t_t, ta_r[p])
                t1 = Q.do("dve", lambda e, u=u: e.reciprocal(u, u), t1)
                t1 = Q.do("dve", lambda e, u=u, tt=tt: e.scalar_tensor_tensor(out=u, in0=tt, scalar=-2.0, in1=u,
                                                                           op0=ALU.mult, op1=ALU.mult), t1)
                t1 = Q.do("dve", lambda e, u=u: e.tensor_scalar(u, u, 0.0, None, ALU.max), t1)
                t1 = Q.do("act", lambda e, u=u: e.activation(u, u, ACT.Sqrt), t1)
                t1 = Q.do("pool", lambda e, p=p, u=u: e.tensor_tensor(u, u, RI[p][:, 1, :], ALU.mult), t1, t_ix)
                ri_r[p] = [t1, t_t, t_a]
                xc_r[2 * (n % 2) + p] = [t_ix]
                t1 = Q.do("dve", lambda e, a=a, u=u, tt=tt: e.tensor_tensor_scan(tt, a, u, 0.0, ALU.mult, ALU.add), t1, t_a)
                t1 = Q.do("dve", lambda e, p=p, tt=tt: e.tensor_tensor(tt, tt, GG[p][:, :], ALU.mult), t1, gg_t[p])
                gg_r[p] = [t1]
                yt[c] = halves(YH[:, c, :], YL[:, c, :], tt, t1)
                ta_r[p] = yt[c]
        for c in range(DC):
            hr[c] = [Q.now()[0]]

        def out_proj(name, g, gi):
            for c in range(DC):
                b, out, tok = lin([(name, (c,), 8)], lambda k: (YH[:, k, :], YL[:, k, :], yt[k]))
                add_x(c, b, out, tok)
                norm_start(c, g, gi)

        out_proj("wout", "gffn", 0)
        ph.close()
        if stop == 1:
            dump()

        def ffn(l, g, gi):
            ph = ExitStack()
            start = Q.now()
            MH = sb(f"MH{l}", [128, FH, T], R, ph)
            ML = sb(f"ML{l}", [128, FH, T], R, ph)
            G1 = sb(f"G1{l}", [128, 2, T], F, ph)
            S1 = sb(f"S1{l}", [128, 2, T], F, ph)
            U1 = sb(f"U1{l}", [128, 2, T], F, ph)
            g_r, s_r, u_r = ([list(start), list(start)] for _ in range(3))
            m_r = list(start)
            for half in range(2):
                mt = [None] * FH
                for f in range(FH):
                    i = half * FH + f
                    z = f % 2
                    b, out, tok = lin([("wg", (l, i), 8)], hrhs)
                    if i == 0:
                        norm_rest()
                    b2, out2, tok2 = lin([("wu", (l, i), 8)], hrhs)
                    tg = scaled(G1[:, z, :], b, out, tok, free=[g_r[z]])
                    ts = Q.do("act", lambda e, z=z: e.activation(S1[:, z, :], G1[:, z, :], ACT.Silu), tg, s_r[z])
                    g_r[z] = [ts]
                    tu = scaled(U1[:, z, :], b2, out2, tok2, free=[u_r[z]])
                    tm = Q.do("dve", lambda e, z=z: e.tensor_tensor(U1[:, z, :], U1[:, z, :], S1[:, z, :], ALU.mult), tu, ts)
                    s_r[z] = [tm]
                    mt[f] = halves(MH[:, f, :], ML[:, f, :], U1[:, z, :], tm, free=[m_r])
                    u_r[z] = mt[f]
                if half == 1:
                    for c in range(DC):
                        hr[c] = [("pe", Q.sems["pe"], Q.n["pe"])]
                for c in range(DC):
                    b, out, tok = lin([("wd", (l, half, c, slice(None), slice(0, 6)), 6),
                                       ("wd", (l, half, c, slice(None), slice(6, 11)), 5)],
                                      lambda k: (MH[:, k, :], ML[:, k, :], mt[k]))
                    add_x(c, b, out, tok)
                    if half == 1:
                        norm_start(c, g, gi)
                m_r = [tok]
            ph.close()

        if stop is None or stop > 1:
            ffn(0, "gmix", 8)
            if stop == 2:
                dump()

        def sb_mixer():
            ph = ExitStack()
            start = Q.now()
            YH = sb("OH", [128, DC, T], R, ph)
            YL = sb("OL", [128, DC, T], R, ph)
            QK = [sb(f"QK{i}", [128, 3, T], F, ph) for i in range(2)]
            VN = [sb(f"VN{i}", [128, T], F, ph) for i in range(2)]
            AL = sb("AL", [128, 1280], F, ph)
            PP = sb("PP", [128, 1280], F, ph)
            PH = sb("PH", [128, 1280], R, ph)
            PL = sb("PL", [128, 1280], R, ph)
            W = sb("W", [128, 1280], F, ph)
            TR = sb("TR", [128, 256], R, ph)
            IB = sb("IB", [128, 256], B16, ph)
            tc = [Q.do("dve", lambda e: e.tensor_scalar(TR[:, 0:128], cst("tri"), -1.0, None, ALU.mult), start),
                  Q.do("dve", lambda e: e.tensor_scalar(TR[:, 128:256], ones, -1.0, None, ALU.mult), start),
                  Q.do("dve", lambda e: e.tensor_copy(IB[:, 0:128], ident), start),
                  Q.do("dve", lambda e: e.tensor_copy(IB[:, 128:256], cst("nmask")), start)]
            off = [0, 512, 1024, 896]
            wid = [512, 384, 256, 128]
            al_r, pp_r, ph_r, w_r = (list(start) for _ in range(4))
            qk_r, vn_r = [list(start), list(start)], [list(start), list(start)]
            grp = Ring([PS[:, 0:3, :].rearrange("p a b -> p (a b)"), PS[:, 3:6, :].rearrange("p a b -> p (a b)")],
                       start)
            banks.only(6, 7)

            def scores(h):
                c, p = h // 2, 64 * (h % 2)
                z = c % 2
                gj, S, w = grp.claim()
                for j in (0, 1, 3, 2):
                    o, n = off[j], wid[j]
                    Q.wait("pe", w, tc, qk_t[z])
                    Q.raw("pe", lambda e, o=o, n=n, j=j: e.matmul(
                        S[:, o:o + n], QK[z][p:p + 64, 1, 128 * j:128 * j + 128], QK[z][p:p + 64, 0, 128 * j:512],
                        start=(j != 3), stop=False, skip_group_check=True))
                    ml = Q.do("pe", lambda e, o=o: e.matmul(S[:, o:o + 128], IB[:, 0:128], IB[:, 128:256],
                                                           start=False, stop=False, skip_group_check=True))
                return gj, S, ml

            def softplus(S, ml):
                nonlocal al_r, pp_r
                t = Q.do("act", lambda e: e.activation(AL[:, :], S[:, 0:1280], ACT.Abs), ml, al_r)
                t = Q.do("act", lambda e: e.activation(AL[:, :], AL[:, :], ACT.Exp, scale=-1.0), t)
                t = Q.do("act", lambda e: e.activation(AL[:, :], AL[:, :], ACT.Ln, bias=1.0), t)
                t = Q.do("dve", lambda e: e.scalar_tensor_tensor(out=PP[:, :], in0=S[:, 0:1280], scalar=0.0,
                                                                 in1=AL[:, :], op0=ALU.max, op1=ALU.add), t, ml, pp_r)
                al_r = [t]
                t1 = Q.do("dve", lambda e: e.tensor_copy(PH[:, :], PP[:, :]), t, ph_r)
                t2 = Q.do("dve", lambda e: e.tensor_tensor(PL[:, :], PP[:, :], PH[:, :].bitcast(F), ALU.subtract),
                          t1, ph_r)
                pp_r = [t2]
                return [t1, t2]

            def weights(gj, S, tp):
                nonlocal ph_r
                Q.wait("pe", tp)
                todo = [(j, jj, P) for j in (0, 1, 3, 2) for jj in range(j, 4) for P in (PH, PL)]
                for i, (j, jj, P) in enumerate(todo):
                    lhs = TR[:, 0:128] if jj == j else TR[:, 128:256]
                    o = off[j] + 128 * (jj - j)
                    f = lambda e, o=o, jj=jj, P=P, lhs=lhs: e.matmul(
                        S[:, o:o + wid[jj]], lhs, P[:, off[jj]:off[jj] + wid[jj]], start=False,
                        stop=(jj == 3 and P is PL), skip_group_check=True)
                    if i < len(todo) - 1:
                        Q.raw("pe", f)
                    else:
                        ms = Q.do("pe", f)
                ph_r = [ms]
                te = Q.do("act", lambda e: e.activation(W[:, :], S[:, 0:1280], ACT.Exp), ms, w_r)
                grp.release(gj, te)
                return te

            def values(h, te, bank, w):
                nonlocal w_r
                c, p = h // 2, 64 * (h % 2)
                z = c % 2
                Q.wait("pe", te, vn_t[z], w)
                for j in range(4):
                    f = lambda e, j=j: e.matmul(bank[p:p + 64, 128 * j:512], VN[z][:, 128 * j + p:128 * j + p + 64],
                                                W[:, off[j]:off[j] + wid[j]], start=(j == 0), stop=(j == 3),
                                                skip_group_check=True)
                    if j < 3:
                        Q.raw("pe", f)
                    else:
                        mo = Q.do("pe", f)
                w_r = [mo]
                return mo

            qk_t, vn_t = [None, None], [None, None]
            yts = [None] * DC

            def project(c):
                z = c % 2
                ts = []
                for i in range(3):
                    b, out, tok = lin([("wqkv", (8 * i + c,), 8)], hrhs)
                    if c == 0 and i == 0:
                        norm_rest()
                    ts.append(scaled(QK[z][:, i, :], b, out, tok, mul=0.125 if i == 0 else 1.0, free=[qk_r[z]]))
                vn_t[z] = natural(VN[z][:, :], [QK[z][:, 2, 128 * j:128 * j + 128] for j in range(4)], ts, vn_r[z])
                qk_t[z] = ts

            project(0)
            for c in range(DC):
                z = c % 2
                g0, S0, m = scores(2 * c)
                a0 = softplus(S0, m)
                g1, S1, m1 = scores(2 * c + 1)
                if c + 1 < DC:
                    project(c + 1)
                te = weights(g0, S0, a0)
                b, bank, w = banks.claim()
                o0 = values(2 * c, te, bank, w)
                a1 = softplus(S1, m1)
                te = weights(g1, S1, a1)
                o1 = values(2 * c + 1, te, bank, [])
                qk_r[z], vn_r[z] = [o1], [o1]
                yts[c] = halves(YH[:, c, :], YL[:, c, :], bank, [o0, o1], free=[start])
                banks.release(b, yts[c])
            for c in range(DC):
                hr[c] = [("pe", Q.sems["pe"], Q.n["pe"])]
            banks.only(*range(8))
            for c in range(DC):
                b, out, tok = lin([("wbo", (c,), 8)], lambda k: (YH[:, k, :], YL[:, k, :], yts[k]))
                add_x(c, b, out, tok)
                norm_start(c, "gffn", 8)
            ph.close()

        if stop is None or stop > 2:
            sb_mixer()
            if stop == 3:
                dump()
        def softmax(S, P, n, scale, k, ready, free, in_max=None, s_free=None):
            m, nm, su, ri = (SM[:, 4 * k + i:4 * k + i + 1] for i in range(4))
            if in_max is None:
                t = Q.do("dve", lambda e: e.tensor_reduce(m, S, AX.X, ALU.max), ready, sm_r[k])
            else:
                t = in_max
            t = Q.do("dve", lambda e: e.tensor_scalar(nm, m, -scale, None, ALU.mult), t, sm_r[k])
            t = te = Q.do("act", lambda e: e.activation(P, S, ACT.Exp, bias=nm, scale=scale, accum_out=su), t, free)
            t = Q.do("dve", lambda e: e.reciprocal(ri, su), t)
            t = Q.do("dve", lambda e: e.tensor_scalar(P, P, ri, None, ALU.mult), t)
            sm_r[k] = [t]
            return te, t

        def turned(dst, P, n, waits, free):
            b, bank, w = banks.claim()
            Q.wait("pe", w, waits)
            for j in range(n):
                f = lambda e, j=j: e.transpose(bank[:, 128 * j:128 * j + 128], P[:, 128 * j:128 * j + 128], ident)
                if j < n - 1:
                    Q.raw("pe", f)
                else:
                    tt = Q.do("pe", f)
            src = bank[:, 0:128 * n].rearrange("p (j q) -> p j q", j=n)
            tv = Q.do("act", lambda e: e.activation(dst, src, ACT.Copy), tt, free)
            banks.release(b, tv)
            return tt, tv

        def staged(groups):
            prev = None
            for g in groups + [None]:
                for u in range(g["n"] if g else 1):
                    cur = None
                    if g:
                        if u == 0:
                            g["project"]()
                        cur = (g, u, g["score"](u))
                    if prev:
                        pg, pu, st = prev
                        pg["turn"](pu, st)
                    prev = cur

        sm_r = [[] for _ in range(4)]

        def mixer2():
            ph = ExitStack()
            start = Q.now()
            Y3H = sb("Y3H", [128, 12, T], R, ph)
            Y3L = sb("Y3L", [128, 12, T], R, ph)
            y3 = [None] * 12
            banks.only(0, 1, 2, 3, 4, 5)
            obanks = Ring([PS[:, 6, :], PS[:, 7, :]], start)

            pm = ExitStack()
            MKV = sb("MKV", [128, 4, 2, 256], F, pm)
            pk = ExitStack()
            MF = sb("MF", [128, 2, 256], F, pk)
            MMH = sb("MMH", [128, DC, 256], R, pk)
            MML = sb("MML", [128, DC, 256], R, pk)
            mf_r = [list(start), list(start)]
            mm_t = [None] * DC
            for c in range(DC):
                t = Q.dma("pool", MF[:, c % 2, :], I["mem"][:, c, :], d_misc[c % 2], mf_r[c % 2])
                mm_t[c] = halves(MMH[:, c, :], MML[:, c, :], MF[:, c % 2, :], t, free=[start])
                mf_r[c % 2] = mm_t[c]
            VT = sb("VT", [128, 2, 256], F, pk)
            vt_r = [list(start), list(start)]
            kv_t = [[] for _ in range(4)]
            for h in range(4):
                b, out, tok = lin([("wmkv", (h,), 8)], lambda k: (MMH[:, k, :], MML[:, k, :], mm_t[k]), n=256)
                t = Q.do("dve", lambda e, out=out, h=h: e.tensor_copy(MKV[:, h, 0, :], out), tok, start)
                banks.release(b, t)
                kv_t[h].append(t)
                b, out, tok = lin([("wmkv", (4 + h,), 8)], lambda k: (MMH[:, k, :], MML[:, k, :], mm_t[k]), n=256)
                t = Q.do("dve", lambda e, out=out, h=h: e.tensor_copy(VT[:, h % 2, :], out), tok, vt_r[h % 2])
                banks.release(b, t)
                t = natural(MKV[:, h, 1, :], [VT[:, h % 2, 0:128], VT[:, h % 2, 128:256]], t, start)
                vt_r[h % 2] = [t]
                kv_t[h].append(t)
            pk.close()
            start = Q.now()
            tg = Q.do("dve", lambda e: e.tensor_scalar(LC[:, 0:8], V[:, VEC["gfin"]:VEC["gfin"] + 8], ALPHA, None,
                                                       ALU.mult), start)
            QM = sb("QM", [128, 2, T], F, pm)
            PM = [sb(f"PM{i}", [128, 256], F, pm) for i in range(2)]
            PT = [sb(f"PT{i}", [128, 2, T], F, pm) for i in range(2)]
            qm_r, qm_t = [list(start), list(start)], [None, None]
            pm_r, pt_r, pt_t = [list(start), list(start)], [list(start), list(start)], [[], []]

            def mem_head(h):
                z = h % 2

                def project():
                    b, out, tok = lin([("w2", (18 + h,), 8)], hrhs)
                    if h == 0:
                        norm_rest()
                        for c in range(DC):
                            t = Q.do("dve", lambda e, c=c: e.scalar_tensor_tensor(
                                out=X[:, c, :], in0=X[:, c, :], scalar=LC[:, c:c + 1], in1=RS[:, :], op0=ALU.mult,
                                op1=ALU.mult), tg, rs_t[0], xt[c], xr[c])
                            xt[c], xr[c] = [t], []
                        rs_r[0] = [t]
                    qm_t[z] = scaled(QM[:, z, :], b, out, tok, free=[qm_r[z]])

                def score(u):
                    b, bank, w = banks.claim()
                    tok = Q.do("pe", lambda e: e.matmul(bank[:, 0:256], QM[:, z, 128 * u:128 * u + 128],
                                                        MKV[:, h, 0, :], start=True, stop=True), w, qm_t[z], kv_t[h])
                    te, t = softmax(bank[:, 0:256], PM[u % 2][:, :], 256, 1.0 / math.sqrt(128.0), u % 2, tok,
                                    pm_r[u % 2])
                    banks.release(b, te)
                    return t

                def turn(u, t):
                    tt, tv = turned(PT[z][:, :, 128 * u:128 * u + 128], PM[u % 2], 2, t, pt_r[z])
                    pm_r[u % 2] = [tt]
                    pt_t[z].append(tv)
                    if u == 3:
                        qm_r[z] = [tt]
                        oj, bank, w = obanks.claim()
                        Q.wait("pe", w, pt_t[z])
                        for j in range(2):
                            tok = Q.do("pe", lambda e, j=j: e.matmul(bank, MKV[:, h, 1, 128 * j:128 * j + 128],
                                                                     PT[z][:, j, :], start=(j == 0), stop=(j == 1)))
                        pt_r[z], pt_t[z] = [tok], []
                        y3[8 + h] = halves(Y3H[:, 8 + h, :], Y3L[:, 8 + h, :], bank, tok, free=[start])
                        obanks.release(oj, *y3[8 + h])

                return {"n": 4, "project": project, "score": score, "turn": turn}

            staged([mem_head(h) for h in range(4)])
            pm.close()

            pg = ExitStack()
            start = Q.now()
            KG = sb("KG", [128, T], F, pg)
            VG = sb("VG", [128, T], F, pg)
            ZG = [sb(f"ZG{i}", [128, T], F, pg) for i in range(2)]
            PG = [sb(f"PG{i}", [128, T], F, pg) for i in range(2)]
            GT2 = [sb(f"GT2{i}", [128, 4, T], F, pg) for i in range(2)]
            z_r, pg_r, gt_r, gt_t = [list(start), list(start)], [list(start), list(start)], [list(start), list(start)], [[], []]

            def rope(Z, tile, gain, free):
                b, out, tok = lin([("w2", (tile,), 8)], hrhs)
                tz = scaled(Z, b, out, tok, free=[free])
                t = Q.do("act", lambda e: e.activation(SQ[:, 0, :], Z, ACT.Square), tz, sq_r[0])
                b, bank, w = banks.claim()
                t = Q.do("pe", lambda e, bank=bank: e.matmul(bank, bones, SQ[:, 0, :], start=True, stop=True), t, w)
                sq_r[0] = [t]
                t = Q.do("act", lambda e, bank=bank: e.activation(ST[:, :], bank, ACT.Sqrt, bias=vec("eps", 0), scale=1.0 / 64),
                         t, st_r)
                banks.release(b, t)
                t = Q.do("dve", lambda e: e.reciprocal(ST[:, :], ST[:, :]), t)
                t = Q.do("dve", lambda e: e.scalar_tensor_tensor(out=Z, in0=Z, scalar=gain, in1=ST[:, :],
                                                                 op0=ALU.mult, op1=ALU.mult), t, tz)
                st_r[:] = [t]
                b, bank, w = banks.claim()
                t2 = Q.do("pe", lambda e: e.matmul(bank, cst("swap"), Z, start=True, stop=True), t, w)
                t3 = Q.do("dve", lambda e: e.tensor_tensor(GX[:, 0, :], bank, cst("sin", 0, 512), ALU.mult), t2, gx_r[0])
                banks.release(b, t3)
                t4 = Q.do("dve", lambda e: e.tensor_tensor(Z, Z, cst("cos", 0, 512), ALU.mult), t, t2)
                t5 = Q.do("dve", lambda e: e.tensor_tensor(Z, Z, GX[:, 0, :], ALU.add), t3, t4)
                gx_r[0] = [t5]
                return t5

            st_r = [rs_t[0]]
            kg_t = rope(KG[:, :], 16, vec("kg"), start)
            b, out, tok = lin([("w2", (17,), 8)], hrhs)
            t = scaled(ZG[1][:, :], b, out, tok, free=[z_r[1]])
            vg_t = natural(VG[:, :], [ZG[1][:, 128 * j:128 * j + 128] for j in range(4)], t, start)
            z_r[1] = [vg_t]

            def gqa_pair(c):
                z = c % 2
                st = {}

                def project():
                    st["q"] = rope(ZG[z][:, :], 12 + c, vec("qg"), z_r[z])

                def score(u):
                    p, qc = 64 * (u // 4), u % 4
                    b, bank, w = banks.claim()
                    tok = Q.do("pe", lambda e: e.matmul(bank, ZG[z][p:p + 64, 128 * qc:128 * qc + 128], KG[p:p + 64, :],
                                                        start=True, stop=True), w, st["q"], kg_t)
                    te, t = softmax(bank, PG[u % 2][:, :], T, 0.125, u % 2, tok, pg_r[u % 2])
                    banks.release(b, te)
                    if u == 7:
                        z_r[z] = [tok]
                    return t

                def turn(u, t):
                    p, qc, y = 64 * (u // 4), u % 4, u // 4
                    tt, tv = turned(GT2[y][:, :, 128 * qc:128 * qc + 128], PG[u % 2], 4, t, gt_r[y])
                    pg_r[u % 2] = [tt]
                    gt_t[y].append(tv)
                    if qc == 3:
                        if y == 0:
                            st["o"] = obanks.claim()
                        oj, bank, w = st["o"]
                        Q.wait("pe", w if y == 0 else [], gt_t[y], vg_t)
                        for j in range(4):
                            tok = Q.do("pe", lambda e, j=j: e.matmul(
                                bank[p:p + 64, :], VG[:, 128 * j + p:128 * j + p + 64], GT2[y][:, j, :],
                                start=(j == 0), stop=(j == 3)))
                        gt_r[y], gt_t[y] = [tok], []
                        if y == 1:
                            y3[4 + c] = halves(Y3H[:, 4 + c, :], Y3L[:, 4 + c, :], bank, tok)
                            obanks.release(oj, *y3[4 + c])

                return {"n": 8, "project": project, "score": score, "turn": turn}

            staged([gqa_pair(c) for c in range(4)])
            pg.close()

            pn = ExitStack()
            start = Q.now()
            NQ = [sb(f"NQ{i}", [128, 2, T], F, pn) for i in range(2)]
            NB = sb("NB", [128, 4, 256], F, pn)
            NV = [sb(f"NV{i}", [128, 1024], F, pn) for i in range(2)]
            BI = [sb(f"BI{i}", [128, 2, 384], F, pn) for i in range(2)]
            SN = [sb(f"SN{i}", [128, 256], F, pn) for i in range(2)]
            PN = [sb(f"PN{i}", [128, 256], F, pn) for i in range(2)]
            NT = [sb(f"NT{i}", [128, 2, 128], F, pn) for i in range(2)]
            nq_r, bi_r, sn_r, pn_r, nt_r = ([list(start), list(start)] for _ in range(5))
            nv_r, nb_r = [list(start), list(start)], [list(start)]
            band = (0, 8, 24, 32)

            def na_pair(c):
                z = c % 2
                st = {"t": None}

                def bias():
                    for p in range(2):
                        for r in range(8):
                            src = bass.AP(I["rpb"].tensor, (2 * c + p) * 465 + 31 * r, [[1, 16], [31, 8], [1, 48]])
                            dst = BI[z][16 * r:16 * r + 16, p, :].rearrange("i (a w) -> i a w", a=8)
                            st["b"] = Q.dma("pool", dst, src, d_misc[2 + z], bi_r[z])

                def project():
                    bias()
                    b, out, tok = lin([("w2", (c,), 8)], hrhs)
                    by = lambda a: a.rearrange("p (r c i) -> p r c i", r=8, c=4)
                    dst = NQ[z][:, 0, :].rearrange("p (c r i) -> p r c i", c=4, r=8)
                    tq = Q.do("dve", lambda e, out=out: e.tensor_tensor(dst, by(out), by(RS[:, :]), ALU.mult), tok, rs_t[0], nq_r[z])
                    banks.release(b, tq)
                    b, out, tok = lin([("w2", (4 + c,), 8)], hrhs)
                    tk = scaled(NQ[z][:, 1, :], b, out, tok, mul=0.125, free=[nq_r[z]])
                    b, vout, tok = lin([("w2", (8 + c,), 8)], hrhs)
                    ts = [tq, tk]
                    for cb in range(4):
                        bd = lambda a, cb=cb: a.rearrange("p (r w) -> p r w", r=8)[:, :, band[cb]:band[cb] + 32]
                        t = Q.do("dve", lambda e, cb=cb, bd=bd: e.tensor_tensor(
                            NB[:, cb, :].rearrange("p (r w) -> p r w", r=8), bd(vout), bd(RS[:, :]), ALU.mult),
                            tok, rs_t[0], nb_r[0])
                    banks.release(b, t)
                    rs_r[0] = [t]
                    parts = [NB[:, cb, 128 * hf:128 * hf + 128] for cb in range(4) for hf in range(2)]
                    t1 = natural(NV[z][:, 0:512], parts[0:4], t, nv_r[z])
                    t2 = natural(NV[z][:, 512:1024], parts[4:8], t, nv_r[z])
                    nb_r[0] = [t1, t2]
                    st["v"] = [t1, t2]
                    st["t"] = ts

                def score(u):
                    y, cb = u // 4, u % 4
                    p = 64 * y
                    bs, o = band[cb], band[cb] - 16 * cb + 16
                    q = NQ[z][p:p + 64, 0, 128 * cb:128 * cb + 128]
                    k = NQ[z][p:p + 64, 1, :].rearrange("p (r w) -> p r w", r=8)[:, :, bs:bs + 32]
                    bi = BI[z][:, y, :].rearrange("p (a w) -> p a w", a=8)[:, :, o:o + 32]
                    b, bank, w = banks.claim()
                    Q.raw("pe", lambda e: e.matmul(bank[:, 0:256], q, k, start=True, stop=False), w, st["t"])
                    tok = Q.do("pe", lambda e: e.matmul(bank[:, 0:256], anti, bi, start=False, stop=True), st["b"])
                    m = SM[:, 4 * (u % 2):4 * (u % 2) + 1]
                    mask = cst("mask", 256 * (0, 1, 1, 2)[cb], 256)
                    t = Q.do("dve", lambda e: e.tensor_tensor_reduce(SN[u % 2][:, :], bank[:, 0:256], mask, 1.0, -3e38,
                                                                     ALU.add, ALU.max, m), tok, sn_r[u % 2], sm_r[u % 2])
                    banks.release(b, t)
                    te, t = softmax(SN[u % 2][:, :], PN[u % 2][:, :], 256, 1.0, u % 2, None, pn_r[u % 2], in_max=t)
                    sn_r[u % 2] = [te]
                    if u == 7:
                        nq_r[z], bi_r[z] = [tok], [tok]
                    return t

                def turn(u, t):
                    y, cb = u // 4, u % 4
                    p = 64 * y
                    tt, tv = turned(NT[u % 2][:, :, :], PN[u % 2], 2, t, nt_r[u % 2])
                    pn_r[u % 2] = [tt]
                    if u == 0:
                        st["o"] = obanks.claim()
                    oj, bank, w = st["o"]
                    Q.wait("pe", w if u == 0 else [], tv, st["v"])
                    for j in range(2):
                        a = (2 * cb + j) * 128 + p
                        tok = Q.do("pe", lambda e, j=j, a=a: e.matmul(
                            bank[p:p + 64, 128 * cb:128 * cb + 128], NV[z][:, a:a + 64], NT[u % 2][:, j, :],
                            start=(j == 0), stop=(j == 1), skip_group_check=True))
                    nt_r[u % 2] = [tok]
                    if u == 7:
                        nv_r[z] = [tok]
                        src = bank.rearrange("p (c r i) -> p r c i", c=4, r=8)
                        hi = Y3H[:, c, :].rearrange("p (r c i) -> p r c i", r=8, c=4)
                        lo = Y3L[:, c, :].rearrange("p (r c i) -> p r c i", r=8, c=4)
                        y3[c] = halves(hi, lo, src, tok)
                        obanks.release(oj, *y3[c])

                return {"n": 8, "project": project, "score": score, "turn": turn}

            staged([na_pair(c) for c in range(4)])
            pn.close()

            start = Q.now()
            banks.only(*range(8))
            GH = sb("GH", [128, DC, T], R, ph)
            GL = sb("GL", [128, DC, T], R, ph)
            gt = [None] * DC
            gx_r[0], gx_r[1], sq_r[0], sq_r[1] = (list(start) for _ in range(4))
            n = 0
            for d in range(DC):
                acc = SQ[:, d % 2, :]
                for g in range(3):
                    G = GX[:, n % 2, :]
                    b, out, tok = lin([("w2", (22 + 8 * g + d,), 8)], hrhs)
                    t = scaled(G, b, out, tok, free=[gx_r[n % 2]])
                    t = Q.do("act", lambda e, G=G, g=g, d=d: e.activation(G, G, ACT.Sigmoid, bias=vec("bg", 8 * g + d)), t)
                    b, out, tok = lin([("wbr", (g, d), 4)], lambda k, g=g: (Y3H[:, 4 * g + k, :], Y3L[:, 4 * g + k, :],
                                                                         y3[4 * g + k]))
                    if g == 0:
                        ta = Q.do("dve", lambda e, G=G, out=out, acc=acc: e.tensor_tensor(acc, G, out, ALU.mult), t, tok,
                                  sq_r[d % 2])
                        gx_r[n % 2] = [ta]
                        banks.release(b, ta)
                    else:
                        t = Q.do("dve", lambda e, G=G, out=out: e.tensor_tensor(G, G, out, ALU.mult), t, tok)
                        banks.release(b, t)
                        ta = Q.do("pool", lambda e, G=G, acc=acc: e.tensor_tensor(acc, acc, G, ALU.add), t, ta)
                        gx_r[n % 2] = [ta]
                    n += 1
                gt[d] = halves(GH[:, d, :], GL[:, d, :], acc, ta, free=[start])
                sq_r[d % 2] = gt[d]
            for c in range(DC):
                b, out, tok = lin([("w2o", (c,), 8)], lambda k: (GH[:, k, :], GL[:, k, :], gt[k]))
                add_x(c, b, out, tok)
                mean_part(c)
            ph.close()

        def mean_part(c):
            if c == 0:
                sa_t[0] = Q.do("pool", lambda e: e.tensor_copy(SA[:, :], X[:, 0, :]), xt[0], sa_r[0])
            else:
                sa_t[0] = Q.do("pool", lambda e: e.tensor_tensor(SA[:, :], SA[:, :], X[:, c, :], ALU.add), xt[c], sa_t[0])
            xr[c] += [sa_t[0]]

        def layer_norm(g, bb, done=None):
            b, bank, w = banks.claim()
            tp = Q.do("pe", lambda e, bank=bank: e.matmul(bank, ones, SA[:, :], start=True, stop=True), w, sa_t[0])
            sa_r[0] = [tp]
            tm = Q.do("dve", lambda e, bank=bank: e.tensor_scalar(ST[:, :], bank, 1.0 / D, None, ALU.mult), tp, Q.now())
            banks.release(b, tm)
            b, bank, w = banks.claim()
            for c in range(DC):
                t = Q.do("dve", lambda e, c=c: e.tensor_tensor(X[:, c, :], X[:, c, :], ST[:, :], ALU.subtract), tm,
                         xt[c], xr[c])
                xt[c], xr[c] = [t], []
                ts = Q.do("act", lambda e, c=c: e.activation(SQ[:, c % 2, :], X[:, c, :], ACT.Square), t, sq_r[c % 2])
                tp = Q.do("pe", lambda e, c=c: e.matmul(bank, ones, SQ[:, c % 2, :], start=(c == 0), stop=(c == 7)),
                          ts, w if c == 0 else [])
                sq_r[c % 2] = [tp]
                xr[c] = [ts]
            ta = Q.do("act", lambda e: e.activation(ST[:, :], bank, ACT.Sqrt, bias=vec("eps", 1), scale=1.0 / D), tp, t)
            banks.release(b, ta)
            tr = Q.do("dve", lambda e: e.reciprocal(RS[:, :], ST[:, :]), ta, rs_r[0])
            for c in range(DC):
                t = Q.do("dve", lambda e, c=c: e.scalar_tensor_tensor(out=X[:, c, :], in0=X[:, c, :], scalar=vec(g, c),
                                                                      in1=RS[:, :], op0=ALU.mult, op1=ALU.mult),
                         tr, xt[c], xr[c])
                t2 = Q.do("act", lambda e, c=c: e.activation(X[:, c, :], X[:, c, :], ACT.Identity, bias=vec(bb, c)), t)
                xt[c], xr[c] = [t2], []
                if done:
                    done(c)
            rs_r[0] = [t]

        if stop is None or stop > 3:
            ffn(1, "gfin", 0)
            if stop == 4:
                dump()
        if stop is None or stop > 5:
            mixer2()
            layer_norm("l1g", "l1b")
            if stop == 6:
                dump()
        dense.close()

        def experts():
            start = Q.now()
            px = ExitStack()
            SL = [sb(f"SL{i}", [128, 2048], F, px) for i in range(8)]
            GT = sb("GT", [128, 8, T], F, px)
            XS = sb("XS", [128, DC, NE * CAP], F, px)
            pr = ExitStack()
            XNH = sb("XNH", [128, 4, D], R, pr)
            XNL = sb("XNL", [128, 4, D], R, pr)

            loads = []
            for i in range(8):
                for k in range(8):
                    for e2 in range(2):
                        loads.append((I["wgu"][2 * i + e2, 128 * k:128 * k + 128, :], None))
                for k in range(4):
                    for e2 in range(2):
                        loads.append((I["wdn"][2 * i + e2, 256 * k:256 * k + 256, :].rearrange("(a p) n -> p a n", p=128), 2))
            slots = [None] * len(loads)
            free = {}
            nslot = [8]

            def load(i, *waits):
                src, two = loads[i]
                j = i % NSLOT
                dst = SL[j][:, :] if two is None else SL[j][:, :].rearrange("p (a n) -> p a n", a=2)
                slots[i] = (SL[j], Q.dma("sp", dst, src, d_slot[j], *waits))

            for i in range(8):
                load(i, start)

            for tc in range(4):
                for half in range(2):
                    b, bank, w = banks.claim()
                    Q.wait("pe", w, t_in)
                    for j in range(4):
                        c = 4 * half + j
                        tt = Q.do("pe", lambda e, bank=bank, j=j, c=c, tc=tc: e.transpose(
                            bank[:, 128 * j:128 * j + 128], X[:, c, 128 * tc:128 * tc + 128], ident), xt[c])
                    xn_t = halves(XNH[:, tc, 512 * half:512 * half + 512], XNL[:, tc, 512 * half:512 * half + 512],
                                  bank, tt, free=[start])
                    banks.release(b, xn_t)

            pa = ExitStack()
            LT = sb("LT", [16, T], F, pa)
            WK = sb("WK", [16, T], F, pa)
            M1 = sb("M1", [16, T], F, pa)
            M2 = sb("M2", [16, T], F, pa)
            M3 = sb("M3", [16, T], F, pa)
            ON = sb("ON", [16, T], F, pa)
            T8 = sb("T8", [16, 16], F, pa)
            t_on = Q.do("pool", lambda e: e.memset(ON[:, :], 1.0), start)
            b, bank, w = banks.claim()
            for c in range(DC):
                tok = Q.do("pe", lambda e, c=c, bank=bank: e.matmul(bank[0:16, :], WRT[:, c, :], X[:, c, :], start=(c == 0),
                                                         stop=(c == 7)), w if c == 0 else [], xt[c], t_in)
            for c in range(DC):
                xr[c] += [tok]
            t = Q.do("dve", lambda e, bank=bank: e.tensor_copy(LT[:, :], bank[0:16, :]), tok, start)
            banks.release(b, t)
            b, bank, w = banks.claim()
            for j in range(4):
                tt = Q.do("pe", lambda e, j=j, bank=bank: e.transpose(bank[:, 16 * j:16 * j + 16],
                                                                     LT[:, 128 * j:128 * j + 128], ident[0:16, 0:16]),
                          w if j == 0 else [], t)
            lg = AF[:, :].rearrange("p (a e) -> p a e", a=4)
            m4 = SM[:, 0:4]
            bc = SM[:, 0:4].unsqueeze(2).to_broadcast([128, 4, 16])
            t0 = Q.do("dve", lambda e, bank=bank: e.tensor_copy(AF[:, :], bank[:, 0:64]), tt, start)
            banks.release(b, t0)
            t = Q.do("dve", lambda e: e.tensor_reduce(m4, lg, AX.X, ALU.max), t0)
            t = Q.do("dve", lambda e: e.tensor_tensor(lg, lg, bc, ALU.subtract), t)
            ta = Q.do("act", lambda e: e.activation(AF[:, :], AF[:, :], ACT.Exp), t)
            t = Q.do("dve", lambda e: e.tensor_reduce(m4, lg, AX.X, ALU.add), ta)
            t = Q.do("dve", lambda e: e.reciprocal(m4, m4), t)
            t_af = Q.do("dve", lambda e: e.tensor_tensor(lg, lg, bc, ALU.mult), t)
            b, bank, w = banks.claim()
            for j in range(4):
                tt = Q.do("pe", lambda e, j=j, bank=bank: e.transpose(bank[0:16, 128 * j:128 * j + 128],
                                                                     AF[:, 16 * j:16 * j + 16], ident),
                          w if j == 0 else [], t_af)
            t1 = Q.do("dve", lambda e, bank=bank: e.tensor_copy(LT[:, :], bank[0:16, :]), tt)
            t = Q.do("dve", lambda e, bank=bank: e.tensor_copy(WK[:, :], bank[0:16, :]), tt)
            banks.release(b, t)
            for i in range(CAP // 8):
                t = Q.do("dve", lambda e: e.max(T8[:, 0:8], WK[:, :]), t)
                if i < CAP // 8 - 1:
                    t = Q.do("dve", lambda e: e.match_replace(out=WK[:, :], in_to_replace=T8[:, 0:8],
                                                              in_values=WK[:, :], imm_value=-1.0), t)
            thr = T8[:, 7:8]
            t = Q.do("dve", lambda e: e.tensor_scalar(M1[:, :], LT[:, :], thr, None, ALU.is_gt, ALU.add,
                                                      accum_out=T8[:, 8:9]), t, t1)
            t2 = Q.do("dve", lambda e: e.tensor_scalar(M2[:, :], LT[:, :], thr, None, ALU.is_equal), t)
            t3 = Q.do("dve", lambda e: e.tensor_scalar(T8[:, 9:10], T8[:, 8:9], -1.0, float(CAP), ALU.mult, ALU.add), t)
            t = Q.do("dve", lambda e: e.tensor_tensor_scan(M3[:, :], ON[:, :], M2[:, :], 0.0, ALU.mult, ALU.add), t2, t_on)
            t = Q.do("dve", lambda e: e.scalar_tensor_tensor(out=M2[:, :], in0=M3[:, :], scalar=T8[:, 9:10],
                                                             in1=M2[:, :], op0=ALU.is_le, op1=ALU.mult), t, t3)
            t = Q.do("dve", lambda e: e.tensor_tensor(M1[:, :], M1[:, :], M2[:, :], ALU.add), t)
            t = Q.do("dve", lambda e: e.tensor_tensor_scan(M3[:, :], ON[:, :], M1[:, :], 0.0, ALU.mult, ALU.add), t)
            t = Q.do("dve", lambda e: e.tensor_tensor(M3[:, :], M3[:, :], M1[:, :], ALU.mult), t)
            b, bank, w = banks.claim()
            for j in range(4):
                tt = Q.do("pe", lambda e, j=j, bank=bank: e.transpose(bank[:, 16 * j:16 * j + 16],
                                                                     M3[:, 128 * j:128 * j + 128], ident[0:16, 0:16]),
                          w if j == 0 else [], t)
            t_po = Q.do("dve", lambda e, bank=bank: e.tensor_copy(PO[:, :], bank[:, 0:64]), tt, start)
            banks.release(b, t_po)
            pa.close()

            start2 = Q.now()
            PE = sb("PE", [128, 4, NE * CAP], R, pr)
            GG = sb("GGX", [128, NE * CAP], F, pr)
            gg_r = list(start2)
            pe_t = []
            for tc in range(4):
                one = PE[:, tc, :].rearrange("p (e c) -> p e c", e=NE)
                io = cst("iota", 0, 64).unsqueeze(1).to_broadcast([128, NE, CAP])
                po = PO[:, 16 * tc:16 * tc + 16].unsqueeze(2).to_broadcast([128, NE, CAP])
                af = AF[:, 16 * tc:16 * tc + 16].unsqueeze(2).to_broadcast([128, NE, CAP])
                t = Q.do("dve", lambda e, one=one, io=io, po=po: e.tensor_tensor(one, io, po, ALU.is_equal), t_po, start2)
                pe_t.append(t)
                gg = GG[:, :].rearrange("p (e c) -> p e c", e=NE)
                t = Q.do("pool", lambda e, one=one, gg=gg, af=af: e.tensor_tensor(gg, one.bitcast(F), af, ALU.mult), t, gg_r)
                for half in range(2):
                    b, bank, w = banks.claim()
                    for j in range(4):
                        i = 4 * half + j
                        tt = Q.do("pe", lambda e, bank=bank, j=j, i=i: e.transpose(
                            bank[:, 128 * j:128 * j + 128], GG[:, 128 * i:128 * i + 128], ident),
                            w if j == 0 else [], t)
                    gt_t = Q.do("act", lambda e, bank=bank, half=half, tc=tc: e.activation(
                        GT[:, 4 * half:4 * half + 4, 128 * tc:128 * tc + 128],
                        bank.rearrange("p (j q) -> p j q", j=4), ACT.Copy), tt, start2)
                    banks.release(b, gt_t)
                gg_r = [tt]

            xs_t = [[], []]
            for half in range(2):
                for d in range(DC):
                    b, bank, w = banks.claim()
                    Q.wait("pe", w, xn_t, pe_t)
                    for tc in range(4):
                        for P in (XNH, XNL):
                            f = lambda e, bank=bank, tc=tc, P=P, d=d, half=half: e.matmul(
                                bank, P[:, tc, 128 * d:128 * d + 128], PE[:, tc, 512 * half:512 * half + 512],
                                start=(tc == 0 and P is XNH), stop=(tc == 3 and P is XNL))
                            tok = Q.do("pe", f) if (tc == 3 and P is XNL) else Q.raw("pe", f)
                    t = Q.do("act" if d % 2 else "dve", (lambda e, bank=bank, d=d, half=half: e.activation(
                        XS[:, d, 512 * half:512 * half + 512], bank, ACT.Copy)) if d % 2 else
                        (lambda e, bank=bank, d=d, half=half: e.tensor_copy(XS[:, d, 512 * half:512 * half + 512], bank)),
                        tok, start2)
                    banks.release(b, t)
                    xs_t[half].append(t)
            pr.close()
            start3 = Q.now()

            for c in range(DC):
                t = Q.do("dve", lambda e, c=c: e.tensor_scalar(X[:, c, :], X[:, c, :], ALPHA, None, ALU.mult), xt[c], xr[c],
                         start3)
                xt[c], xr[c] = [t], []
            SG = sb("SG", [128, D], F, px)
            HP = sb("HP", [128, D], F, px)
            HT = sb("HT", [128, DC, 128], F, px)
            YS = sb("YS", [128, D], F, px)
            for i in range(8, NSLOT):
                SL.append(sb(f"SL{i}", [128, 2048], F, px))
                load(i, start3)
            sg_r, hp_r, ht_r, ys_r = (list(start3) for _ in range(4))
            at = [0]

            def take():
                i = at[0]
                at[0] += 1
                return i, slots[i][0], slots[i][1]

            def drop(i, tok):
                if i + NSLOT < len(loads):
                    load(i + NSLOT, tok)

            for i in range(8):
                hb = [banks.claim() for _ in range(4)]
                Q.wait("pe", *[h[2] for h in hb], *xs_t[i // 4])
                for k in range(8):
                    two = [take(), take()]
                    Q.wait("pe", two[0][2], two[1][2])
                    for n in range(4):
                        for e2 in range(2):
                            s = two[e2][1]
                            tok = Q.do("pe", lambda e, n=n, e2=e2, s=s, k=k, i=i, bank=hb[n][1]: e.matmul(
                                bank[64 * e2:64 * e2 + 64, :], XS[:, k, (2 * i + e2) * 64:(2 * i + e2) * 64 + 64],
                                s[:, 512 * n:512 * n + 512], start=(k == 0), stop=(k == 7)))
                    drop(two[0][0], tok)
                    drop(two[1][0], tok)
                ht_t = []
                for n in range(2):
                    t = Q.do("act", lambda e, n=n, bank=hb[n][1]: e.activation(SG[:, 512 * n:512 * n + 512], bank, ACT.Silu), tok, sg_r)
                    banks.release(hb[n][0], t)
                    t = Q.do("dve", lambda e, n=n, bank=hb[2 + n][1]: e.tensor_tensor(
                        HP[:, 512 * n:512 * n + 512], SG[:, 512 * n:512 * n + 512], bank, ALU.mult), t, tok, hp_r)
                    banks.release(hb[2 + n][0], t)
                    ht_t.append(t)
                sg_r = [t]
                tts = []
                for half in range(2):
                    tt, tv = turned(HT[:, 4 * half:4 * half + 4, :], HP[:, 512 * half:512 * half + 512], 4,
                                    ht_t[half], ht_r)
                    tts.append(tv)
                hp_r = [tt]
                yb = [banks.claim() for _ in range(2)]
                Q.wait("pe", *[y[2] for y in yb], tts)
                for k in range(4):
                    two = [take(), take()]
                    Q.wait("pe", two[0][2], two[1][2])
                    for a in range(2):
                        for n in range(2):
                            for e2 in range(2):
                                s = two[e2][1]
                                tok = Q.do("pe", lambda e, n=n, e2=e2, s=s, k=k, a=a, bank=yb[n][1]: e.matmul(
                                    bank[64 * e2:64 * e2 + 64, :], HT[:, 2 * k + a, 64 * e2:64 * e2 + 64],
                                    s[:, 1024 * a + 512 * n:1024 * a + 512 * n + 512], start=(k == 0 and a == 0),
                                    stop=(k == 3 and a == 1)))
                    drop(two[0][0], tok)
                    drop(two[1][0], tok)
                ht_r = [tok]
                ty = []
                for n in range(2):
                    t = Q.do("act", lambda e, n=n, bank=yb[n][1]: e.activation(YS[:, 512 * n:512 * n + 512], bank, ACT.Copy), tok, ys_r)
                    banks.release(yb[n][0], t)
                    ty.append(t)
                for d in range(DC):
                    b, bank, w = banks.claim()
                    tok = Q.do("pe", lambda e, d=d, bank=bank, i=i: e.matmul(bank, YS[:, 128 * d:128 * d + 128], GT[:, i, :],
                                                                            start=True, stop=True), w, ty, gt_t)
                    add_x(d, b, bank, tok)
                    if i == 7:
                        mean_part(d)
                ys_r = [tok]
            px.close()

        if stop is None:
            experts()
            outs = []

            def store(c):
                outs.append(Q.dma("sp", OUT[c], X[:, c, :], d_out, xt[c]))

            layer_norm("l2g", "l2b", done=store)
            Q.wait("sp", outs[-1])


        engines = (("sync", "sp"), ("gpsimd", "pool"), ("scalar", "act"), ("vector", "dve"), ("tensor", "pe"))
        with nc.Block() as block:
            def body(key):
                def run(e):
                    for f in Q.q[key]:
                        f(e)
                return run
            block.sync(body("sp"))
            block.gpsimd(body("pool"))
            block.scalar(body("act"))
            block.vector(body("dve"))
            block.tensor(body("pe"))
    return rec
def _consts():
    c = np.zeros((128, NCST), np.float32)
    i = np.arange(128)

    def put(n, a):
        c[:, CST[n]:CST[n] + a.shape[1]] = a

    put("ident", np.eye(128, dtype=np.float32))
    put("ones", np.ones((128, 128), np.float32))
    put("bones", (i[:, None] // 64 == i[None, :] // 64).astype(np.float32))
    put("anti", np.eye(128, dtype=np.float32)[::-1])
    put("tri", (i[:, None] >= i[None, :]).astype(np.float32))
    put("nmask", np.where(i[:, None] < i[None, :], 0.0, -1e30).astype(np.float32))
    sw = np.zeros((128, 128), np.float32)
    sw[i[1::2], i[0::2]] = -1.0
    sw[i[0::2], i[1::2]] = 1.0
    put("swap", sw)
    t = np.arange(T)
    half = 32
    inv = (np.float32(10000.0) ** (-np.arange(0, half, 2, dtype=np.float32) / np.float32(half))).astype(np.float32)
    ang = np.concatenate([(t // 64).astype(np.float32)[:, None] * inv, (t % 64).astype(np.float32)[:, None] * inv], 1)
    ang = ang[:, (i % 64) // 2].T
    put("cos", np.cos(ang).astype(np.float32))
    put("sin", np.sin(ang).astype(np.float32))
    for n, cb in enumerate((0, 1, 3)):
        bs = min(max(cb * 16 - 8, 0), 32)
        col = cb * 16 + i % 16
        st = np.clip(col - 8, 0, 48)
        kc = bs + np.arange(256) % 32
        m = (kc[None, :] >= st[:, None]) & (kc[None, :] < st[:, None] + 16)
        c[:, CST["mask"] + 256 * n:CST["mask"] + 256 * n + 256] = np.where(m, 0.0, -1e30)
    put("iota", np.tile(np.arange(1, 65, dtype=np.float32), (128, 1)))
    return c


def _tiles(w):
    k, n = w.shape
    return np.ascontiguousarray(w.reshape(k // 128, 128, n // 128, 128).transpose(2, 1, 0, 3))


def _layout(a):
    f = {k: np.asarray(v) for k, v in a.items()}
    col = lambda v: np.ascontiguousarray(v.reshape(-1, 128).T)
    vec = np.zeros((128, NVEC), np.float32)

    def put(n, v):
        vec[:, VEC[n]:VEC[n] + v.shape[1]] = v

    put("gmix", col(f["norm_mix_g"]))
    put("gffn", col(f["norm_ffn_g"]))
    put("gfin", col(f["final_g"]))
    put("cw", col(f["a_conv_w"]))
    put("cb", col(f["a_conv_b"]))
    put("br", col(f["a_b_r"]))
    put("bi", col(f["a_b_i"]))
    put("lam", col(f["a_lambda"]))
    put("bg", col(f["b_gate_2"]))
    put("qg", np.concatenate([f["gqa_q_gain_2"]] * 2, 1).T)
    put("kg", np.concatenate([f["gqa_k_gain_2"]] * 2, 1).T)
    put("l1g", col(f["ln1_g_2"]))
    put("l1b", col(f["ln1_b_2"]))
    put("l2g", col(f["ln2_g_2"]))
    put("l2b", col(f["ln2_b_2"]))
    vec[:, VEC["eps"]] = RMS_EPS
    vec[:, VEC["eps"] + 1] = LN_EPS
    rows = lambda m: np.ascontiguousarray(m.T.reshape(-1, 128, m.shape[0]).transpose(1, 0, 2))
    heads = np.array([0, 4, 1, 5, 2, 6, 3, 7])
    order = (heads[:, None] * 64 + np.arange(64)).ravel()
    w2 = f["w_in_2"][0]
    w2 = np.concatenate([w2[:, :1536], w2[:, 1536 + order], w2[:, 2048:]], 1)
    wb = f["w_branch_2"][0].copy()
    wb[1] = wb[1][order]
    wr, wi = f["a_w_r"][0], f["a_w_i"][0]
    wri = np.stack([np.stack([_tiles(w[n]) for w in (wr, wi)]) for n in range(4)])
    wri = np.ascontiguousarray(wri.transpose(0, 3, 1, 2, 4, 5).reshape(4, 128, 8, 128))
    wd = f["ffn_w_down"]
    rpb = np.zeros(16 + 8 * 465 + 32, np.float32)
    rpb[16:16 + 3720] = f["na_rpb_2"].reshape(-1)
    return {
        "x": rows(f["x"][0]),
        "mem": rows(f["mem_2"][0]),
        "vec": vec,
        "cst": _consts(),
        "win": _tiles(f["a_w_in"][0]),
        "wri": wri,
        "wout": _tiles(f["a_w_out"][0]),
        "wg": np.stack([_tiles(w) for w in f["ffn_w_gate"]]),
        "wu": np.stack([_tiles(w) for w in f["ffn_w_up"]]),
        "wd": np.stack([np.stack([_tiles(w[:1408]), _tiles(w[1408:])]) for w in wd]),
        "wqkv": _tiles(f["b_w_qkv"][0]),
        "wbo": _tiles(f["b_w_out"][0]),
        "w2": _tiles(w2),
        "wmkv": _tiles(f["w_mem_kv_2"][0]),
        "wbr": np.stack([_tiles(w) for w in wb]),
        "w2o": _tiles(f["w_out_2"][0]),
        "rpb": rpb,
        "wrt": np.ascontiguousarray(f["w_router_2"][0].reshape(8, 128, 16).transpose(1, 0, 2)),
        "wgu": np.ascontiguousarray(f["w_gate_up_2"][0]),
        "wdn": np.ascontiguousarray(f["w_down_2"][0]),
    }


def _build(nc, arrays, plan, stop=None):
    aps = {n: nc.dram_tensor(f"in_{n}_dram", a.shape, mybir.dt.from_np(a.dtype), kind="ExternalInput").ap()
           for n, a in arrays.items()}
    out = nc.dram_tensor("out_dram", (DC, 128, T), F, kind="ExternalOutput").ap()
    return program(nc, aps, out, plan, stop)


def kernel(**inputs):
    import concourse.bacc as _bacc
    from concourse.bass_utils import run_bass_kernel_spmd as _run

    arrays = _layout(inputs)
    plan = _build(_bacc.Bacc("TRN2", target_bir_lowering=False, num_devices=1), arrays, None)
    nc = _bacc.Bacc("TRN2", target_bir_lowering=False, num_devices=1)
    _build(nc, arrays, plan)
    r = _run(nc, [{f"in_{n}_dram": a for n, a in arrays.items()}], core_ids=[0])
    got = r.results[0]["out_dram"]
    return np.ascontiguousarray(got.reshape(D, T).T)[None]
```

```python
import math
from contextlib import ExitStack

import numpy as np

import concourse.bass as bass
from concourse import mybir

F = mybir.dt.float32
R = mybir.dt.float32r
B16 = mybir.dt.bfloat16
ALU = mybir.AluOpType
ACT = mybir.ActivationFunctionType
AX = mybir.AxisListType

T = 512
D = 1024
DC = 8
FF = 2816
FH = 11
ALPHA = 2.0 ** 0.25
RMS_EPS = 1e-6
LN_EPS = 1e-5
NRAW = 6
NSPL = 3
AHEAD = 2
NE = 16
CAP = 64
NSLOT = 12

VEC = {}
_at = 0
for _n, _w in (("gmix", 16), ("gffn", 16), ("gfin", 8), ("cw", 32), ("cb", 8), ("br", 8), ("bi", 8),
               ("lam", 8), ("bg", 24), ("qg", 1), ("kg", 1), ("l1g", 8), ("l1b", 8), ("l2g", 8),
               ("l2b", 8), ("eps", 2)):
    VEC[_n] = _at
    _at += _w
NVEC = _at

CST = {}
_at = 0
for _n, _w in (("ident", 128), ("ones", 128), ("bones", 128), ("anti", 128), ("tri", 128), ("nmask", 128),
               ("swap", 128), ("cos", 512), ("sin", 512), ("mask", 768), ("iota", 64)):
    CST[_n] = _at
    _at += _w
NCST = _at


class Queues:

    def __init__(self, sems):
        self.sems = sems
        self.q = {e: [] for e in sems}
        self.q["sp"] = []
        self.n = {e: 0 for e in sems}
        self.seen = {}

    def wait(self, eng, *toks):
        for t in toks:
            if t is None:
                continue
            if isinstance(t, list):
                self.wait(eng, *t)
                continue
            name, sem, v = t
            if self.seen.get((eng, name), 0) >= v:
                continue
            self.seen[(eng, name)] = v
            self.q[eng].append(lambda e, s=sem, v=v: e.wait_ge(s, v))

    def do(self, eng, fn, *waits):
        self.wait(eng, *waits)
        self.n[eng] += 1
        sem = self.sems[eng]
        self.q[eng].append(lambda e: fn(e).then_inc(sem, 1))
        return (eng, sem, self.n[eng])

    def raw(self, eng, fn, *waits):
        self.wait(eng, *waits)
        self.q[eng].append(fn)

    def dma(self, eng, dst, src, ds, *waits):
        self.wait(eng, *waits)
        ds.n += 16
        self.q[eng].append(lambda e: e.dma_start(dst, src).then_inc(ds.sem, 16))
        return (ds.name, ds.sem, ds.n)

    def now(self):
        return [(e, self.sems[e], self.n[e]) for e in self.sems if self.n[e]]


class DmaSem:
    def __init__(self, name, sem):
        self.name, self.sem, self.n = name, sem, 0


class Ring:

    def __init__(self, bufs, after=None):
        self.bufs = bufs
        self.free = [list(after or []) for _ in bufs]
        self.i = 0

    def claim(self):
        j = self.i % len(self.bufs)
        self.i += 1
        w, self.free[j] = self.free[j], None
        assert w is not None, "claimed again before its release"
        return j, self.bufs[j], w

    def release(self, j, *toks):
        self.free[j] = (self.free[j] or []) + list(toks)


def program(nc, I, OUT, plan, stop=None):
    ctx = ExitStack()
    rec = []
    with ctx:
        def sb(name, shape, dt=F, cx=None):
            return (cx or ctx).enter_context(nc.sbuf_tensor(name, shape, dt))

        def sem(name):
            return ctx.enter_context(nc.semaphore(name))

        Q = Queues({e: sem("s_" + e) for e in ("pe", "act", "dve", "pool")})
        PS = ctx.enter_context(nc.psum_tensor("PS", [128, 8, 512], F))

        X = sb("X", [128, DC, T])
        V = sb("V", [128, NVEC])
        C = sb("C", [128, NCST])
        RS = sb("RS", [128, T])
        ST = sb("ST", [128, T])
        SQ = sb("SQ", [128, 2, T])
        SA = sb("SA", [128, T])
        LC = sb("LC", [128, 16])
        WRT = sb("WRT", [128, DC, NE])
        AF = sb("AF", [128, 4 * NE])
        PO = sb("PO", [128, 4 * NE])
        SM = sb("SM", [128, 16])
        dense = ExitStack()
        HH = sb("HH", [128, DC, T], R, dense)
        HL = sb("HL", [128, DC, T], R, dense)
        RAW = [sb(f"RAW{i}", [128, 1024], F, dense) for i in range(NRAW)]
        WH = [sb(f"WH{i}", [128, 1024], R, dense) for i in range(NSPL)]
        WL = [sb(f"WL{i}", [128, 1024], R, dense) for i in range(NSPL)]

        d_in = DmaSem("d_in", sem("d_in"))
        d_vec = DmaSem("d_vec", sem("d_vec"))
        d_x = [DmaSem(f"d_x{i}", sem(f"d_x{i}")) for i in range(4)]
        d_raw = [DmaSem(f"d_raw{i}", sem(f"d_raw{i}")) for i in range(NRAW)]
        d_misc = [DmaSem(f"d_misc{i}", sem(f"d_misc{i}")) for i in range(4)]
        d_slot = [DmaSem(f"d_slot{i}", sem(f"d_slot{i}")) for i in range(NSLOT)]
        d_out = DmaSem("d_out", sem("d_out"))

        def vec(n, i=0):
            return V[:, VEC[n] + i:VEC[n] + i + 1]

        def cst(n, a=0, w=128):
            return C[:, CST[n] + a:CST[n] + a + w]

        ident, ones, bones, anti = cst("ident"), cst("ones"), cst("bones"), cst("anti")

        t_v = Q.dma("pool", V[:, :], I["vec"], d_vec)
        t_x = [Q.dma("act", X[:, 2 * i:2 * i + 2, :], I["x"][:, 2 * i:2 * i + 2, :], d_x[i]) for i in range(4)]
        Q.dma("act", C[:, :], I["cst"], d_in)
        t_in = Q.dma("act", WRT[:, :, :], I["wrt"], d_in)

        class Banks:
            ring = Ring([PS[:, i, :] for i in range(8)])

            def claim(self):
                j, buf, w = self.ring.claim()
                return (self.ring, j), buf, w

            def release(self, b, *toks):
                b[0].release(b[1], *toks)

            def only(self, *which):
                self.ring = Ring([PS[:, i, :] for i in which], Q.now())

        banks = Banks()

        raw_at = {}
        raws = Ring(RAW)
        spls = Ring(list(zip(WH, WL)))
        ready = {}
        count = [0]
        hi_on = ["dve"]

        def load_unit(i):
            name, idx, nt = plan[i]
            j, buf, w = raws.claim()
            src = I[name][idx].rearrange("p a b -> p (a b)")
            raw_at[i] = (j, buf, Q.dma("sp", buf[:, 0:nt * 128], src, d_raw[j], *w))

        def split_unit(i):
            nt = plan[i][2]
            n = nt * 128
            rj, buf, t_raw = raw_at.pop(i)
            j, (wh, wl), w = spls.claim()
            if hi_on[0] == "act":
                t_hi = Q.do("act", lambda e: e.activation(wh[:, 0:n], buf[:, 0:n], ACT.Copy), t_raw, w)
            else:
                t_hi = Q.do("dve", lambda e: e.tensor_copy(wh[:, 0:n], buf[:, 0:n]), t_raw, w)
            t_lo = Q.do("dve", lambda e: e.tensor_tensor(wl[:, 0:n], buf[:, 0:n], wh[:, 0:n].bitcast(F), ALU.subtract),
                        t_hi, t_raw, w)
            raws.release(rj, t_lo)
            if i + NRAW < len(plan):
                load_unit(i + NRAW)
            ready[i] = (j, wh, wl, t_hi, t_lo)

        def use(name, idx, nt):
            i = count[0]
            count[0] += 1
            rec.append((name, idx, nt))
            if plan is None:
                return (0, WH[0], WL[0], None, None)
            assert plan[i] == (name, idx, nt)
            if i + AHEAD < len(plan):
                split_unit(i + AHEAD)
            return ready.pop(i)

        def mm3(out, wh, wl, xh, xl, start, stop, waits):
            Q.wait("pe", *waits)
            Q.raw("pe", lambda e: e.matmul(out, wh, xh, start=start, stop=False))
            Q.raw("pe", lambda e: e.matmul(out, wh, xl, start=False, stop=False))
            return Q.do("pe", lambda e: e.matmul(out, wl, xh, start=False, stop=stop))

        def lin(units, rhs, n=T):
            b, bank, w = banks.claim()
            out = bank[:, 0:n]
            total = sum(u[2] for u in units)
            k = 0
            for name, idx, nt in units:
                j, wh, wl, th, tl = use(name, idx, nt)
                for t in range(nt):
                    xh, xl, tx = rhs(k)
                    tok = mm3(out, wh[:, t * 128:t * 128 + 128], wl[:, t * 128:t * 128 + 128], xh, xl,
                              k == 0, k == total - 1, [w, th, tl, tx])
                    w = []
                    k += 1
                spls.release(j, tok)
            return b, out, tok

        def lin_steps(units, rhs, done, n=T):
            b, bank, w = banks.claim()
            out = bank[:, 0:n]
            total = sum(u[2] for u in units)
            k = 0
            for name, idx, nt in units:
                j, wh, wl, th, tl = use(name, idx, nt)
                for t in range(nt):
                    xh, xl, tx = rhs(k)
                    tok = mm3(out, wh[:, t * 128:t * 128 + 128], wl[:, t * 128:t * 128 + 128], xh, xl,
                              k == 0, k == total - 1, [w, th, tl, tx])
                    w = []
                    k += 1
                    if t == nt - 1:
                        spls.release(j, tok)
                    if k == total:
                        done(b, out, tok)
                    if k % 4 == 0 or k == total:
                        yield

        def step(gen, n=1):
            for _ in range(n):
                if gen is not None:
                    next(gen, None)

        def finish(gen):
            for _ in gen:
                pass

        xt = [[t_v, t_x[c // 2]] for c in range(DC)]
        xr = [[] for _ in range(DC)]
        ht = [None] * DC
        hr = [[] for _ in range(DC)]
        rs_t = [None]
        rs_r = [[]]
        sq_r = [[], []]
        sa_r = [[]]

        def norm_start(c, g, gi):
            t = Q.do("act", lambda e: e.activation(SQ[:, c % 2, :], X[:, c, :], ACT.Square), xt[c], sq_r[c % 2])
            if c == 0:
                t2 = Q.do("pool", lambda e: e.tensor_copy(SA[:, :], SQ[:, 0, :]), t, sa_r[0])
            else:
                t2 = Q.do("pool", lambda e: e.tensor_tensor(SA[:, :], SA[:, :], SQ[:, c % 2, :], ALU.add),
                          t, sa_t[0])
            sa_t[0] = t2
            sq_r[c % 2] = [t2]
            tg = Q.do("dve", lambda e: e.tensor_scalar(GX[:, c % 2, :], X[:, c, :], vec(g, gi + c), None, ALU.mult),
                      xt[c], gx_r[c % 2])
            th = Q.do("act", lambda e: e.activation(HH[:, c, :], GX[:, c % 2, :], ACT.Copy), tg, hr[c])
            tl = Q.do("dve", lambda e: e.tensor_tensor(HL[:, c, :], GX[:, c % 2, :], HH[:, c, :].bitcast(F),
                                                       ALU.subtract), th, hr[c])
            gx_r[c % 2] = [tl]
            xr[c] += [t, tg]
            hr[c] = []
            ht[c] = [th, tl]

        def norm_rest():
            b, bank, w = banks.claim()
            tp = Q.do("pe", lambda e: e.matmul(bank, ones, SA[:, :], start=True, stop=True), w, sa_t[0], t_in)
            sa_r[0] = [tp]
            ta = Q.do("act", lambda e: e.activation(ST[:, :], bank, ACT.Sqrt, bias=vec("eps", 0), scale=1.0 / D),
                      tp, rs_t[0])
            banks.release(b, ta)
            rs_t[0] = Q.do("dve", lambda e: e.reciprocal(RS[:, :], ST[:, :]), ta, rs_r[0])
            rs_r[0] = []

        sa_t = [None]
        GX = sb("GX", [128, 2, T], F, dense)
        gx_r = [[], []]

        def hrhs(k):
            return HH[:, k, :], HL[:, k, :], ht[k]

        def add_x(c, b, out, tok, mul=1.0):
            if mul == 1.0:
                t = Q.do("dve", lambda e: e.tensor_tensor(X[:, c, :], X[:, c, :], out, ALU.add), tok, xt[c], xr[c])
            else:
                t = Q.do("dve", lambda e: e.scalar_tensor_tensor(out=X[:, c, :], in0=out, scalar=mul, in1=X[:, c, :],
                                                                 op0=ALU.mult, op1=ALU.add), tok, xt[c], xr[c])
            banks.release(b, t)
            xt[c], xr[c] = [t], []

        def scaled(dst, b, out, tok, mul=1.0, free=()):
            n = out.shape[-1]
            if mul == 1.0:
                t = Q.do("dve", lambda e: e.tensor_tensor(dst, out, RS[:, 0:n], ALU.mult), tok, rs_t[0], *free)
            else:
                t = Q.do("dve", lambda e: e.scalar_tensor_tensor(out=dst, in0=out, scalar=mul, in1=RS[:, 0:n],
                                                                 op0=ALU.mult, op1=ALU.mult), tok, rs_t[0], *free)
            banks.release(b, t)
            rs_r[0] = [t]
            return t

        def halves(hi, lo, src, tok, free=()):
            th = Q.do("act", lambda e: e.activation(hi, src, ACT.Copy), tok, *free)
            tl = Q.do("dve", lambda e: e.tensor_tensor(lo, src, hi.bitcast(F), ALU.subtract), th, tok, *free)
            return [th, tl]

        def natural(dst, parts, waits, free):
            b, bank, w = banks.claim()
            Q.wait("pe", w, waits, t_in)
            n = len(parts)
            for j, src in enumerate(parts):
                tt = Q.do("pe", lambda e, j=j, src=src: e.transpose(bank[:, 128 * j:128 * j + 128], src, ident))
            tv = Q.do("dve", lambda e: e.tensor_copy(dst, bank[:, 0:128 * n]), tt, free)
            banks.release(b, tv)
            return tv

        def dump():
            t = Q.dma("sp", OUT.rearrange("c p t -> p c t"), X[:, :, :], d_out, Q.now())
            Q.wait("sp", t)

        if plan is not None:
            for k in range(NRAW):
                load_unit(k)
        norm_start(0, "gmix", 0)
        if plan is not None:
            split_unit(0)
        for c in range(1, DC):
            norm_start(c, "gmix", 0)
            if plan is not None and c == 4:
                split_unit(1)
        ph = ExitStack()
        YH = sb("YH", [128, DC, T], R, ph)
        YL = sb("YL", [128, DC, T], R, ph)
        XB = [sb(f"XB{i}", [128, T + 4], F, ph) for i in range(2)]
        XC = [sb(f"XC{i}", [128, T], F, ph) for i in range(4)]
        XCH = [sb(f"XCH{i}", [128, T], R, ph) for i in range(4)]
        XCL = [sb(f"XCL{i}", [128, T], R, ph) for i in range(4)]
        GG = [sb(f"GG{i}", [128, T], F, ph) for i in range(2)]
        RI = [sb(f"RI{i}", [128, 2, T], F, ph) for i in range(2)]
        TA = [sb(f"TA{i}", [128, 3, T], F, ph) for i in range(2)]
        tz = [Q.do("pool", lambda e, i=i: e.memset(XB[i][:, 0:4], 0.0)) for i in range(2)]
        xb_r, xc_r, xch_r, gg_r, ri_r, ta_r = ([[] for _ in range(4)] for _ in range(6))
        xc_t, xcs_t = [None] * 4, [None] * 4
        yt = [None] * DC

        def conv_part(n, ps):
            for p in ps:
                c, s = 2 * n + p, 2 * (n % 2) + p
                b, out, tok = lin([("win", (8 + c,), 8)], hrhs)
                if n == 0 and p == 0:
                    norm_rest()
                tb = scaled(XB[p][:, 4:T + 4], b, out, tok, free=[tz[p], xb_r[p]])
                t = Q.do("dve", lambda e, p=p, c=c, s=s: e.tensor_scalar(
                    XC[s][:, :], XB[p][:, 4:T + 4], vec("cw", 24 + c), vec("cb", c), ALU.mult, ALU.add), tb, xc_r[s])
                for j in (2, 1, 0):
                    t = Q.do("dve", lambda e, p=p, c=c, s=s, j=j: e.scalar_tensor_tensor(
                        out=XC[s][:, :], in0=XB[p][:, 1 + j:T + 1 + j], scalar=vec("cw", 8 * j + c), in1=XC[s][:, :],
                        op0=ALU.mult, op1=ALU.add), t)
                xb_r[p] = [t]
                xc_t[s] = t
                xcs_t[s] = halves(XCH[s][:, :], XCL[s][:, :], XC[s][:, :], t, free=[xch_r[s]])

        def gates_part(n):
            j, wh, wl, th, tl = use("wri", (n,), 8)
            rib = []
            for p in range(2):
                for w in range(2):
                    b, bank, wt = banks.claim()
                    for k in range(2):
                        m = (w * 2 + p) * 2 + k
                        s = 2 * (n % 2) + k
                        tok = mm3(bank, wh[:, m * 128:m * 128 + 128], wl[:, m * 128:m * 128 + 128],
                                  XCH[s][:, :], XCL[s][:, :], k == 0, k == 1, [wt, th, tl, xcs_t[s]])
                    rib.append((b, bank, tok))
            spls.release(j, tok)
            for k in range(2):
                xch_r[2 * (n % 2) + k] = [tok]
            ts = []
            for p in range(2):
                for w in range(2):
                    b, bank, tok = rib[2 * p + w]
                    t = Q.do("act", lambda e, p=p, w=w, bank=bank: e.activation(
                        RI[p][:, w, :], bank, ACT.Sigmoid, bias=vec(("br", "bi")[w], 2 * n + p)), tok, ri_r[p])
                    banks.release(b, t)
                    ts.append(t)
            ats = []
            for p in range(2):
                c, s = 2 * n + p, 2 * (n % 2) + p
                a, tt, u = TA[p][:, 0, :], TA[p][:, 1, :], TA[p][:, 2, :]
                t_a = Q.do("act", lambda e, p=p, c=c, a=a: e.activation(a, RI[p][:, 0, :], ACT.Exp, scale=LC[:, c:c + 1]),
                           ts[2 * p], t_lc, ta_r[p])
                t_t = Q.do("act", lambda e, p=p, c=c, tt=tt: e.activation(tt, RI[p][:, 0, :], ACT.Tanh,
                                                                          scale=LC[:, 8 + c:9 + c]), ts[2 * p], t_lc, ta_r[p])
                t_q = Q.do("act", lambda e, a=a, u=u: e.activation(u, a, ACT.Square), t_a, ta_r[p])
                t_ix = Q.do("pool", lambda e, p=p, s=s: e.tensor_tensor(RI[p][:, 1, :], RI[p][:, 1, :], XC[s][:, :], ALU.mult),
                            ts[2 * p + 1], xc_t[s])
                xc_r[s] = [t_ix]
                ats.append((t_q, t_ix, t_a, t_t))
            return ats

        def scan_a(n, ats):
            gt_ = []
            for p in range(2):
                b, out, tok = lin([("win", (2 * n + p,), 8)], hrhs)
                tg = scaled(GG[p][:, :], b, out, tok, free=[gg_r[p]])
                if p == 0:
                    for p2 in range(2):
                        tt, u = TA[p2][:, 1, :], TA[p2][:, 2, :]
                        t_q, t_ix, t_a, t_t = ats[p2]
                        t1 = Q.do("dve", lambda e, u=u, tt=tt: e.scalar_tensor_tensor(
                            out=u, in0=u, scalar=1.0, in1=tt, op0=ALU.add, op1=ALU.mult), t_q, t_t)
                        t1 = Q.do("dve", lambda e, u=u: e.tensor_scalar(u, u, 0.0, None, ALU.max), t1)
                        t1 = Q.do("act", lambda e, u=u: e.activation(u, u, ACT.Sqrt), t1)
                        ats[p2] = (t1, t_ix, t_a, t_t)
                gt_.append(tg)
            for p in range(2):
                gt_[p] = Q.do("act", lambda e, p=p: e.activation(GG[p][:, :], GG[p][:, :], ACT.Gelu_apprx_tanh), gt_[p])
            return ats, gt_

        def scan_b(n, ats, gt_):
            for p in range(2):
                u = TA[p][:, 2, :]
                t1, t_ix, t_a, t_t = ats[p]
                t1 = Q.do("pool", lambda e, p=p, u=u: e.tensor_tensor(u, u, RI[p][:, 1, :], ALU.mult), t1, t_ix)
                ri_r[p] = [t1, t_t, t_a]
                ats[p] = t1
            for p in range(2):
                a, tt, u = TA[p][:, 0, :], TA[p][:, 1, :], TA[p][:, 2, :]
                t1 = Q.do("dve", lambda e, a=a, u=u, tt=tt: e.tensor_tensor_scan(tt, a, u, 0.0, ALU.mult, ALU.add),
                          ats[p], ri_r[p])
                t1 = Q.do("dve", lambda e, p=p, tt=tt: e.tensor_tensor(tt, tt, GG[p][:, :], ALU.mult), t1, gt_[p])
                gg_r[p] = [t1]
                yt[2 * n + p] = halves(YH[:, 2 * n + p, :], YL[:, 2 * n + p, :], tt, t1)
                ta_r[p] = yt[2 * n + p]

        conv_part(0, (0, 1))
        lam = V[:, VEC["lam"]:VEC["lam"] + 8]
        t = Q.do("act", lambda e: e.activation(LC[:, 8:16], lam, ACT.Abs), t_v)
        t = Q.do("act", lambda e: e.activation(LC[:, 8:16], LC[:, 8:16], ACT.Exp, scale=-1.0), t)
        t = Q.do("act", lambda e: e.activation(LC[:, 8:16], LC[:, 8:16], ACT.Ln, bias=1.0), t)
        t2 = Q.do("dve", lambda e: e.tensor_scalar(LC[:, 0:8], lam, 0.0, 8.0, ALU.min, ALU.mult), t_v)
        t2 = Q.do("dve", lambda e: e.scalar_tensor_tensor(out=LC[:, 0:8], in0=LC[:, 8:16], scalar=-8.0,
                                                          in1=LC[:, 0:8], op0=ALU.mult, op1=ALU.add), t, t2)
        t_lc = Q.do("dve", lambda e: e.tensor_scalar(LC[:, 8:16], LC[:, 0:8], -1.0, None, ALU.mult), t2)
        for n in range(4):
            if n < 3:
                conv_part(n + 1, (0,))
            if n > 0:
                scan_b(n - 1, *pend)
            if n < 3:
                conv_part(n + 1, (1,))
            pend = scan_a(n, gates_part(n))
        scan_b(3, *pend)
        for c in range(DC):
            hr[c] = [("pe", Q.sems["pe"], Q.n["pe"])]

        hi_on[0] = "act"

        def out_proj(name, g, gi):
            for c in range(DC):
                b, out, tok = lin([(name, (c,), 8)], lambda k: (YH[:, k, :], YL[:, k, :], yt[k]))
                add_x(c, b, out, tok)
                norm_start(c, g, gi)

        out_proj("wout", "gffn", 0)
        ph.close()
        if stop == 1:
            dump()

        def ffn(l, g, gi):
            ph = ExitStack()
            start = Q.now()
            MH = sb(f"MH{l}", [128, FH, T], R, ph)
            ML = sb(f"ML{l}", [128, FH, T], R, ph)
            G1 = sb(f"G1{l}", [128, 2, T], F, ph)
            S1 = sb(f"S1{l}", [128, 2, T], F, ph)
            U1 = sb(f"U1{l}", [128, 2, T], F, ph)
            g_r, s_r, u_r = ([list(start), list(start)] for _ in range(3))
            m_r = list(start)
            for half in range(2):
                mt = [None] * FH
                for f in range(FH):
                    i = half * FH + f
                    z = f % 2
                    b, out, tok = lin([("wg", (l, i), 8)], hrhs)
                    if i == 0:
                        norm_rest()
                    b2, out2, tok2 = lin([("wu", (l, i), 8)], hrhs)
                    tg = scaled(G1[:, z, :], b, out, tok, free=[g_r[z]])
                    ts = Q.do("act", lambda e, z=z: e.activation(S1[:, z, :], G1[:, z, :], ACT.Silu), tg, s_r[z])
                    g_r[z] = [ts]
                    tu = scaled(U1[:, z, :], b2, out2, tok2, free=[u_r[z]])
                    tm = Q.do("dve", lambda e, z=z: e.tensor_tensor(U1[:, z, :], U1[:, z, :], S1[:, z, :], ALU.mult), tu, ts)
                    s_r[z] = [tm]
                    mt[f] = halves(MH[:, f, :], ML[:, f, :], U1[:, z, :], tm, free=[m_r])
                    u_r[z] = mt[f]
                if half == 1:
                    for c in range(DC):
                        hr[c] = [("pe", Q.sems["pe"], Q.n["pe"])]
                for c in range(DC):
                    b, out, tok = lin([("wd", (l, half, c, slice(None), slice(0, 6)), 6),
                                       ("wd", (l, half, c, slice(None), slice(6, 11)), 5)],
                                      lambda k: (MH[:, k, :], ML[:, k, :], mt[k]))
                    add_x(c, b, out, tok)
                    if half == 1:
                        norm_start(c, g, gi)
                m_r = [tok]
            ph.close()

        if stop is None or stop > 1:
            ffn(0, "gmix", 8)
            if stop == 2:
                dump()

        def sb_mixer():
            ph = ExitStack()
            start = Q.now()
            YH = sb("OH", [128, DC, T], R, ph)
            YL = sb("OL", [128, DC, T], R, ph)
            QK = [sb(f"QK{i}", [128, 3, T], F, ph) for i in range(2)]
            VN = [sb(f"VN{i}", [128, T], F, ph) for i in range(2)]
            AL = sb("AL", [128, 1280], F, ph)
            PP = sb("PP", [128, 1280], F, ph)
            PH = sb("PH", [128, 1280], R, ph)
            PL = sb("PL", [128, 1280], R, ph)
            W = sb("W", [128, 1280], F, ph)
            TR = sb("TR", [128, 256], R, ph)
            IB = sb("IB", [128, 256], B16, ph)
            tc = [Q.do("dve", lambda e: e.tensor_scalar(TR[:, 0:128], cst("tri"), -1.0, None, ALU.mult), start),
                  Q.do("dve", lambda e: e.tensor_scalar(TR[:, 128:256], ones, -1.0, None, ALU.mult), start),
                  Q.do("dve", lambda e: e.tensor_copy(IB[:, 0:128], ident), start),
                  Q.do("dve", lambda e: e.tensor_copy(IB[:, 128:256], cst("nmask")), start)]
            off = [0, 512, 1024, 896]
            wid = [512, 384, 256, 128]
            al_r, pp_r, ph_r, w_r = (list(start) for _ in range(4))
            qk_r, vn_r = [list(start), list(start)], [list(start), list(start)]
            grp = Ring([PS[:, 0:3, :].rearrange("p a b -> p (a b)"), PS[:, 3:6, :].rearrange("p a b -> p (a b)")],
                       start)
            banks.only(6, 7)

            def scores(h):
                c, p = h // 2, 64 * (h % 2)
                z = c % 2
                gj, S, w = grp.claim()
                for j in (0, 1, 3, 2):
                    o, n = off[j], wid[j]
                    Q.wait("pe", w, tc, qk_t[z])
                    Q.raw("pe", lambda e, o=o, n=n, j=j: e.matmul(
                        S[:, o:o + n], QK[z][p:p + 64, 1, 128 * j:128 * j + 128], QK[z][p:p + 64, 0, 128 * j:512],
                        start=(j != 3), stop=False, skip_group_check=True))
                    ml = Q.do("pe", lambda e, o=o: e.matmul(S[:, o:o + 128], IB[:, 0:128], IB[:, 128:256],
                                                           start=False, stop=False, skip_group_check=True))
                return gj, S, ml

            def softplus_a(S, ml):
                nonlocal al_r, pp_r
                t = Q.do("act", lambda e: e.activation(AL[:, :], S[:, 0:1280], ACT.Abs), ml, al_r)
                t = Q.do("act", lambda e: e.activation(AL[:, :], AL[:, :], ACT.Exp, scale=-1.0), t)
                t = Q.do("act", lambda e: e.activation(AL[:, :], AL[:, :], ACT.Ln, bias=1.0), t)
                t = Q.do("dve", lambda e: e.scalar_tensor_tensor(out=PP[:, :], in0=S[:, 0:1280], scalar=0.0,
                                                                 in1=AL[:, :], op0=ALU.max, op1=ALU.add), t, ml, pp_r)
                al_r = [t]
                return t

            def softplus_b(t):
                nonlocal pp_r
                t1 = Q.do("dve", lambda e: e.tensor_copy(PH[:, :], PP[:, :]), t, ph_r)
                t2 = Q.do("dve", lambda e: e.tensor_tensor(PL[:, :], PP[:, :], PH[:, :].bitcast(F), ALU.subtract),
                          t1, ph_r)
                pp_r = [t2]
                return [t1, t2]

            def weights(S, tp):
                nonlocal ph_r
                Q.wait("pe", tp)
                todo = [(j, jj, P) for j in (0, 1, 3, 2) for jj in range(j, 4) for P in (PH, PL)]
                for i, (j, jj, P) in enumerate(todo):
                    lhs = TR[:, 0:128] if jj == j else TR[:, 128:256]
                    o = off[j] + 128 * (jj - j)
                    f = lambda e, o=o, jj=jj, P=P, lhs=lhs: e.matmul(
                        S[:, o:o + wid[jj]], lhs, P[:, off[jj]:off[jj] + wid[jj]], start=False,
                        stop=(jj == 3 and P is PL), skip_group_check=True)
                    if i < len(todo) - 1:
                        Q.raw("pe", f)
                    else:
                        ms = Q.do("pe", f)
                ph_r = [ms]
                return Q.do("act", lambda e: e.activation(W[:, :], S[:, 0:1280], ACT.Exp), ms, w_r)

            def values(h, S, te):
                nonlocal w_r
                p, z = 64 * (h % 2), (h // 2) % 2
                Q.wait("pe", te, vn_t[z])
                for j in range(4):
                    f = lambda e, j=j: e.matmul(S[p:p + 64, 128 * j:512], VN[z][:, 128 * j + p:128 * j + p + 64],
                                                W[:, off[j]:off[j] + wid[j]], start=(j == 0), stop=(j == 3),
                                                skip_group_check=True)
                    if j < 3:
                        Q.raw("pe", f)
                    else:
                        mo = Q.do("pe", f)
                w_r = [mo]
                return mo

            qk_t, vn_t = [None, None], [None, None]
            yts = [[] for _ in range(DC)]

            def project(c):
                z = c % 2
                ts = []

                def done(i):
                    def f(b, out, tok):
                        if c == 0 and i == 0:
                            norm_rest()
                        ts.append(scaled(QK[z][:, i, :], b, out, tok, mul=0.125 if i == 0 else 1.0, free=[qk_r[z]]))
                        if i == 1:
                            qk_t[z] = list(ts)
                        if i == 2:
                            vn_t[z] = natural(VN[z][:, :], [QK[z][:, 2, 128 * j:128 * j + 128] for j in range(4)],
                                              ts, vn_r[z])
                    return f

                for i in range(3):
                    yield from lin_steps([("wqkv", (8 * i + c,), 8)], hrhs, done(i))

            finish(project(0))
            gen = None
            g, S, m = scores(0)
            tp = softplus_b(softplus_a(S, m))
            for h in range(2 * DC):
                c, p, z = h // 2, 64 * (h % 2), (h // 2) % 2
                if p == 0:
                    gen = project(c + 1) if c + 1 < DC else None
                step(gen, 2)
                if h + 1 < 2 * DC:
                    g1, S1, m1 = scores(h + 1)
                    if p == 0:
                        qk_r[z] = [m1, vn_t[z]]
                    ta = softplus_a(S1, m1)
                te = weights(S, tp)
                if h + 1 < 2 * DC:
                    tp = softplus_b(ta)
                step(gen, 1)
                mo = values(h, S, te)
                if p:
                    vn_r[z] = [mo]
                t = halves(YH[p:p + 64, c, :], YL[p:p + 64, c, :], S[p:p + 64, 0:512], mo, free=[start])
                yts[c] += t
                grp.release(g, *t)
                if h + 1 < 2 * DC:
                    g, S = g1, S1
            for c in range(DC):
                hr[c] = [("pe", Q.sems["pe"], Q.n["pe"])]
            banks.only(*range(8))
            for c in range(DC):
                b, out, tok = lin([("wbo", (c,), 8)], lambda k: (YH[:, k, :], YL[:, k, :], yts[k]))
                add_x(c, b, out, tok)
                norm_start(c, "gffn", 8)
            ph.close()

        if stop is None or stop > 2:
            sb_mixer()
            if stop == 3:
                dump()
        def softmax(S, P, n, scale, k, ready, free, in_max=None, s_free=None):
            m, nm, su, ri = (SM[:, 4 * k + i:4 * k + i + 1] for i in range(4))
            if in_max is None:
                t = Q.do("dve", lambda e: e.tensor_reduce(m, S, AX.X, ALU.max), ready, sm_r[k])
            else:
                t = in_max
            t = Q.do("dve", lambda e: e.tensor_scalar(nm, m, -scale, None, ALU.mult), t, sm_r[k])
            t = te = Q.do("act", lambda e: e.activation(P, S, ACT.Exp, bias=nm, scale=scale, accum_out=su), t, free)
            t = Q.do("dve", lambda e: e.reciprocal(ri, su), t)
            t = Q.do("dve", lambda e: e.tensor_scalar(P, P, ri, None, ALU.mult), t)
            sm_r[k] = [t]
            return te, t

        def turned(dst, P, n, waits, free):
            b, bank, w = banks.claim()
            Q.wait("pe", w, waits)
            for j in range(n):
                f = lambda e, j=j: e.transpose(bank[:, 128 * j:128 * j + 128], P[:, 128 * j:128 * j + 128], ident)
                if j < n - 1:
                    Q.raw("pe", f)
                else:
                    tt = Q.do("pe", f)
            src = bank[:, 0:128 * n].rearrange("p (j q) -> p j q", j=n)
            tv = Q.do("act", lambda e: e.activation(dst, src, ACT.Copy), tt, free)
            banks.release(b, tv)
            return tt, tv

        def staged(groups, work, counts):
            prev = None
            i = 0
            for g in groups + [None]:
                for u in range(g["n"] if g else 1):
                    cur = None
                    if g:
                        while u == 0 and not g["there"]():
                            step(work)
                        cur = (g, u, g["score"](u))
                    step(work, counts[i % len(counts)])
                    i += 1
                    if prev:
                        pg, pu, st = prev
                        pg["turn"](pu, st)
                    prev = cur
            finish(work)

        sm_r = [[] for _ in range(4)]

        def mixer2():
            ph = ExitStack()
            start = Q.now()
            ACC = sb("ACC", [128, DC, T], F, ph)
            YP = [sb(f"YP{i}", [128, 2, 4, T], R, ph) for i in range(2)]
            HB = sb("HB", [128, 24], F, ph)
            pa = ExitStack()
            AT = sb("AT", [128, 4, T], F, pa)
            y3 = [None] * 12
            acc_t = [None] * DC
            yb_r = []
            thb = Q.do("dve", lambda e: e.tensor_scalar(HB[:, :], V[:, VEC["bg"]:VEC["bg"] + 24], 0.5, None, ALU.mult),
                       start)

            def branch(g, d, n):
                G = GX[:, n % 2, :]
                tg = []

                def gate(b, out, tok):
                    t = scaled(G, b, out, tok, free=[gx_r[n % 2]])
                    tg.append(Q.do("act", lambda e: e.activation(G, G, ACT.Tanh, bias=HB[:, 8 * g + d:8 * g + d + 1],
                                                                 scale=0.5), t, thb))

                def product(b, out, tok):
                    if g == 2:
                        t = Q.do("dve", lambda e: e.scalar_tensor_tensor(
                            out=ACC[:, d, :], in0=G, scalar=1.0, in1=out, op0=ALU.add, op1=ALU.mult), tg, tok, start)
                        banks.release(b, t)
                    else:
                        t = Q.do("dve", lambda e: e.scalar_tensor_tensor(
                            out=G, in0=G, scalar=1.0, in1=out, op0=ALU.add, op1=ALU.mult), tg, tok)
                        banks.release(b, t)
                        t = Q.do("dve" if g == 0 else "pool", lambda e: e.tensor_tensor(
                            ACC[:, d, :], ACC[:, d, :], G, ALU.add), t, acc_t[d])
                    gx_r[n % 2] = [t]
                    acc_t[d] = [t]
                    if d == DC - 1:
                        yb_r[:] = [tok]

                yield from lin_steps([("w2", (22 + 8 * g + d,), 8)], hrhs, gate)
                Y = YP[g % 2]
                yield from lin_steps([("wbr", (g, d), 4)], lambda k: (Y[:, 0, k, :], Y[:, 1, k, :], y3[4 * g + k]),
                                     product)

            def branches(g):
                for d in range(DC):
                    yield from branch(g, d, d)
            banks.only(0, 1, 2, 3, 4, 5)
            obanks = Ring([PS[:, 6, :], PS[:, 7, :]], start)

            pm = ExitStack()
            MKV = sb("MKV", [128, 4, 2, 256], F, pm)
            pk = ExitStack()
            MF = sb("MF", [128, 2, 256], F, pk)
            MMH = YP[1][:, 0, :, :].rearrange("p a (b n) -> p (a b) n", n=256)
            MML = YP[1][:, 1, :, :].rearrange("p a (b n) -> p (a b) n", n=256)
            mf_r = [list(start), list(start)]
            mm_t = [None] * DC
            for c in range(DC):
                t = Q.dma("pool", MF[:, c % 2, :], I["mem"][:, c, :], d_misc[c % 2], mf_r[c % 2])
                mm_t[c] = halves(MMH[:, c, :], MML[:, c, :], MF[:, c % 2, :], t, free=[start])
                mf_r[c % 2] = mm_t[c]
            VT = sb("VT", [128, 2, 256], F, pk)
            vt_r = [list(start), list(start)]
            kv_t = [[] for _ in range(4)]
            for h in range(4):
                b, out, tok = lin([("wmkv", (h,), 8)], lambda k: (MMH[:, k, :], MML[:, k, :], mm_t[k]), n=256)
                t = Q.do("dve", lambda e, out=out, h=h: e.tensor_copy(MKV[:, h, 0, :], out), tok, start)
                banks.release(b, t)
                kv_t[h].append(t)
                b, out, tok = lin([("wmkv", (4 + h,), 8)], lambda k: (MMH[:, k, :], MML[:, k, :], mm_t[k]), n=256)
                t = Q.do("dve", lambda e, out=out, h=h: e.tensor_copy(VT[:, h % 2, :], out), tok, vt_r[h % 2])
                banks.release(b, t)
                t = natural(MKV[:, h, 1, :], [VT[:, h % 2, 0:128], VT[:, h % 2, 128:256]], t, start)
                vt_r[h % 2] = [t]
                kv_t[h].append(t)
            pk.close()
            start = Q.now()
            tg = Q.do("dve", lambda e: e.tensor_scalar(LC[:, 0:8], V[:, VEC["gfin"]:VEC["gfin"] + 8], ALPHA, None,
                                                       ALU.mult), start)
            QM = sb("QM", [128, 2, T], F, pm)
            PM = [sb(f"PM{i}", [128, 256], F, pm) for i in range(2)]
            PT = [sb(f"PT{i}", [128, 2, T], F, pm) for i in range(2)]
            qm_r, qm_t = [list(start), list(start)], [None, None]
            pm_r, pt_r, pt_t = [list(start), list(start)], [list(start), list(start)], [[], []]

            started = [-1]

            def mem_head(h):
                z = h % 2

                def done(b, out, tok):
                    if h == 0:
                        norm_rest()
                        for c in range(DC):
                            t = Q.do("dve", lambda e, c=c: e.scalar_tensor_tensor(
                                out=X[:, c, :], in0=X[:, c, :], scalar=LC[:, c:c + 1], in1=RS[:, :], op0=ALU.mult,
                                op1=ALU.mult), tg, rs_t[0], xt[c], xr[c])
                            xt[c], xr[c] = [t], []
                        rs_r[0] = [t]
                    started[0] = h
                    qm_t[z] = scaled(QM[:, z, :], b, out, tok, free=[qm_r[z]])

                def score(u):
                    b, bank, w = banks.claim()
                    tok = Q.do("pe", lambda e: e.matmul(bank[:, 0:256], QM[:, z, 128 * u:128 * u + 128],
                                                        MKV[:, h, 0, :], start=True, stop=True), w, qm_t[z], kv_t[h])
                    te, t = softmax(bank[:, 0:256], PM[u % 2][:, :], 256, 1.0 / math.sqrt(128.0), u % 2, tok,
                                    pm_r[u % 2])
                    banks.release(b, te)
                    return t

                def turn(u, t):
                    tt, tv = turned(PT[z][:, :, 128 * u:128 * u + 128], PM[u % 2], 2, t, pt_r[z])
                    pm_r[u % 2] = [tt]
                    pt_t[z].append(tv)
                    if u == 3:
                        qm_r[z] = [tt]
                        oj, bank, w = obanks.claim()
                        Q.wait("pe", w, pt_t[z])
                        for j in range(2):
                            tok = Q.do("pe", lambda e, j=j: e.matmul(bank, MKV[:, h, 1, 128 * j:128 * j + 128],
                                                                     PT[z][:, j, :], start=(j == 0), stop=(j == 1)))
                        pt_r[z], pt_t[z] = [tok], []
                        y3[8 + h] = halves(YP[0][:, 0, h, :], YP[0][:, 1, h, :], bank, tok, free=[start])
                        obanks.release(oj, *y3[8 + h])

                return {"n": 4, "there": lambda: started[0] >= h, "score": score, "turn": turn,
                        "q": lambda: lin_steps([("w2", (18 + h,), 8)], hrhs, done)}

            heads = [mem_head(h) for h in range(4)]
            finish(heads[0]["q"]())

            KG, VG = AT[:, 0, :], AT[:, 1, :]
            ZG = [AT[:, 2, :], AT[:, 3, :]]
            z_r = [list(start), list(start)]
            st_r = []
            gq = {}

            def rope(key, Z, tile, gain, free):
                st = {}

                def done(b, out, tok):
                    st["z"] = scaled(Z, b, out, tok, free=[free])
                    st["s"] = Q.do("act", lambda e: e.activation(SQ[:, 0, :], Z, ACT.Square), st["z"], sq_r[0])

                yield from lin_steps([("w2", (tile,), 8)], hrhs, done)
                b, bank, w = banks.claim()
                t = Q.do("pe", lambda e, bank=bank: e.matmul(bank, bones, SQ[:, 0, :], start=True, stop=True), st["s"], w)
                sq_r[0] = [t]
                t = Q.do("act", lambda e, bank=bank: e.activation(ST[:, :], bank, ACT.Sqrt, bias=vec("eps", 0),
                                                                  scale=1.0 / 64), t, st_r, rs_t[0])
                banks.release(b, t)
                t = Q.do("dve", lambda e: e.reciprocal(ST[:, :], ST[:, :]), t)
                t = Q.do("dve", lambda e: e.scalar_tensor_tensor(out=Z, in0=Z, scalar=gain, in1=ST[:, :],
                                                                 op0=ALU.mult, op1=ALU.mult), t, st["z"])
                st_r[:] = [t]
                yield
                yield
                b, bank, w = banks.claim()
                t2 = Q.do("pe", lambda e, bank=bank: e.matmul(bank, cst("swap"), Z, start=True, stop=True), t, w)
                t3 = Q.do("dve", lambda e, bank=bank: e.tensor_tensor(SQ[:, 1, :], bank, cst("sin", 0, 512), ALU.mult),
                          t2, sq_r[1])
                banks.release(b, t3)
                t4 = Q.do("dve", lambda e: e.tensor_tensor(Z, Z, cst("cos", 0, 512), ALU.mult), t, t2)
                t5 = Q.do("dve", lambda e: e.tensor_tensor(Z, Z, SQ[:, 1, :], ALU.add), t3, t4)
                sq_r[1] = [t5]
                gq[key] = t5
                yield

            def values_gq():
                def done(b, out, tok):
                    gq["vt"] = scaled(ZG[1], b, out, tok, free=[z_r[1]])

                yield from lin_steps([("w2", (17,), 8)], hrhs, done)
                gq["v"] = natural(VG, [ZG[1][:, 128 * j:128 * j + 128] for j in range(4)], gq["vt"], start)
                z_r[1] = [gq["v"]]

            def mem_work():
                yield from heads[1]["q"]()
                kg = rope("k", KG, 16, vec("kg"), start)
                step(kg, 1)
                yield
                step(kg, 1)
                yield
                yield from heads[2]["q"]()
                step(kg, 3)
                yield
                step(kg, 2)
                vg = values_gq()
                step(vg, 1)
                yield
                step(vg, 1)
                yield
                yield from heads[3]["q"]()
                finish(vg)
                yield from rope("q0", ZG[0], 12, vec("qg"), z_r[0])

            staged(heads, mem_work(), [1])
            pm.close()

            pg = ExitStack()
            start = Q.now()
            PG = [sb(f"PG{i}", [128, T], F, pg) for i in range(2)]
            GT2 = [sb(f"GT2{i}", [128, 4, T], F, pg) for i in range(2)]
            pg_r, gt_r, gt_t = [list(start), list(start)], [list(start), list(start)], [[], []]
            yp1_r = list(start)

            def gqa_pair(c):
                z = c % 2
                st = {}

                def score(u):
                    p, qc = 64 * (u // 4), u % 4
                    b, bank, w = banks.claim()
                    tok = Q.do("pe", lambda e: e.matmul(bank, ZG[z][p:p + 64, 128 * qc:128 * qc + 128], KG[p:p + 64, :],
                                                        start=True, stop=True), w, gq[f"q{c}"], gq["k"])
                    te, t = softmax(bank, PG[u % 2][:, :], T, 0.125, u % 2, tok, pg_r[u % 2])
                    banks.release(b, te)
                    if u == 7:
                        z_r[z] = [tok]
                    return t

                def turn(u, t):
                    p, qc, y = 64 * (u // 4), u % 4, u // 4
                    tt, tv = turned(GT2[y][:, :, 128 * qc:128 * qc + 128], PG[u % 2], 4, t, gt_r[y])
                    pg_r[u % 2] = [tt]
                    gt_t[y].append(tv)
                    if qc == 3:
                        if y == 0:
                            st["o"] = obanks.claim()
                        oj, bank, w = st["o"]
                        Q.wait("pe", w if y == 0 else [], gt_t[y], gq["v"])
                        for j in range(4):
                            tok = Q.do("pe", lambda e, j=j: e.matmul(
                                bank[p:p + 64, :], VG[:, 128 * j + p:128 * j + p + 64], GT2[y][:, j, :],
                                start=(j == 0), stop=(j == 3)))
                        gt_r[y], gt_t[y] = [tok], []
                        if y == 1:
                            y3[4 + c] = halves(YP[1][:, 0, c, :], YP[1][:, 1, c, :], bank, tok, free=[yp1_r])
                            obanks.release(oj, *y3[4 + c])

                return {"n": 8, "there": lambda: f"q{c}" in gq, "score": score, "turn": turn}

            def gqa_work():
                br = branches(2)
                for c in range(1, 4):
                    q = rope(f"q{c}", ZG[c % 2], 12 + c, vec("qg"), z_r[c % 2])
                    step(q, 1)
                    yield
                    step(q, 1)
                    yield
                    step(br, 1)
                    yield
                    step(q, 1)
                    step(br, 1)
                    yield
                    step(br, 1)
                    yield
                    step(q, 3)
                    step(br, 1)
                    yield
                    step(br, 1)
                    yield
                    step(br, 1)
                    yield
                yield from br

            staged([gqa_pair(c) for c in range(4)], gqa_work(), [1])
            pg.close()

            pn = ExitStack()
            start = Q.now()
            NQ = [AT[:, 2 * i:2 * i + 2, :] for i in range(2)]
            yp0_r = list(yb_r) + start
            NB = sb("NB", [128, 4, 256], F, pn)
            NV = [sb(f"NV{i}", [128, 1024], F, pn) for i in range(2)]
            BI = [sb(f"BI{i}", [128, 2, 384], F, pn) for i in range(2)]
            SN = [sb(f"SN{i}", [128, 256], F, pn) for i in range(2)]
            PN = [sb(f"PN{i}", [128, 256], F, pn) for i in range(2)]
            NT = [sb(f"NT{i}", [128, 2, 128], F, pn) for i in range(2)]
            nq_r, bi_r, sn_r, pn_r, nt_r = ([list(start), list(start)] for _ in range(5))
            nv_r, nb_r = [list(start), list(start)], [list(start)]
            band = (0, 8, 24, 32)

            def na_pair(c):
                z = c % 2
                st = {"t": None}

                def bias():
                    for p in range(2):
                        for r in range(8):
                            src = bass.AP(I["rpb"].tensor, (2 * c + p) * 465 + 31 * r, [[1, 16], [31, 8], [1, 48]])
                            dst = BI[z][16 * r:16 * r + 16, p, :].rearrange("i (a w) -> i a w", a=8)
                            st["b"] = Q.dma("pool", dst, src, d_misc[2 + z], bi_r[z])

                def queries(b, out, tok):
                    by = lambda a: a.rearrange("p (r c i) -> p r c i", r=8, c=4)
                    dst = NQ[z][:, 0, :].rearrange("p (c r i) -> p r c i", c=4, r=8)
                    tq = Q.do("dve", lambda e: e.tensor_tensor(dst, by(out), by(RS[:, :]), ALU.mult), tok, rs_t[0],
                              nq_r[z])
                    banks.release(b, tq)
                    st["t"] = [tq]

                def keys(b, out, tok):
                    st["t"].append(scaled(NQ[z][:, 1, :], b, out, tok, mul=0.125, free=[nq_r[z]]))

                def vals(b, out, tok):
                    for cb in range(4):
                        bd = lambda a, cb=cb: a.rearrange("p (r w) -> p r w", r=8)[:, :, band[cb]:band[cb] + 32]
                        t = Q.do("dve", lambda e, cb=cb, bd=bd: e.tensor_tensor(
                            NB[:, cb, :].rearrange("p (r w) -> p r w", r=8), bd(out), bd(RS[:, :]), ALU.mult),
                            tok, rs_t[0], nb_r[0])
                    banks.release(b, t)
                    rs_r[0] = [t]
                    st["nb"] = t

                def project():
                    bias()
                    yield from lin_steps([("w2", (c,), 8)], hrhs, queries)
                    yield from lin_steps([("w2", (4 + c,), 8)], hrhs, keys)
                    yield from lin_steps([("w2", (8 + c,), 8)], hrhs, vals)
                    parts = [NB[:, cb, 128 * hf:128 * hf + 128] for cb in range(4) for hf in range(2)]
                    t1 = natural(NV[z][:, 0:512], parts[0:4], st["nb"], nv_r[z])
                    t2 = natural(NV[z][:, 512:1024], parts[4:8], st["nb"], nv_r[z])
                    nb_r[0] = [t1, t2]
                    st["v"] = [t1, t2]

                def score(u):
                    y, cb = u // 4, u % 4
                    p = 64 * y
                    bs, o = band[cb], band[cb] - 16 * cb + 16
                    q = NQ[z][p:p + 64, 0, 128 * cb:128 * cb + 128]
                    k = NQ[z][p:p + 64, 1, :].rearrange("p (r w) -> p r w", r=8)[:, :, bs:bs + 32]
                    bi = BI[z][:, y, :].rearrange("p (a w) -> p a w", a=8)[:, :, o:o + 32]
                    b, bank, w = banks.claim()
                    Q.raw("pe", lambda e: e.matmul(bank[:, 0:256], q, k, start=True, stop=False), w, st["t"])
                    tok = Q.do("pe", lambda e: e.matmul(bank[:, 0:256], anti, bi, start=False, stop=True), st["b"])
                    m = SM[:, 4 * (u % 2):4 * (u % 2) + 1]
                    mask = cst("mask", 256 * (0, 1, 1, 2)[cb], 256)
                    t = Q.do("dve", lambda e: e.tensor_tensor_reduce(SN[u % 2][:, :], bank[:, 0:256], mask, 1.0, -3e38,
                                                                     ALU.add, ALU.max, m), tok, sn_r[u % 2], sm_r[u % 2])
                    banks.release(b, t)
                    te, t = softmax(SN[u % 2][:, :], PN[u % 2][:, :], 256, 1.0, u % 2, None, pn_r[u % 2], in_max=t)
                    sn_r[u % 2] = [te]
                    if u == 7:
                        nq_r[z], bi_r[z] = [tok], [tok]
                    return t

                def turn(u, t):
                    y, cb = u // 4, u % 4
                    p = 64 * y
                    tt, tv = turned(NT[u % 2][:, :, :], PN[u % 2], 2, t, nt_r[u % 2])
                    pn_r[u % 2] = [tt]
                    if u == 0:
                        st["o"] = obanks.claim()
                    oj, bank, w = st["o"]
                    Q.wait("pe", w if u == 0 else [], tv, st["v"])
                    for j in range(2):
                        a = (2 * cb + j) * 128 + p
                        tok = Q.do("pe", lambda e, j=j, a=a: e.matmul(
                            bank[p:p + 64, 128 * cb:128 * cb + 128], NV[z][:, a:a + 64], NT[u % 2][:, j, :],
                            start=(j == 0), stop=(j == 1), skip_group_check=True))
                    nt_r[u % 2] = [tok]
                    if u == 7:
                        nv_r[z] = [tok]
                        src = bank.rearrange("p (c r i) -> p r c i", c=4, r=8)
                        hi = YP[0][:, 0, c, :].rearrange("p (r c i) -> p r c i", r=8, c=4)
                        lo = YP[0][:, 1, c, :].rearrange("p (r c i) -> p r c i", r=8, c=4)
                        y3[c] = halves(hi, lo, src, tok, free=[yp0_r])
                        obanks.release(oj, *y3[c])

                return {"n": 8, "there": lambda: "v" in st, "score": score, "turn": turn, "qkv": project}

            pairs = [na_pair(c) for c in range(4)]

            def na_work():
                br = branches(1)
                for c, order in ((1, "qqbbbqqqqqbbb"), (2, "qqbbbqqqqq"), (3, "qqbbbqqqqqbbb")):
                    q = pairs[c]["qkv"]()
                    for w in order:
                        step(q if w == "q" else br, 1)
                        yield
                yield from br

            finish(pairs[0]["qkv"]())
            staged(pairs, na_work(), [1, 2])
            pn.close()
            pa.close()

            start = Q.now()
            banks.only(*range(8))
            GH = sb("GH", [128, DC, T], R, ph)
            GL = sb("GL", [128, DC, T], R, ph)
            gt = [None] * DC
            gx_r[0], gx_r[1], sq_r[0], sq_r[1] = (list(start) for _ in range(4))
            for d in range(DC):
                finish(branch(0, d, d))
                gt[d] = halves(GH[:, d, :], GL[:, d, :], ACC[:, d, :], acc_t[d], free=[start])
            for c in range(DC):
                b, out, tok = lin([("w2o", (c,), 8)], lambda k: (GH[:, k, :], GL[:, k, :], gt[k]))
                add_x(c, b, out, tok, 0.5)
                mean_part(c)
            ph.close()

        def mean_part(c):
            if c == 0:
                sa_t[0] = Q.do("pool", lambda e: e.tensor_copy(SA[:, :], X[:, 0, :]), xt[0], sa_r[0])
            else:
                sa_t[0] = Q.do("pool", lambda e: e.tensor_tensor(SA[:, :], SA[:, :], X[:, c, :], ALU.add), xt[c], sa_t[0])
            xr[c] += [sa_t[0]]

        def layer_norm(g, bb, done=None):
            b, bank, w = banks.claim()
            tp = Q.do("pe", lambda e, bank=bank: e.matmul(bank, ones, SA[:, :], start=True, stop=True), w, sa_t[0])
            sa_r[0] = [tp]
            tm = Q.do("dve", lambda e, bank=bank: e.tensor_scalar(ST[:, :], bank, 1.0 / D, None, ALU.mult), tp, Q.now())
            banks.release(b, tm)
            b, bank, w = banks.claim()
            for c in range(DC):
                t = Q.do("dve", lambda e, c=c: e.tensor_tensor(X[:, c, :], X[:, c, :], ST[:, :], ALU.subtract), tm,
                         xt[c], xr[c])
                xt[c], xr[c] = [t], []
                ts = Q.do("act", lambda e, c=c: e.activation(SQ[:, c % 2, :], X[:, c, :], ACT.Square), t, sq_r[c % 2])
                tp = Q.do("pe", lambda e, c=c: e.matmul(bank, ones, SQ[:, c % 2, :], start=(c == 0), stop=(c == 7)),
                          ts, w if c == 0 else [])
                sq_r[c % 2] = [tp]
                xr[c] = [ts]
            ta = Q.do("act", lambda e: e.activation(ST[:, :], bank, ACT.Sqrt, bias=vec("eps", 1), scale=1.0 / D), tp, t)
            banks.release(b, ta)
            tr = Q.do("dve", lambda e: e.reciprocal(RS[:, :], ST[:, :]), ta, rs_r[0])
            for c in range(DC):
                t = Q.do("dve", lambda e, c=c: e.scalar_tensor_tensor(out=X[:, c, :], in0=X[:, c, :], scalar=vec(g, c),
                                                                      in1=RS[:, :], op0=ALU.mult, op1=ALU.mult),
                         tr, xt[c], xr[c])
                t2 = Q.do("act", lambda e, c=c: e.activation(X[:, c, :], X[:, c, :], ACT.Identity, bias=vec(bb, c)), t)
                xt[c], xr[c] = [t2], []
                if done:
                    done(c)
            rs_r[0] = [t]

        if stop is None or stop > 3:
            ffn(1, "gfin", 0)
            if stop == 4:
                dump()
        if stop is None or stop > 5:
            mixer2()
            layer_norm("l1g", "l1b")
            if stop == 6:
                dump()
        dense.close()

        def experts():
            start = Q.now()
            px = ExitStack()
            SL = [sb(f"SL{i}", [128, 2048], F, px) for i in range(8)]
            GT = sb("GT", [128, 8, T], F, px)
            XS = sb("XS", [128, DC, NE * CAP], F, px)
            pr = ExitStack()
            XNH = sb("XNH", [128, 4, D], R, pr)
            XNL = sb("XNL", [128, 4, D], R, pr)

            loads = []
            for i in range(8):
                for k in range(8):
                    for e2 in range(2):
                        loads.append((I["wgu"][2 * i + e2, 128 * k:128 * k + 128, :], None))
                for k in range(4):
                    for e2 in range(2):
                        loads.append((I["wdn"][2 * i + e2, 256 * k:256 * k + 256, :].rearrange("(a p) n -> p a n", p=128), 2))
            slots = [None] * len(loads)
            free = {}
            nslot = [8]

            def load(i, *waits):
                src, two = loads[i]
                j = i % NSLOT
                dst = SL[j][:, :] if two is None else SL[j][:, :].rearrange("p (a n) -> p a n", a=2)
                slots[i] = (SL[j], Q.dma("sp", dst, src, d_slot[j], *waits))

            for i in range(8):
                load(i, start)

            for tc in range(4):
                for half in range(2):
                    b, bank, w = banks.claim()
                    Q.wait("pe", w, t_in)
                    for j in range(4):
                        c = 4 * half + j
                        tt = Q.do("pe", lambda e, bank=bank, j=j, c=c, tc=tc: e.transpose(
                            bank[:, 128 * j:128 * j + 128], X[:, c, 128 * tc:128 * tc + 128], ident), xt[c])
                    xn_t = halves(XNH[:, tc, 512 * half:512 * half + 512], XNL[:, tc, 512 * half:512 * half + 512],
                                  bank, tt, free=[start])
                    banks.release(b, xn_t)

            pa = ExitStack()
            LT = sb("LT", [16, T], F, pa)
            WK = sb("WK", [16, T], F, pa)
            M1 = sb("M1", [16, T], F, pa)
            M2 = sb("M2", [16, T], F, pa)
            M3 = sb("M3", [16, T], F, pa)
            ON = sb("ON", [16, T], F, pa)
            T8 = sb("T8", [16, 16], F, pa)
            t_on = Q.do("pool", lambda e: e.memset(ON[:, :], 1.0), start)
            b, bank, w = banks.claim()
            for c in range(DC):
                tok = Q.do("pe", lambda e, c=c, bank=bank: e.matmul(bank[0:16, :], WRT[:, c, :], X[:, c, :], start=(c == 0),
                                                         stop=(c == 7)), w if c == 0 else [], xt[c], t_in)
            for c in range(DC):
                xr[c] += [tok]
            t = Q.do("dve", lambda e, bank=bank: e.tensor_copy(LT[:, :], bank[0:16, :]), tok, start)
            banks.release(b, t)
            b, bank, w = banks.claim()
            for j in range(4):
                tt = Q.do("pe", lambda e, j=j, bank=bank: e.transpose(bank[:, 16 * j:16 * j + 16],
                                                                     LT[:, 128 * j:128 * j + 128], ident[0:16, 0:16]),
                          w if j == 0 else [], t)
            lg = AF[:, :].rearrange("p (a e) -> p a e", a=4)
            m4 = SM[:, 0:4]
            bc = SM[:, 0:4].unsqueeze(2).to_broadcast([128, 4, 16])
            t0 = Q.do("dve", lambda e, bank=bank: e.tensor_copy(AF[:, :], bank[:, 0:64]), tt, start)
            banks.release(b, t0)
            t = Q.do("dve", lambda e: e.tensor_reduce(m4, lg, AX.X, ALU.max), t0)
            t = Q.do("dve", lambda e: e.tensor_tensor(lg, lg, bc, ALU.subtract), t)
            ta = Q.do("act", lambda e: e.activation(AF[:, :], AF[:, :], ACT.Exp), t)
            t = Q.do("dve", lambda e: e.tensor_reduce(m4, lg, AX.X, ALU.add), ta)
            t = Q.do("dve", lambda e: e.reciprocal(m4, m4), t)
            t_af = Q.do("dve", lambda e: e.tensor_tensor(lg, lg, bc, ALU.mult), t)
            b, bank, w = banks.claim()
            for j in range(4):
                tt = Q.do("pe", lambda e, j=j, bank=bank: e.transpose(bank[0:16, 128 * j:128 * j + 128],
                                                                     AF[:, 16 * j:16 * j + 16], ident),
                          w if j == 0 else [], t_af)
            t1 = Q.do("dve", lambda e, bank=bank: e.tensor_copy(LT[:, :], bank[0:16, :]), tt)
            t = Q.do("dve", lambda e, bank=bank: e.tensor_copy(WK[:, :], bank[0:16, :]), tt)
            banks.release(b, t)
            for i in range(CAP // 8):
                t = Q.do("dve", lambda e: e.max(T8[:, 0:8], WK[:, :]), t)
                if i < CAP // 8 - 1:
                    t = Q.do("dve", lambda e: e.match_replace(out=WK[:, :], in_to_replace=T8[:, 0:8],
                                                              in_values=WK[:, :], imm_value=-1.0), t)
            thr = T8[:, 7:8]
            t = Q.do("dve", lambda e: e.tensor_scalar(M1[:, :], LT[:, :], thr, None, ALU.is_gt, ALU.add,
                                                      accum_out=T8[:, 8:9]), t, t1)
            t2 = Q.do("dve", lambda e: e.tensor_scalar(M2[:, :], LT[:, :], thr, None, ALU.is_equal), t)
            t3 = Q.do("dve", lambda e: e.tensor_scalar(T8[:, 9:10], T8[:, 8:9], -1.0, float(CAP), ALU.mult, ALU.add), t)
            t = Q.do("dve", lambda e: e.tensor_tensor_scan(M3[:, :], ON[:, :], M2[:, :], 0.0, ALU.mult, ALU.add), t2, t_on)
            t = Q.do("dve", lambda e: e.scalar_tensor_tensor(out=M2[:, :], in0=M3[:, :], scalar=T8[:, 9:10],
                                                             in1=M2[:, :], op0=ALU.is_le, op1=ALU.mult), t, t3)
            t = Q.do("dve", lambda e: e.tensor_tensor(M1[:, :], M1[:, :], M2[:, :], ALU.add), t)
            t = Q.do("dve", lambda e: e.tensor_tensor_scan(M3[:, :], ON[:, :], M1[:, :], 0.0, ALU.mult, ALU.add), t)
            t = Q.do("dve", lambda e: e.tensor_tensor(M3[:, :], M3[:, :], M1[:, :], ALU.mult), t)
            b, bank, w = banks.claim()
            for j in range(4):
                tt = Q.do("pe", lambda e, j=j, bank=bank: e.transpose(bank[:, 16 * j:16 * j + 16],
                                                                     M3[:, 128 * j:128 * j + 128], ident[0:16, 0:16]),
                          w if j == 0 else [], t)
            t_po = Q.do("dve", lambda e, bank=bank: e.tensor_copy(PO[:, :], bank[:, 0:64]), tt, start)
            banks.release(b, t_po)
            pa.close()

            start2 = Q.now()
            PE = sb("PE", [128, 4, NE * CAP], R, pr)
            GG = sb("GGX", [128, NE * CAP], F, pr)
            gg_r = list(start2)
            pe_t = []
            for tc in range(4):
                one = PE[:, tc, :].rearrange("p (e c) -> p e c", e=NE)
                io = cst("iota", 0, 64).unsqueeze(1).to_broadcast([128, NE, CAP])
                po = PO[:, 16 * tc:16 * tc + 16].unsqueeze(2).to_broadcast([128, NE, CAP])
                af = AF[:, 16 * tc:16 * tc + 16].unsqueeze(2).to_broadcast([128, NE, CAP])
                t = Q.do("dve", lambda e, one=one, io=io, po=po: e.tensor_tensor(one, io, po, ALU.is_equal), t_po, start2)
                pe_t.append(t)
                gg = GG[:, :].rearrange("p (e c) -> p e c", e=NE)
                t = Q.do("pool", lambda e, one=one, gg=gg, af=af: e.tensor_tensor(gg, one.bitcast(F), af, ALU.mult), t, gg_r)
                for half in range(2):
                    b, bank, w = banks.claim()
                    for j in range(4):
                        i = 4 * half + j
                        tt = Q.do("pe", lambda e, bank=bank, j=j, i=i: e.transpose(
                            bank[:, 128 * j:128 * j + 128], GG[:, 128 * i:128 * i + 128], ident),
                            w if j == 0 else [], t)
                    gt_t = Q.do("act", lambda e, bank=bank, half=half, tc=tc: e.activation(
                        GT[:, 4 * half:4 * half + 4, 128 * tc:128 * tc + 128],
                        bank.rearrange("p (j q) -> p j q", j=4), ACT.Copy), tt, start2)
                    banks.release(b, gt_t)
                gg_r = [tt]

            xs_t = [[], []]
            for half in range(2):
                for d in range(DC):
                    b, bank, w = banks.claim()
                    Q.wait("pe", w, xn_t, pe_t)
                    for tc in range(4):
                        for P in (XNH, XNL):
                            f = lambda e, bank=bank, tc=tc, P=P, d=d, half=half: e.matmul(
                                bank, P[:, tc, 128 * d:128 * d + 128], PE[:, tc, 512 * half:512 * half + 512],
                                start=(tc == 0 and P is XNH), stop=(tc == 3 and P is XNL))
                            tok = Q.do("pe", f) if (tc == 3 and P is XNL) else Q.raw("pe", f)
                    t = Q.do("act" if d % 2 else "dve", (lambda e, bank=bank, d=d, half=half: e.activation(
                        XS[:, d, 512 * half:512 * half + 512], bank, ACT.Copy)) if d % 2 else
                        (lambda e, bank=bank, d=d, half=half: e.tensor_copy(XS[:, d, 512 * half:512 * half + 512], bank)),
                        tok, start2)
                    banks.release(b, t)
                    xs_t[half].append(t)
            pr.close()
            start3 = Q.now()

            for c in range(DC):
                t = Q.do("dve", lambda e, c=c: e.tensor_scalar(X[:, c, :], X[:, c, :], ALPHA, None, ALU.mult), xt[c], xr[c],
                         start3)
                xt[c], xr[c] = [t], []
            SG = sb("SG", [128, D], F, px)
            HP = sb("HP", [128, D], F, px)
            HT = sb("HT", [128, DC, 128], F, px)
            YS = sb("YS", [128, D], F, px)
            for i in range(8, NSLOT):
                SL.append(sb(f"SL{i}", [128, 2048], F, px))
                load(i, start3)
            sg_r, hp_r, ht_r, ys_r = (list(start3) for _ in range(4))
            at = [0]

            def take():
                i = at[0]
                at[0] += 1
                return i, slots[i][0], slots[i][1]

            def drop(i, tok):
                if i + NSLOT < len(loads):
                    load(i + NSLOT, tok)

            for i in range(8):
                hb = [banks.claim() for _ in range(4)]
                Q.wait("pe", *[h[2] for h in hb], *xs_t[i // 4])
                for k in range(8):
                    two = [take(), take()]
                    Q.wait("pe", two[0][2], two[1][2])
                    for n in range(4):
                        for e2 in range(2):
                            s = two[e2][1]
                            tok = Q.do("pe", lambda e, n=n, e2=e2, s=s, k=k, i=i, bank=hb[n][1]: e.matmul(
                                bank[64 * e2:64 * e2 + 64, :], XS[:, k, (2 * i + e2) * 64:(2 * i + e2) * 64 + 64],
                                s[:, 512 * n:512 * n + 512], start=(k == 0), stop=(k == 7)))
                    drop(two[0][0], tok)
                    drop(two[1][0], tok)
                ht_t = []
                for n in range(2):
                    t = Q.do("act", lambda e, n=n, bank=hb[n][1]: e.activation(SG[:, 512 * n:512 * n + 512], bank, ACT.Silu), tok, sg_r)
                    banks.release(hb[n][0], t)
                    t = Q.do("dve", lambda e, n=n, bank=hb[2 + n][1]: e.tensor_tensor(
                        HP[:, 512 * n:512 * n + 512], SG[:, 512 * n:512 * n + 512], bank, ALU.mult), t, tok, hp_r)
                    banks.release(hb[2 + n][0], t)
                    ht_t.append(t)
                sg_r = [t]
                tts = []
                for half in range(2):
                    tt, tv = turned(HT[:, 4 * half:4 * half + 4, :], HP[:, 512 * half:512 * half + 512], 4,
                                    ht_t[half], ht_r)
                    tts.append(tv)
                hp_r = [tt]
                yb = [banks.claim() for _ in range(2)]
                Q.wait("pe", *[y[2] for y in yb], tts)
                for k in range(4):
                    two = [take(), take()]
                    Q.wait("pe", two[0][2], two[1][2])
                    for a in range(2):
                        for n in range(2):
                            for e2 in range(2):
                                s = two[e2][1]
                                tok = Q.do("pe", lambda e, n=n, e2=e2, s=s, k=k, a=a, bank=yb[n][1]: e.matmul(
                                    bank[64 * e2:64 * e2 + 64, :], HT[:, 2 * k + a, 64 * e2:64 * e2 + 64],
                                    s[:, 1024 * a + 512 * n:1024 * a + 512 * n + 512], start=(k == 0 and a == 0),
                                    stop=(k == 3 and a == 1)))
                    drop(two[0][0], tok)
                    drop(two[1][0], tok)
                ht_r = [tok]
                ty = []
                for n in range(2):
                    t = Q.do("act", lambda e, n=n, bank=yb[n][1]: e.activation(YS[:, 512 * n:512 * n + 512], bank, ACT.Copy), tok, ys_r)
                    banks.release(yb[n][0], t)
                    ty.append(t)
                for d in range(DC):
                    b, bank, w = banks.claim()
                    tok = Q.do("pe", lambda e, d=d, bank=bank, i=i: e.matmul(bank, YS[:, 128 * d:128 * d + 128], GT[:, i, :],
                                                                            start=True, stop=True), w, ty, gt_t)
                    add_x(d, b, bank, tok)
                    if i == 7:
                        mean_part(d)
                ys_r = [tok]
            px.close()

        if stop is None:
            experts()
            outs = []

            def store(c):
                outs.append(Q.dma("sp", OUT[c], X[:, c, :], d_out, xt[c]))

            layer_norm("l2g", "l2b", done=store)
            Q.wait("sp", outs[-1])


        engines = (("sync", "sp"), ("gpsimd", "pool"), ("scalar", "act"), ("vector", "dve"), ("tensor", "pe"))
        with nc.Block() as block:
            def body(key):
                def run(e):
                    for f in Q.q[key]:
                        f(e)
                return run
            block.sync(body("sp"))
            block.gpsimd(body("pool"))
            block.scalar(body("act"))
            block.vector(body("dve"))
            block.tensor(body("pe"))
    return rec
def _consts():
    c = np.zeros((128, NCST), np.float32)
    i = np.arange(128)

    def put(n, a):
        c[:, CST[n]:CST[n] + a.shape[1]] = a

    put("ident", np.eye(128, dtype=np.float32))
    put("ones", np.ones((128, 128), np.float32))
    put("bones", (i[:, None] // 64 == i[None, :] // 64).astype(np.float32))
    put("anti", np.eye(128, dtype=np.float32)[::-1])
    put("tri", (i[:, None] >= i[None, :]).astype(np.float32))
    put("nmask", np.where(i[:, None] < i[None, :], 0.0, -1e30).astype(np.float32))
    sw = np.zeros((128, 128), np.float32)
    sw[i[1::2], i[0::2]] = -1.0
    sw[i[0::2], i[1::2]] = 1.0
    put("swap", sw)
    t = np.arange(T)
    half = 32
    inv = (np.float32(10000.0) ** (-np.arange(0, half, 2, dtype=np.float32) / np.float32(half))).astype(np.float32)
    ang = np.concatenate([(t // 64).astype(np.float32)[:, None] * inv, (t % 64).astype(np.float32)[:, None] * inv], 1)
    ang = ang[:, (i % 64) // 2].T
    put("cos", np.cos(ang).astype(np.float32))
    put("sin", np.sin(ang).astype(np.float32))
    for n, cb in enumerate((0, 1, 3)):
        bs = min(max(cb * 16 - 8, 0), 32)
        col = cb * 16 + i % 16
        st = np.clip(col - 8, 0, 48)
        kc = bs + np.arange(256) % 32
        m = (kc[None, :] >= st[:, None]) & (kc[None, :] < st[:, None] + 16)
        c[:, CST["mask"] + 256 * n:CST["mask"] + 256 * n + 256] = np.where(m, 0.0, -1e30)
    put("iota", np.tile(np.arange(1, 65, dtype=np.float32), (128, 1)))
    return c


def _tiles(w):
    k, n = w.shape
    return np.ascontiguousarray(w.reshape(k // 128, 128, n // 128, 128).transpose(2, 1, 0, 3))


def _layout(a):
    f = {k: np.asarray(v) for k, v in a.items()}
    col = lambda v: np.ascontiguousarray(v.reshape(-1, 128).T)
    vec = np.zeros((128, NVEC), np.float32)

    def put(n, v):
        vec[:, VEC[n]:VEC[n] + v.shape[1]] = v

    put("gmix", col(f["norm_mix_g"]))
    put("gffn", col(f["norm_ffn_g"]))
    put("gfin", col(f["final_g"]))
    put("cw", col(f["a_conv_w"]))
    put("cb", col(f["a_conv_b"]))
    put("br", col(f["a_b_r"]))
    put("bi", col(f["a_b_i"]))
    put("lam", col(f["a_lambda"]))
    put("bg", col(f["b_gate_2"]))
    put("qg", np.concatenate([f["gqa_q_gain_2"]] * 2, 1).T)
    put("kg", np.concatenate([f["gqa_k_gain_2"]] * 2, 1).T)
    put("l1g", col(f["ln1_g_2"]))
    put("l1b", col(f["ln1_b_2"]))
    put("l2g", col(f["ln2_g_2"]))
    put("l2b", col(f["ln2_b_2"]))
    vec[:, VEC["eps"]] = RMS_EPS
    vec[:, VEC["eps"] + 1] = LN_EPS
    rows = lambda m: np.ascontiguousarray(m.T.reshape(-1, 128, m.shape[0]).transpose(1, 0, 2))
    heads = np.array([0, 4, 1, 5, 2, 6, 3, 7])
    order = (heads[:, None] * 64 + np.arange(64)).ravel()
    w2 = f["w_in_2"][0]
    w2 = np.concatenate([w2[:, :1536], w2[:, 1536 + order], w2[:, 2048:]], 1)
    wb = f["w_branch_2"][0].copy()
    wb[1] = wb[1][order]
    wr, wi = f["a_w_r"][0], f["a_w_i"][0]
    wri = np.stack([np.stack([_tiles(w[n]) for w in (wr, wi)]) for n in range(4)])
    wri = np.ascontiguousarray(wri.transpose(0, 3, 1, 2, 4, 5).reshape(4, 128, 8, 128))
    wd = f["ffn_w_down"]
    rpb = np.zeros(16 + 8 * 465 + 32, np.float32)
    rpb[16:16 + 3720] = f["na_rpb_2"].reshape(-1)
    return {
        "x": rows(f["x"][0]),
        "mem": rows(f["mem_2"][0]),
        "vec": vec,
        "cst": _consts(),
        "win": _tiles(f["a_w_in"][0]),
        "wri": wri,
        "wout": _tiles(f["a_w_out"][0]),
        "wg": np.stack([_tiles(w) for w in f["ffn_w_gate"]]),
        "wu": np.stack([_tiles(w) for w in f["ffn_w_up"]]),
        "wd": np.stack([np.stack([_tiles(w[:1408]), _tiles(w[1408:])]) for w in wd]),
        "wqkv": _tiles(f["b_w_qkv"][0]),
        "wbo": _tiles(f["b_w_out"][0]),
        "w2": _tiles(w2),
        "wmkv": _tiles(f["w_mem_kv_2"][0]),
        "wbr": np.stack([_tiles(w) for w in wb]),
        "w2o": _tiles(f["w_out_2"][0]),
        "rpb": rpb,
        "wrt": np.ascontiguousarray(f["w_router_2"][0].reshape(8, 128, 16).transpose(1, 0, 2)),
        "wgu": np.ascontiguousarray(f["w_gate_up_2"][0]),
        "wdn": np.ascontiguousarray(f["w_down_2"][0]),
    }


def _build(nc, arrays, plan, stop=None):
    aps = {n: nc.dram_tensor(f"in_{n}_dram", a.shape, mybir.dt.from_np(a.dtype), kind="ExternalInput").ap()
           for n, a in arrays.items()}
    out = nc.dram_tensor("out_dram", (DC, 128, T), F, kind="ExternalOutput").ap()
    return program(nc, aps, out, plan, stop)


def kernel(**inputs):
    import concourse.bacc as _bacc
    from concourse.bass_utils import run_bass_kernel_spmd as _run

    arrays = _layout(inputs)
    plan = _build(_bacc.Bacc("TRN2", target_bir_lowering=False, num_devices=1), arrays, None)
    nc = _bacc.Bacc("TRN2", target_bir_lowering=False, num_devices=1)
    _build(nc, arrays, plan)
    r = _run(nc, [{f"in_{n}_dram": a for n, a in arrays.items()}], core_ids=[0])
    got = r.results[0]["out_dram"]
    return np.ascontiguousarray(got.reshape(D, T).T)[None]
```

```python
import math
from contextlib import ExitStack

import numpy as np

import concourse.bass as bass
from concourse import mybir

F = mybir.dt.float32
R = mybir.dt.float32r
B16 = mybir.dt.bfloat16
ALU = mybir.AluOpType
ACT = mybir.ActivationFunctionType
AX = mybir.AxisListType

T = 512
D = 1024
DC = 8
FF = 2816
FH = 11
ALPHA = 2.0 ** 0.25
RMS_EPS = 1e-6
LN_EPS = 1e-5
NRAW = 6
NSPL = 3
AHEAD = 2
NE = 16
CAP = 64
NSLOT = 14
NGATE = 4

VEC = {}
_at = 0
for _n, _w in (("gmix", 16), ("gffn", 16), ("gfin", 8), ("cw", 32), ("cb", 8), ("br", 8), ("bi", 8),
               ("lam", 8), ("bg", 24), ("qg", 1), ("kg", 1), ("l1g", 8), ("l1b", 8), ("l2g", 8),
               ("l2b", 8), ("eps", 2)):
    VEC[_n] = _at
    _at += _w
NVEC = _at

CST = {}
_at = 0
for _n, _w in (("ident", 128), ("ones", 128), ("bones", 128), ("anti", 128), ("tri", 128), ("nmask", 128),
               ("swap", 128), ("cos", 512), ("sin", 512), ("mask", 768), ("iota", 64)):
    CST[_n] = _at
    _at += _w
NCST = _at


class Queues:

    def __init__(self, sems):
        self.sems = sems
        self.q = {e: [] for e in sems}
        self.q["sp"] = []
        self.n = {e: 0 for e in sems}
        self.seen = {}

    def wait(self, eng, *toks):
        for t in toks:
            if t is None:
                continue
            if isinstance(t, list):
                self.wait(eng, *t)
                continue
            name, sem, v = t
            if self.seen.get((eng, name), 0) >= v:
                continue
            self.seen[(eng, name)] = v
            self.q[eng].append(lambda e, s=sem, v=v: e.wait_ge(s, v))

    def do(self, eng, fn, *waits):
        self.wait(eng, *waits)
        self.n[eng] += 1
        sem = self.sems[eng]
        self.q[eng].append(lambda e: fn(e).then_inc(sem, 1))
        return (eng, sem, self.n[eng])

    def raw(self, eng, fn, *waits):
        self.wait(eng, *waits)
        self.q[eng].append(fn)

    def dma(self, eng, dst, src, ds, *waits):
        self.wait(eng, *waits)
        ds.n += 16
        self.q[eng].append(lambda e: e.dma_start(dst, src).then_inc(ds.sem, 16))
        return (ds.name, ds.sem, ds.n)

    def now(self):
        return [(e, self.sems[e], self.n[e]) for e in self.sems if self.n[e]]


class DmaSem:
    def __init__(self, name, sem):
        self.name, self.sem, self.n = name, sem, 0


class Pool:

    def __init__(self, bufs, after=None):
        self.bufs = bufs
        self.free = [(j, list(after or [])) for j in range(len(bufs))]

    def claim(self):
        j, w = self.free.pop(0)
        return j, self.bufs[j], w

    def release(self, j, *toks):
        assert all(j != f[0] for f in self.free)
        self.free.append((j, list(toks)))


class Ring:

    def __init__(self, bufs, after=None):
        self.bufs = bufs
        self.free = [list(after or []) for _ in bufs]
        self.i = 0

    def claim(self):
        j = self.i % len(self.bufs)
        self.i += 1
        w, self.free[j] = self.free[j], None
        assert w is not None, "claimed again before its release"
        return j, self.bufs[j], w

    def release(self, j, *toks):
        self.free[j] = (self.free[j] or []) + list(toks)


def program(nc, I, OUT, plan):
    ctx = ExitStack()
    rec = []
    with ctx:
        def sb(name, shape, dt=F, cx=None):
            return (cx or ctx).enter_context(nc.sbuf_tensor(name, shape, dt))

        def sem(name):
            return ctx.enter_context(nc.semaphore(name))

        Q = Queues({e: sem("s_" + e) for e in ("pe", "act", "dve", "pool")})
        PS = ctx.enter_context(nc.psum_tensor("PS", [128, 8, 512], F))

        X = sb("X", [128, DC, T])
        V = sb("V", [128, NVEC])
        C = sb("C", [128, NCST])
        RS = sb("RS", [128, T])
        ST = sb("ST", [128, T])
        SQ = sb("SQ", [128, 2, T])
        SA = sb("SA", [128, T])
        LC = sb("LC", [128, 16])
        WRT = sb("WRT", [128, DC, NE])
        AF = sb("AF", [128, 4 * NE])
        PO = sb("PO", [128, 4 * NE])
        SM = sb("SM", [128, 16])
        dense = ExitStack()
        HH = sb("HH", [128, DC, T], R, dense)
        HL = sb("HL", [128, DC, T], R, dense)
        RAW = [sb(f"RAW{i}", [128, 1024], F, dense) for i in range(NRAW)]
        WH = [sb(f"WH{i}", [128, 1024], R, dense) for i in range(NSPL)]
        WL = [sb(f"WL{i}", [128, 1024], R, dense) for i in range(NSPL)]

        d_in = DmaSem("d_in", sem("d_in"))
        d_vec = DmaSem("d_vec", sem("d_vec"))
        d_x = [DmaSem(f"d_x{i}", sem(f"d_x{i}")) for i in range(4)]
        d_raw = [DmaSem(f"d_raw{i}", sem(f"d_raw{i}")) for i in range(NRAW)]
        d_misc = [DmaSem(f"d_misc{i}", sem(f"d_misc{i}")) for i in range(4)]
        d_slot = [DmaSem(f"d_slot{i}", sem(f"d_slot{i}")) for i in range(NSLOT)]
        d_out = DmaSem("d_out", sem("d_out"))

        def vec(n, i=0):
            return V[:, VEC[n] + i:VEC[n] + i + 1]

        def cst(n, a=0, w=128):
            return C[:, CST[n] + a:CST[n] + a + w]

        ident, ones, bones, anti = cst("ident"), cst("ones"), cst("bones"), cst("anti")

        t_v = Q.dma("pool", V[:, :], I["vec"], d_vec)
        t_x = [Q.dma("act", X[:, 2 * i:2 * i + 2, :], I["x"][:, 2 * i:2 * i + 2, :], d_x[i]) for i in range(4)]
        Q.dma("act", C[:, :], I["cst"], d_in)
        t_in = Q.dma("act", WRT[:, :, :], I["wrt"], d_in)

        class Banks:
            ring = Pool([PS[:, i, :] for i in range(8)])

            def claim(self):
                j, buf, w = self.ring.claim()
                return (self.ring, j), buf, w

            def release(self, b, *toks):
                b[0].release(b[1], *toks)

            def only(self, *which):
                self.ring = Pool([PS[:, i, :] for i in which], Q.now())

        banks = Banks()

        raw_at = {}
        raws = Ring(RAW)
        spls = Ring(list(zip(WH, WL)))
        ready = {}
        count = [0]
        hi_on = ["dve"]

        def load_unit(i):
            name, idx, nt = plan[i]
            j, buf, w = raws.claim()
            src = I[name][idx].rearrange("p a b -> p (a b)")
            raw_at[i] = (j, buf, Q.dma("sp", buf[:, 0:nt * 128], src, d_raw[j], *w))

        def split_unit(i):
            nt = plan[i][2]
            n = nt * 128
            rj, buf, t_raw = raw_at.pop(i)
            j, (wh, wl), w = spls.claim()
            if hi_on[0] == "act":
                t_hi = Q.do("act", lambda e: e.activation(wh[:, 0:n], buf[:, 0:n], ACT.Copy), t_raw, w)
            else:
                t_hi = Q.do("dve", lambda e: e.tensor_copy(wh[:, 0:n], buf[:, 0:n]), t_raw, w)
            t_lo = Q.do("dve", lambda e: e.tensor_tensor(wl[:, 0:n], buf[:, 0:n], wh[:, 0:n].bitcast(F), ALU.subtract),
                        t_hi, t_raw, w)
            raws.release(rj, t_lo)
            if i + NRAW < len(plan):
                load_unit(i + NRAW)
            ready[i] = (j, wh, wl, t_hi, t_lo)

        def use(name, idx, nt):
            i = count[0]
            count[0] += 1
            rec.append((name, idx, nt))
            if plan is None:
                return (0, WH[0], WL[0], None, None)
            assert plan[i] == (name, idx, nt)
            if i + AHEAD < len(plan):
                split_unit(i + AHEAD)
            return ready.pop(i)

        def mm3(out, wh, wl, xh, xl, start, stop, waits):
            Q.wait("pe", *waits)
            Q.raw("pe", lambda e: e.matmul(out, wh, xh, start=start, stop=False))
            Q.raw("pe", lambda e: e.matmul(out, wh, xl, start=False, stop=False))
            return Q.do("pe", lambda e: e.matmul(out, wl, xh, start=False, stop=stop))

        def lin(units, rhs, n=T):
            b, bank, w = banks.claim()
            out = bank[:, 0:n]
            total = sum(u[2] for u in units)
            k = 0
            for name, idx, nt in units:
                j, wh, wl, th, tl = use(name, idx, nt)
                for t in range(nt):
                    xh, xl, tx = rhs(k)
                    tok = mm3(out, wh[:, t * 128:t * 128 + 128], wl[:, t * 128:t * 128 + 128], xh, xl,
                              k == 0, k == total - 1, [w, th, tl, tx])
                    w = []
                    k += 1
                spls.release(j, tok)
            return b, out, tok

        def lin_steps(units, rhs, done, n=T):
            b, bank, w = banks.claim()
            out = bank[:, 0:n]
            total = sum(u[2] for u in units)
            k = 0
            for name, idx, nt in units:
                j, wh, wl, th, tl = use(name, idx, nt)
                for t in range(nt):
                    xh, xl, tx = rhs(k)
                    tok = mm3(out, wh[:, t * 128:t * 128 + 128], wl[:, t * 128:t * 128 + 128], xh, xl,
                              k == 0, k == total - 1, [w, th, tl, tx])
                    w = []
                    k += 1
                    if t == nt - 1:
                        spls.release(j, tok)
                    if k == total:
                        done(b, out, tok)
                    if k % 4 == 0 or k == total:
                        yield

        def step(gen, n=1):
            for _ in range(n):
                if gen is not None:
                    next(gen, None)

        def finish(gen):
            for _ in gen:
                pass

        xt = [[t_v, t_x[c // 2]] for c in range(DC)]
        xr = [[] for _ in range(DC)]
        ht = [None] * DC
        hr = [[] for _ in range(DC)]
        rs_t = [None]
        rs_r = [[]]
        sq_r = [[], []]
        sa_r = [[]]

        def norm_start(c, g, gi):
            norm_low(c, norm_high(c, g, gi))

        def norm_high(c, g, gi):
            t = Q.do("act", lambda e: e.activation(SQ[:, c % 2, :], X[:, c, :], ACT.Square), xt[c], sq_r[c % 2])
            if c == 0:
                t2 = Q.do("pool", lambda e: e.tensor_copy(SA[:, :], SQ[:, 0, :]), t, sa_r[0])
            else:
                t2 = Q.do("pool", lambda e: e.tensor_tensor(SA[:, :], SA[:, :], SQ[:, c % 2, :], ALU.add),
                          t, sa_t[0])
            sa_t[0] = t2
            sq_r[c % 2] = [t2]
            tg = Q.do("dve", lambda e: e.tensor_scalar(GX[:, c % 2, :], X[:, c, :], vec(g, gi + c), None, ALU.mult),
                      xt[c], gx_r[c % 2])
            xr[c] += [t, tg]
            return Q.do("act", lambda e: e.activation(HH[:, c, :], GX[:, c % 2, :], ACT.Copy), tg, hr[c])

        def norm_low(c, th):
            tl = Q.do("dve", lambda e: e.tensor_tensor(HL[:, c, :], GX[:, c % 2, :], HH[:, c, :].bitcast(F),
                                                       ALU.subtract), th, hr[c])
            gx_r[c % 2] = [tl]
            hr[c] = []
            ht[c] = [th, tl]

        def norm_rest():
            b, bank, w = banks.claim()
            tp = Q.do("pe", lambda e: e.matmul(bank, ones, SA[:, :], start=True, stop=True), w, sa_t[0], t_in)
            sa_r[0] = [tp]
            ta = Q.do("act", lambda e: e.activation(ST[:, :], bank, ACT.Sqrt, bias=vec("eps", 0), scale=1.0 / D),
                      tp, rs_t[0])
            banks.release(b, ta)
            rs_t[0] = Q.do("dve", lambda e: e.reciprocal(RS[:, :], ST[:, :]), ta, rs_r[0])
            rs_r[0] = []

        sa_t = [None]
        GX = sb("GX", [128, 2, T], F, dense)
        gx_r = [[], []]

        def hrhs(k):
            return HH[:, k, :], HL[:, k, :], ht[k]

        def add_x(c, b, out, tok, mul=1.0):
            if mul == 1.0:
                t = Q.do("dve", lambda e: e.tensor_tensor(X[:, c, :], X[:, c, :], out, ALU.add), tok, xt[c], xr[c])
            else:
                t = Q.do("dve", lambda e: e.scalar_tensor_tensor(out=X[:, c, :], in0=out, scalar=mul, in1=X[:, c, :],
                                                                 op0=ALU.mult, op1=ALU.add), tok, xt[c], xr[c])
            banks.release(b, t)
            xt[c], xr[c] = [t], []

        def scaled(dst, b, out, tok, mul=1.0, free=()):
            n = out.shape[-1]
            if mul == 1.0:
                t = Q.do("dve", lambda e: e.tensor_tensor(dst, out, RS[:, 0:n], ALU.mult), tok, rs_t[0], *free)
            else:
                t = Q.do("dve", lambda e: e.scalar_tensor_tensor(out=dst, in0=out, scalar=mul, in1=RS[:, 0:n],
                                                                 op0=ALU.mult, op1=ALU.mult), tok, rs_t[0], *free)
            banks.release(b, t)
            rs_r[0] = [t]
            return t

        def halves(hi, lo, src, tok, free=()):
            th = Q.do("act", lambda e: e.activation(hi, src, ACT.Copy), tok, *free)
            tl = Q.do("dve", lambda e: e.tensor_tensor(lo, src, hi.bitcast(F), ALU.subtract), th, tok, *free)
            return [th, tl]

        def natural(dst, parts, waits, free):
            b, bank, w = banks.claim()
            Q.wait("pe", w, waits, t_in)
            n = len(parts)
            for j, src in enumerate(parts):
                tt = Q.do("pe", lambda e, j=j, src=src: e.transpose(bank[:, 128 * j:128 * j + 128], src, ident))
            tv = Q.do("dve", lambda e: e.tensor_copy(dst, bank[:, 0:128 * n]), tt, free)
            banks.release(b, tv)
            return tv

        if plan is not None:
            for k in range(NRAW):
                load_unit(k)
        th = norm_high(0, "gmix", 0)
        if plan is not None:
            split_unit(0)
        for c in range(1, DC):
            th1 = norm_high(c, "gmix", 0)
            norm_low(c - 1, th)
            th = th1
            if plan is not None and c == 4:
                split_unit(1)
        norm_low(7, th)
        ph = ExitStack()
        YH = sb("YH", [128, DC, T], R, ph)
        YL = sb("YL", [128, DC, T], R, ph)
        XB = [sb(f"XB{i}", [128, T + 4], F, ph) for i in range(2)]
        XC = [sb(f"XC{i}", [128, T], F, ph) for i in range(4)]
        XCH = [sb(f"XCH{i}", [128, T], R, ph) for i in range(4)]
        XCL = [sb(f"XCL{i}", [128, T], R, ph) for i in range(4)]
        GG = [sb(f"GG{i}", [128, T], F, ph) for i in range(2)]
        RI = [sb(f"RI{i}", [128, 2, T], F, ph) for i in range(2)]
        TA = [sb(f"TA{i}", [128, 3, T], F, ph) for i in range(2)]
        tz = [Q.do("pool", lambda e, i=i: e.memset(XB[i][:, 0:4], 0.0)) for i in range(2)]
        xb_r, xc_r, xch_r, gg_r, ri_r, ta_r = ([[] for _ in range(4)] for _ in range(6))
        xc_t, xcs_t = [None] * 4, [None] * 4
        yt = [None] * DC

        def conv_part(n, ps):
            for p in ps:
                c, s = 2 * n + p, 2 * (n % 2) + p
                b, out, tok = lin([("win", (8 + c,), 8)], hrhs)
                if n == 0 and p == 0:
                    norm_rest()
                tb = scaled(XB[p][:, 4:T + 4], b, out, tok, free=[tz[p], xb_r[p]])
                t = Q.do("dve", lambda e, p=p, c=c, s=s: e.tensor_scalar(
                    XC[s][:, :], XB[p][:, 4:T + 4], vec("cw", 24 + c), vec("cb", c), ALU.mult, ALU.add), tb, xc_r[s])
                for j in (2, 1, 0):
                    t = Q.do("dve", lambda e, p=p, c=c, s=s, j=j: e.scalar_tensor_tensor(
                        out=XC[s][:, :], in0=XB[p][:, 1 + j:T + 1 + j], scalar=vec("cw", 8 * j + c), in1=XC[s][:, :],
                        op0=ALU.mult, op1=ALU.add), t)
                xb_r[p] = [t]
                xc_t[s] = t
                xcs_t[s] = halves(XCH[s][:, :], XCL[s][:, :], XC[s][:, :], t, free=[xch_r[s]])

        def gates_part(n):
            j, wh, wl, th, tl = use("wri", (n,), 8)
            rib = []
            for p in range(2):
                for w in range(2):
                    b, bank, wt = banks.claim()
                    for k in range(2):
                        m = (w * 2 + p) * 2 + k
                        s = 2 * (n % 2) + k
                        tok = mm3(bank, wh[:, m * 128:m * 128 + 128], wl[:, m * 128:m * 128 + 128],
                                  XCH[s][:, :], XCL[s][:, :], k == 0, k == 1, [wt, th, tl, xcs_t[s]])
                    rib.append((b, bank, tok))
            spls.release(j, tok)
            for k in range(2):
                xch_r[2 * (n % 2) + k] = [tok]
            ts = []
            for p in range(2):
                for w in range(2):
                    b, bank, tok = rib[2 * p + w]
                    t = Q.do("act", lambda e, p=p, w=w, bank=bank: e.activation(
                        RI[p][:, w, :], bank, ACT.Sigmoid, bias=vec(("br", "bi")[w], 2 * n + p)), tok, ri_r[p])
                    banks.release(b, t)
                    ts.append(t)
            ats = []
            for p in range(2):
                c, s = 2 * n + p, 2 * (n % 2) + p
                a, tt, u = TA[p][:, 0, :], TA[p][:, 1, :], TA[p][:, 2, :]
                t_a = Q.do("act", lambda e, p=p, c=c, a=a: e.activation(a, RI[p][:, 0, :], ACT.Exp, scale=LC[:, c:c + 1]),
                           ts[2 * p], t_lc, ta_r[p])
                t_t = Q.do("act", lambda e, p=p, c=c, tt=tt: e.activation(tt, RI[p][:, 0, :], ACT.Tanh,
                                                                          scale=LC[:, 8 + c:9 + c]), ts[2 * p], t_lc, ta_r[p])
                t_q = Q.do("act", lambda e, a=a, u=u: e.activation(u, a, ACT.Square), t_a, ta_r[p])
                t_ix = Q.do("pool", lambda e, p=p, s=s: e.tensor_tensor(RI[p][:, 1, :], RI[p][:, 1, :], XC[s][:, :], ALU.mult),
                            ts[2 * p + 1], xc_t[s])
                xc_r[s] = [t_ix]
                ats.append((t_q, t_ix, t_a, t_t))
            return ats

        def scan_a(n, ats):
            gt_ = []
            for p in range(2):
                b, out, tok = lin([("win", (2 * n + p,), 8)], hrhs)
                tg = scaled(GG[p][:, :], b, out, tok, free=[gg_r[p]])
                if p == 0:
                    for p2 in range(2):
                        tt, u = TA[p2][:, 1, :], TA[p2][:, 2, :]
                        t_q, t_ix, t_a, t_t = ats[p2]
                        t1 = Q.do("dve", lambda e, u=u, tt=tt: e.scalar_tensor_tensor(
                            out=u, in0=u, scalar=1.0, in1=tt, op0=ALU.add, op1=ALU.mult), t_q, t_t)
                        t1 = Q.do("dve", lambda e, u=u: e.tensor_scalar(u, u, 0.0, None, ALU.max), t1)
                        t1 = Q.do("act", lambda e, u=u: e.activation(u, u, ACT.Sqrt), t1)
                        ats[p2] = (t1, t_ix, t_a, t_t)
                gt_.append(tg)
            for p in range(2):
                gt_[p] = Q.do("act", lambda e, p=p: e.activation(GG[p][:, :], GG[p][:, :], ACT.Gelu_apprx_tanh), gt_[p])
            return ats, gt_

        def scan_b(n, ats, gt_):
            for p in range(2):
                u = TA[p][:, 2, :]
                t1, t_ix, t_a, t_t = ats[p]
                t1 = Q.do("pool", lambda e, p=p, u=u: e.tensor_tensor(u, u, RI[p][:, 1, :], ALU.mult), t1, t_ix)
                ri_r[p] = [t1, t_t, t_a]
                ats[p] = t1
            for p in range(2):
                a, tt, u = TA[p][:, 0, :], TA[p][:, 1, :], TA[p][:, 2, :]
                t1 = Q.do("dve", lambda e, a=a, u=u, tt=tt: e.tensor_tensor_scan(tt, a, u, 0.0, ALU.mult, ALU.add),
                          ats[p], ri_r[p])
                t1 = Q.do("dve", lambda e, p=p, tt=tt: e.tensor_tensor(tt, tt, GG[p][:, :], ALU.mult), t1, gt_[p])
                gg_r[p] = [t1]
                yt[2 * n + p] = halves(YH[:, 2 * n + p, :], YL[:, 2 * n + p, :], tt, t1)
                ta_r[p] = yt[2 * n + p]

        conv_part(0, (0, 1))
        lam = V[:, VEC["lam"]:VEC["lam"] + 8]
        t = Q.do("act", lambda e: e.activation(LC[:, 8:16], lam, ACT.Abs), t_v)
        t = Q.do("act", lambda e: e.activation(LC[:, 8:16], LC[:, 8:16], ACT.Exp, scale=-1.0), t)
        t = Q.do("act", lambda e: e.activation(LC[:, 8:16], LC[:, 8:16], ACT.Ln, bias=1.0), t)
        t2 = Q.do("dve", lambda e: e.tensor_scalar(LC[:, 0:8], lam, 0.0, 8.0, ALU.min, ALU.mult), t_v)
        t2 = Q.do("dve", lambda e: e.scalar_tensor_tensor(out=LC[:, 0:8], in0=LC[:, 8:16], scalar=-8.0,
                                                          in1=LC[:, 0:8], op0=ALU.mult, op1=ALU.add), t, t2)
        t_lc = Q.do("dve", lambda e: e.tensor_scalar(LC[:, 8:16], LC[:, 0:8], -1.0, None, ALU.mult), t2)
        for n in range(4):
            if n < 3:
                conv_part(n + 1, (0,))
            if n > 0:
                scan_b(n - 1, *pend)
            if n < 3:
                conv_part(n + 1, (1,))
            pend = scan_a(n, gates_part(n))
        scan_b(3, *pend)
        for c in range(DC):
            hr[c] = [("pe", Q.sems["pe"], Q.n["pe"])]

        hi_on[0] = "act"

        def out_proj(name, g, gi):
            for c in range(DC):
                b, out, tok = lin([(name, (c,), 8)], lambda k: (YH[:, k, :], YL[:, k, :], yt[k]))
                add_x(c, b, out, tok)
                norm_start(c, g, gi)

        out_proj("wout", "gffn", 0)
        ph.close()

        def ffn(l, g, gi):
            ph = ExitStack()
            start = Q.now()
            MH = sb(f"MH{l}", [128, FH, T], R, ph)
            ML = sb(f"ML{l}", [128, FH, T], R, ph)
            G1 = sb(f"G1{l}", [128, 2, T], F, ph)
            S1 = sb(f"S1{l}", [128, 2, T], F, ph)
            U1 = sb(f"U1{l}", [128, 2, T], F, ph)
            g_r, s_r, u_r = ([list(start), list(start)] for _ in range(3))
            m_r = list(start)
            for half in range(2):
                mt = [None] * FH
                for f in range(FH):
                    i = half * FH + f
                    z = f % 2
                    b, out, tok = lin([("wg", (l, i), 8)], hrhs)
                    if i == 0:
                        norm_rest()
                    b2, out2, tok2 = lin([("wu", (l, i), 8)], hrhs)
                    tg = scaled(G1[:, z, :], b, out, tok, free=[g_r[z]])
                    ts = Q.do("act", lambda e, z=z: e.activation(S1[:, z, :], G1[:, z, :], ACT.Silu), tg, s_r[z])
                    g_r[z] = [ts]
                    tu = scaled(U1[:, z, :], b2, out2, tok2, free=[u_r[z]])
                    tm = Q.do("dve", lambda e, z=z: e.tensor_tensor(U1[:, z, :], U1[:, z, :], S1[:, z, :], ALU.mult), tu, ts)
                    s_r[z] = [tm]
                    mt[f] = halves(MH[:, f, :], ML[:, f, :], U1[:, z, :], tm, free=[m_r])
                    u_r[z] = mt[f]
                if half == 1:
                    for c in range(DC):
                        hr[c] = [("pe", Q.sems["pe"], Q.n["pe"])]
                for c in range(DC):
                    b, out, tok = lin([("wd", (l, half, c, slice(None), slice(0, 6)), 6),
                                       ("wd", (l, half, c, slice(None), slice(6, 11)), 5)],
                                      lambda k: (MH[:, k, :], ML[:, k, :], mt[k]))
                    add_x(c, b, out, tok)
                    if half == 1:
                        norm_start(c, g, gi)
                m_r = [tok]
            ph.close()

        ffn(0, "gmix", 8)

        def sb_mixer():
            ph = ExitStack()
            start = Q.now()
            YH = sb("OH", [128, DC, T], R, ph)
            YL = sb("OL", [128, DC, T], R, ph)
            QK = [sb(f"QK{i}", [128, 3, T], F, ph) for i in range(2)]
            VN = [sb(f"VN{i}", [128, T], F, ph) for i in range(2)]
            AL = sb("AL", [128, 1280], F, ph)
            PP = sb("PP", [128, 1280], F, ph)
            PH = sb("PH", [128, 1280], R, ph)
            PL = sb("PL", [128, 1280], R, ph)
            W = sb("W", [128, 1280], F, ph)
            TR = sb("TR", [128, 256], R, ph)
            IB = sb("IB", [128, 256], B16, ph)
            tc = [Q.do("dve", lambda e: e.tensor_scalar(TR[:, 0:128], cst("tri"), -1.0, None, ALU.mult), start),
                  Q.do("dve", lambda e: e.tensor_scalar(TR[:, 128:256], ones, -1.0, None, ALU.mult), start),
                  Q.do("dve", lambda e: e.tensor_copy(IB[:, 0:128], ident), start),
                  Q.do("dve", lambda e: e.tensor_copy(IB[:, 128:256], cst("nmask")), start)]
            off = [0, 512, 1024, 896]
            wid = [512, 384, 256, 128]
            al_r, pp_r, ph_r, w_r = (list(start) for _ in range(4))
            qk_r, vn_r = [list(start), list(start)], [list(start), list(start)]
            grp = Ring([PS[:, 0:3, :].rearrange("p a b -> p (a b)"), PS[:, 3:6, :].rearrange("p a b -> p (a b)")],
                       start)
            banks.only(6, 7)

            def scores(h):
                c, p = h // 2, 64 * (h % 2)
                z = c % 2
                gj, S, w = grp.claim()
                for j in (0, 1, 3, 2):
                    o, n = off[j], wid[j]
                    Q.wait("pe", w, tc, qk_t[z])
                    Q.raw("pe", lambda e, o=o, n=n, j=j: e.matmul(
                        S[:, o:o + n], QK[z][p:p + 64, 1, 128 * j:128 * j + 128], QK[z][p:p + 64, 0, 128 * j:512],
                        start=(j != 3), stop=False, skip_group_check=True))
                    ml = Q.do("pe", lambda e, o=o: e.matmul(S[:, o:o + 128], IB[:, 0:128], IB[:, 128:256],
                                                           start=False, stop=False, skip_group_check=True))
                return gj, S, ml

            def softplus_exp(S, ml):
                t = Q.do("act", lambda e: e.activation(AL[:, :], S[:, 0:1280], ACT.Abs), ml, al_r)
                return Q.do("act", lambda e: e.activation(AL[:, :], AL[:, :], ACT.Exp, scale=-1.0), t)

            def softplus_log(S, ml, t):
                nonlocal al_r, pp_r
                t = Q.do("act", lambda e: e.activation(AL[:, :], AL[:, :], ACT.Ln, bias=1.0), t)
                t = Q.do("dve", lambda e: e.scalar_tensor_tensor(out=PP[:, :], in0=S[:, 0:1280], scalar=0.0,
                                                                 in1=AL[:, :], op0=ALU.max, op1=ALU.add), t, ml, pp_r)
                al_r = [t]
                return t

            def softplus_b(t):
                nonlocal pp_r
                t1 = Q.do("dve", lambda e: e.tensor_copy(PH[:, :], PP[:, :]), t, ph_r)
                t2 = Q.do("dve", lambda e: e.tensor_tensor(PL[:, :], PP[:, :], PH[:, :].bitcast(F), ALU.subtract),
                          t1, ph_r)
                pp_r = [t2]
                return [t1, t2]

            def weights(S, tp):
                nonlocal ph_r
                Q.wait("pe", tp)
                todo = [(j, jj, P) for j in (0, 1, 3, 2) for jj in range(j, 4) for P in (PH, PL)]
                for i, (j, jj, P) in enumerate(todo):
                    lhs = TR[:, 0:128] if jj == j else TR[:, 128:256]
                    o = off[j] + 128 * (jj - j)
                    f = lambda e, o=o, jj=jj, P=P, lhs=lhs: e.matmul(
                        S[:, o:o + wid[jj]], lhs, P[:, off[jj]:off[jj] + wid[jj]], start=False,
                        stop=(jj == 3 and P is PL), skip_group_check=True)
                    if i < len(todo) - 1:
                        Q.raw("pe", f)
                    else:
                        ms = Q.do("pe", f)
                ph_r = [ms]
                return Q.do("act", lambda e: e.activation(W[:, :], S[:, 0:1280], ACT.Exp), ms, w_r)

            def values(h, S, te):
                nonlocal w_r
                p, z = 64 * (h % 2), (h // 2) % 2
                Q.wait("pe", te, vn_t[z])
                for j in range(4):
                    f = lambda e, j=j: e.matmul(S[p:p + 64, 128 * j:512], VN[z][:, 128 * j + p:128 * j + p + 64],
                                                W[:, off[j]:off[j] + wid[j]], start=(j == 0), stop=(j == 3),
                                                skip_group_check=True)
                    if j < 3:
                        Q.raw("pe", f)
                    else:
                        mo = Q.do("pe", f)
                w_r = [mo]
                return mo

            qk_t, vn_t = [None, None], [None, None]
            yts = [[] for _ in range(DC)]

            def project(c):
                z = c % 2
                ts = []

                def done(i):
                    def f(b, out, tok):
                        if c == 0 and i == 0:
                            norm_rest()
                        ts.append(scaled(QK[z][:, i, :], b, out, tok, mul=0.125 if i == 0 else 1.0, free=[qk_r[z]]))
                        if i == 1:
                            qk_t[z] = list(ts)
                    return f

                for i in range(3):
                    yield from lin_steps([("wqkv", (8 * i + c,), 8)], hrhs, done(i))
                vn_t[z] = natural(VN[z][:, :], [QK[z][:, 2, 128 * j:128 * j + 128] for j in range(4)], ts, vn_r[z])

            finish(project(0))
            gen = None
            g, S, m = scores(0)
            tp = softplus_b(softplus_log(S, m, softplus_exp(S, m)))
            for h in range(2 * DC):
                c, p, z = h // 2, 64 * (h % 2), (h // 2) % 2
                if p == 0:
                    gen = project(c + 1) if c + 1 < DC else None
                step(gen, 1 if p else 2)
                if h + 1 < 2 * DC:
                    g1, S1, m1 = scores(h + 1)
                    if p == 0:
                        qk_r[z] = [m1, vn_t[z]]
                    ta = softplus_exp(S1, m1)
                te = weights(S, tp)
                step(gen, 1)
                if h + 1 < 2 * DC:
                    tp = softplus_b(softplus_log(S1, m1, ta))
                mo = values(h, S, te)
                step(gen, 1)
                if p:
                    vn_r[z] = [mo]
                t = halves(YH[p:p + 64, c, :], YL[p:p + 64, c, :], S[p:p + 64, 0:512], mo, free=[start])
                yts[c] += t
                grp.release(g, *t)
                if h + 1 < 2 * DC:
                    g, S = g1, S1
            for c in range(DC):
                hr[c] = [("pe", Q.sems["pe"], Q.n["pe"])]
            banks.only(*range(8))
            for c in range(DC):
                b, out, tok = lin([("wbo", (c,), 8)], lambda k: (YH[:, k, :], YL[:, k, :], yts[k]))
                add_x(c, b, out, tok)
                norm_start(c, "gffn", 8)
            ph.close()

        sb_mixer()
        def softmax(S, P, n, scale, k, ready, free, in_max=None, s_free=None):
            m, nm, su, ri = (SM[:, 4 * k + i:4 * k + i + 1] for i in range(4))
            if in_max is None:
                t = Q.do("dve", lambda e: e.tensor_reduce(m, S, AX.X, ALU.max), ready, sm_r[k])
            else:
                t = in_max
            t = Q.do("dve", lambda e: e.tensor_scalar(nm, m, -scale, None, ALU.mult), t, sm_r[k])
            t = te = Q.do("act", lambda e: e.activation(P, S, ACT.Exp, bias=nm, scale=scale, accum_out=su), t, free)
            t = Q.do("dve", lambda e: e.reciprocal(ri, su), t)
            t = Q.do("dve", lambda e: e.tensor_scalar(P, P, ri, None, ALU.mult), t)
            sm_r[k] = [t]
            return te, t

        def turned(dst, P, n, waits, free):
            b, bank, w = banks.claim()
            Q.wait("pe", w, waits)
            for j in range(n):
                f = lambda e, j=j: e.transpose(bank[:, 128 * j:128 * j + 128], P[:, 128 * j:128 * j + 128], ident)
                if j < n - 1:
                    Q.raw("pe", f)
                else:
                    tt = Q.do("pe", f)
            src = bank[:, 0:128 * n].rearrange("p (j q) -> p j q", j=n)
            tv = Q.do("act", lambda e: e.activation(dst, src, ACT.Copy), tt, free)
            banks.release(b, tv)
            return tt, tv

        def staged(groups, work, counts):
            units = [(g, u) for g in groups for u in range(g["n"])]
            made = {}
            then = None
            for i in range(len(units) + 2):
                if i < len(units):
                    g, u = units[i]
                    while u == 0 and not g["there"]():
                        step(work)
                    made[i] = g["score"](u, i % 3)
                step(work, counts[i % len(counts)])
                if then:
                    then()
                then = None
                if i >= 2:
                    g, u = units[i - 2]
                    then = g["turn"](u, (i - 2) % 3, made[i - 2])
            finish(work)
            if then:
                then()

        sm_r = [[] for _ in range(4)]

        def mixer2():
            ph = ExitStack()
            start = Q.now()
            ACC = sb("ACC", [128, DC, T], F, ph)
            YP = [sb(f"YP{i}", [128, 2, 4, T], R, ph) for i in range(2)]
            HB = sb("HB", [128, 24], F, ph)
            pa = ExitStack()
            AT = sb("AT", [128, 4, T], F, pa)
            y3 = [None] * 12
            acc_t = [None] * DC
            yb_r = []
            thb = Q.do("dve", lambda e: e.tensor_scalar(HB[:, :], V[:, VEC["bg"]:VEC["bg"] + 24], 0.5, None, ALU.mult),
                       start)

            gates = {}

            def gate(g, d):
                G = ACC[:, d, :] if g == 2 else GX[:, d % 2, :]

                def done(b, out, tok):
                    t = scaled(G, b, out, tok, free=[start if g == 2 else gx_r[d % 2]])
                    gates[g, d] = G, Q.do("act", lambda e: e.activation(
                        G, G, ACT.Tanh, bias=HB[:, 8 * g + d:8 * g + d + 1], scale=0.5), t, thb)

                yield from lin_steps([("w2", (22 + 8 * g + d,), 8)], hrhs, done)

            def branch(g, d):
                def product(b, out, tok):
                    G, tg = gates[g, d]
                    t = Q.do("dve", lambda e: e.scalar_tensor_tensor(
                        out=G, in0=G, scalar=1.0, in1=out, op0=ALU.add, op1=ALU.mult), tg, tok)
                    banks.release(b, t)
                    if g != 2:
                        t = Q.do("dve" if g == 0 else "pool", lambda e: e.tensor_tensor(
                            ACC[:, d, :], ACC[:, d, :], G, ALU.add), t, acc_t[d])
                        gx_r[d % 2] = [t]
                    acc_t[d] = [t]
                    if d == DC - 1:
                        yb_r[:] = [tok]

                if (g, d) not in gates:
                    yield from gate(g, d)
                Y = YP[g % 2]
                yield from lin_steps([("wbr", (g, d), 4)], lambda k: (Y[:, 0, k, :], Y[:, 1, k, :], y3[4 * g + k]),
                                     product)

            def branches(g):
                for d in range(DC):
                    yield from branch(g, d)
            banks.only(0, 1, 2, 3, 4, 5)
            obanks = Ring([PS[:, 6, :], PS[:, 7, :]], start)

            pm = ExitStack()
            MKV = sb("MKV", [128, 4, 2, 256], F, pm)
            QM = sb("QM", [128, 2, T], F, pm)
            pk = ExitStack()
            MF = AT[:, :, :].rearrange("p a (b n) -> p (a b) n", n=256)
            MMH = YP[1][:, 0, :, :].rearrange("p a (b n) -> p (a b) n", n=256)
            MML = YP[1][:, 1, :, :].rearrange("p a (b n) -> p (a b) n", n=256)
            t_mem = Q.dma("pool", MF, I["mem"], d_misc[0], start)
            tg = Q.do("dve", lambda e: e.tensor_scalar(LC[:, 0:8], V[:, VEC["gfin"]:VEC["gfin"] + 8], ALPHA, None,
                                                       ALU.mult), start)
            qm_r, qm_t = [list(start), list(start)], [None, None]

            def mem_query(h):
                def done(b, out, tok):
                    if h == 0:
                        norm_rest()
                        for c in range(DC):
                            t = Q.do("dve", lambda e, c=c: e.scalar_tensor_tensor(
                                out=X[:, c, :], in0=X[:, c, :], scalar=LC[:, c:c + 1], in1=RS[:, :], op0=ALU.mult,
                                op1=ALU.mult), tg, rs_t[0], xt[c], xr[c])
                            xt[c], xr[c] = [t], []
                        rs_r[0] = [t]
                    started[0] = h
                    qm_t[h % 2] = scaled(QM[:, h % 2, :], b, out, tok, free=[qm_r[h % 2]])

                yield from lin_steps([("w2", (18 + h,), 8)], hrhs, done)

            started = [-1]
            finish(mem_query(0))
            mm_t = [halves(MMH[:, c, :], MML[:, c, :], MF[:, c, :], t_mem, free=[start]) for c in range(DC)]
            finish(mem_query(1))
            VT = sb("VT", [128, 2, 256], F, pk)
            vt_r = [list(start), list(start)]
            kv_t = [[] for _ in range(4)]
            late = None
            for h in range(4):
                b, out, tok = lin([("wmkv", (h,), 8)], lambda k: (MMH[:, k, :], MML[:, k, :], mm_t[k]), n=256)
                t = Q.do("dve", lambda e, out=out, h=h: e.tensor_copy(MKV[:, h, 0, :], out), tok, start)
                banks.release(b, t)
                kv_t[h].append(t)
                if late:
                    late()
                b, out, tok = lin([("wmkv", (4 + h,), 8)], lambda k: (MMH[:, k, :], MML[:, k, :], mm_t[k]), n=256)
                t = Q.do("dve", lambda e, out=out, h=h: e.tensor_copy(VT[:, h % 2, :], out), tok, vt_r[h % 2])
                banks.release(b, t)

                def late(h=h, t=t):
                    t = natural(MKV[:, h, 1, :], [VT[:, h % 2, 0:128], VT[:, h % 2, 128:256]], t, start)
                    vt_r[h % 2] = [t]
                    kv_t[h].append(t)
            late()
            pk.close()
            start = Q.now()
            PM = [sb(f"PM{i}", [128, 256], F, pm) for i in range(3)]
            PT = [sb(f"PT{i}", [128, 2, T], F, pm) for i in range(2)]
            pm_r, pt_r, pt_t = [list(start) for _ in range(3)], [list(start), list(start)], [[], []]

            def mem_head(h):
                z = h % 2

                def score(u, k):
                    b, bank, w = banks.claim()
                    tok = Q.do("pe", lambda e: e.matmul(bank[:, 0:256], QM[:, z, 128 * u:128 * u + 128],
                                                        MKV[:, h, 0, :], start=True, stop=True), w, qm_t[z], kv_t[h])
                    te, t = softmax(bank[:, 0:256], PM[k][:, :], 256, 1.0 / math.sqrt(128.0), k, tok,
                                    pm_r[k])
                    banks.release(b, te)
                    if u == 3:
                        qm_r[z] = [tok]
                    return t

                def turn(u, k, t):
                    tt, tv = turned(PT[z][:, :, 128 * u:128 * u + 128], PM[k], 2, t, pt_r[z])
                    pm_r[k] = [tt]
                    pt_t[z].append(tv)

                    def values():
                        oj, bank, w = obanks.claim()
                        Q.wait("pe", w, pt_t[z])
                        for j in range(2):
                            tok = Q.do("pe", lambda e, j=j: e.matmul(bank, MKV[:, h, 1, 128 * j:128 * j + 128],
                                                                     PT[z][:, j, :], start=(j == 0), stop=(j == 1)))
                        pt_r[z], pt_t[z] = [tok], []
                        y3[8 + h] = halves(YP[0][:, 0, h, :], YP[0][:, 1, h, :], bank, tok, free=[start])
                        obanks.release(oj, *y3[8 + h])

                    return values if u == 3 else None

                return {"n": 4, "there": lambda: started[0] >= h, "score": score, "turn": turn}

            heads = [mem_head(h) for h in range(4)]

            KG, VG = AT[:, 0, :], AT[:, 1, :]
            ZG = [AT[:, 2, :], AT[:, 3, :]]
            z_r = [list(start), list(start)]
            st_r = []
            gq = {}

            def rope(key, Z, tile, gain, free):
                st = {}

                def done(b, out, tok):
                    st["z"] = scaled(Z, b, out, tok, free=[free])
                    st["s"] = Q.do("act", lambda e: e.activation(SQ[:, 0, :], Z, ACT.Square), st["z"], sq_r[0])

                yield from lin_steps([("w2", (tile,), 8)], hrhs, done)
                b, bank, w = banks.claim()
                t = Q.do("pe", lambda e, bank=bank: e.matmul(bank, bones, SQ[:, 0, :], start=True, stop=True), st["s"], w)
                sq_r[0] = [t]
                t = Q.do("act", lambda e, bank=bank: e.activation(ST[:, :], bank, ACT.Sqrt, bias=vec("eps", 0),
                                                                  scale=1.0 / 64), t, st_r, rs_t[0])
                banks.release(b, t)
                t = Q.do("dve", lambda e: e.reciprocal(ST[:, :], ST[:, :]), t)
                t = Q.do("dve", lambda e: e.scalar_tensor_tensor(out=Z, in0=Z, scalar=gain, in1=ST[:, :],
                                                                 op0=ALU.mult, op1=ALU.mult), t, st["z"])
                st_r[:] = [t]
                yield
                yield
                b, bank, w = banks.claim()
                t2 = Q.do("pe", lambda e, bank=bank: e.matmul(bank, cst("swap"), Z, start=True, stop=True), t, w)
                t3 = Q.do("dve", lambda e, bank=bank: e.tensor_tensor(SQ[:, 1, :], bank, cst("sin", 0, 512), ALU.mult),
                          t2, sq_r[1])
                banks.release(b, t3)
                t4 = Q.do("dve", lambda e: e.tensor_tensor(Z, Z, cst("cos", 0, 512), ALU.mult), t, t2)
                t5 = Q.do("dve", lambda e: e.tensor_tensor(Z, Z, SQ[:, 1, :], ALU.add), t3, t4)
                sq_r[1] = [t5]
                gq[key] = t5
                yield

            def values_gq():
                def done(b, out, tok):
                    gq["vt"] = scaled(ZG[1], b, out, tok, free=[z_r[1]])

                yield from lin_steps([("w2", (17,), 8)], hrhs, done)
                gq["v"] = natural(VG, [ZG[1][:, 128 * j:128 * j + 128] for j in range(4)], gq["vt"], start)
                z_r[1] = [gq["v"]]

            def mem_work():
                kg = rope("k", KG, 16, vec("kg"), start)
                vg = values_gq()
                step(kg, 1)
                yield
                step(kg, 1)
                yield
                step(kg, 1)
                step(vg, 1)
                yield
                step(vg, 1)
                yield
                yield from mem_query(2)
                q0 = rope("q0", ZG[0], 12, vec("qg"), z_r[0])
                finish(kg)
                finish(vg)
                step(q0, 1)
                yield
                step(q0, 1)
                yield
                yield from mem_query(3)
                for i in range(NGATE):
                    step(q0, 1)
                    yield from gate(2, i)
                finish(q0)

            staged(heads, mem_work(), [1])
            pm.close()

            pg = ExitStack()
            start = Q.now()
            PG = [sb(f"PG{i}", [128, T], F, pg) for i in range(3)]
            GT2 = [sb(f"GT2{i}", [128, 4, T], F, pg) for i in range(2)]
            pg_r, gt_r, gt_t = [list(start) for _ in range(3)], [list(start), list(start)], [[], []]
            yp1_r = list(start)

            def gqa_pair(c):
                z = c % 2
                st = {}

                def score(u, k):
                    p, qc = 64 * (u // 4), u % 4
                    b, bank, w = banks.claim()
                    tok = Q.do("pe", lambda e: e.matmul(bank, ZG[z][p:p + 64, 128 * qc:128 * qc + 128], KG[p:p + 64, :],
                                                        start=True, stop=True), w, gq[f"q{c}"], gq["k"])
                    te, t = softmax(bank, PG[k][:, :], T, 0.125, k, tok, pg_r[k])
                    banks.release(b, te)
                    if u == 7:
                        z_r[z] = [tok]
                    return t

                def turn(u, k, t):
                    p, qc, y = 64 * (u // 4), u % 4, u // 4
                    tt, tv = turned(GT2[y][:, :, 128 * qc:128 * qc + 128], PG[k], 4, t, gt_r[y])
                    pg_r[k] = [tt]
                    gt_t[y].append(tv)

                    def values():
                        if y == 0:
                            st["o"] = obanks.claim()
                        oj, bank, w = st["o"]
                        Q.wait("pe", w if y == 0 else [], gt_t[y], gq["v"])
                        for j in range(4):
                            tok = Q.do("pe", lambda e, j=j: e.matmul(
                                bank[p:p + 64, :], VG[:, 128 * j + p:128 * j + p + 64], GT2[y][:, j, :],
                                start=(j == 0), stop=(j == 3)))
                        gt_r[y], gt_t[y] = [tok], []
                        if y == 1:
                            y3[4 + c] = halves(YP[1][:, 0, c, :], YP[1][:, 1, c, :], bank, tok, free=[yp1_r])
                            obanks.release(oj, *y3[4 + c])

                    return values if qc == 3 else None

                return {"n": 8, "there": lambda: f"q{c}" in gq, "score": score, "turn": turn}

            def gqa_work():
                br = branches(2)
                for c in range(1, 4):
                    q = rope(f"q{c}", ZG[c % 2], 12 + c, vec("qg"), z_r[c % 2])
                    step(q, 1)
                    yield
                    step(q, 1)
                    yield
                    step(br, 1)
                    yield
                    step(q, 1)
                    step(br, 1)
                    yield
                    step(br, 1)
                    yield
                    step(q, 3)
                    step(br, 1)
                    yield
                    step(br, 1)
                    yield
                    step(br, 1)
                    yield
                yield from br

            staged([gqa_pair(c) for c in range(4)], gqa_work(), [1])
            pg.close()

            pn = ExitStack()
            start = Q.now()
            NQ = [AT[:, 2 * i:2 * i + 2, :] for i in range(2)]
            yp0_r = list(yb_r) + start
            NB = sb("NB", [128, 4, 256], F, pn)
            NV = [sb(f"NV{i}", [128, 1024], F, pn) for i in range(2)]
            BI = [sb(f"BI{i}", [128, 2, 384], F, pn) for i in range(2)]
            SN = [sb(f"SN{i}", [128, 256], F, pn) for i in range(3)]
            PN = [sb(f"PN{i}", [128, 256], F, pn) for i in range(3)]
            NT = [sb(f"NT{i}", [128, 2, 128], F, pn) for i in range(2)]
            nq_r, bi_r, sn_r, pn_r, nt_r = ([list(start) for _ in range(3)] for _ in range(5))
            nv_r, nb_r = [list(start), list(start)], [list(start)]
            band = (0, 8, 24, 32)

            def na_pair(c):
                z = c % 2
                st = {"t": None}

                def bias():
                    for p in range(2):
                        for r in range(8):
                            src = bass.AP(I["rpb"].tensor, (2 * c + p) * 465 + 31 * r, [[1, 16], [31, 8], [1, 48]])
                            dst = BI[z][16 * r:16 * r + 16, p, :].rearrange("i (a w) -> i a w", a=8)
                            st["b"] = Q.dma("pool", dst, src, d_misc[2 + z], bi_r[z])

                def queries(b, out, tok):
                    by = lambda a: a.rearrange("p (r c i) -> p r c i", r=8, c=4)
                    dst = NQ[z][:, 0, :].rearrange("p (c r i) -> p r c i", c=4, r=8)
                    tq = Q.do("dve", lambda e: e.tensor_tensor(dst, by(out), by(RS[:, :]), ALU.mult), tok, rs_t[0],
                              nq_r[z])
                    banks.release(b, tq)
                    st["t"] = [tq]

                def keys(b, out, tok):
                    st["t"].append(scaled(NQ[z][:, 1, :], b, out, tok, mul=0.125, free=[nq_r[z]]))

                def vals(b, out, tok):
                    for cb in range(4):
                        bd = lambda a, cb=cb: a.rearrange("p (r w) -> p r w", r=8)[:, :, band[cb]:band[cb] + 32]
                        t = Q.do("dve", lambda e, cb=cb, bd=bd: e.tensor_tensor(
                            NB[:, cb, :].rearrange("p (r w) -> p r w", r=8), bd(out), bd(RS[:, :]), ALU.mult),
                            tok, rs_t[0], nb_r[0])
                    banks.release(b, t)
                    rs_r[0] = [t]
                    st["nb"] = t

                def project():
                    bias()
                    yield from lin_steps([("w2", (c,), 8)], hrhs, queries)
                    yield from lin_steps([("w2", (4 + c,), 8)], hrhs, keys)
                    yield from lin_steps([("w2", (8 + c,), 8)], hrhs, vals)
                    parts = [NB[:, cb, 128 * hf:128 * hf + 128] for cb in range(4) for hf in range(2)]
                    t1 = natural(NV[z][:, 0:512], parts[0:4], st["nb"], nv_r[z])
                    t2 = natural(NV[z][:, 512:1024], parts[4:8], st["nb"], nv_r[z])
                    nb_r[0] = [t1, t2]
                    st["v"] = [t1, t2]

                def score(u, k):
                    y, cb = u // 4, u % 4
                    p = 64 * y
                    bs, o = band[cb], band[cb] - 16 * cb + 16
                    q = NQ[z][p:p + 64, 0, 128 * cb:128 * cb + 128]
                    kv = NQ[z][p:p + 64, 1, :].rearrange("p (r w) -> p r w", r=8)[:, :, bs:bs + 32]
                    bi = BI[z][:, y, :].rearrange("p (a w) -> p a w", a=8)[:, :, o:o + 32]
                    b, bank, w = banks.claim()
                    Q.raw("pe", lambda e: e.matmul(bank[:, 0:256], q, kv, start=True, stop=False), w, st["t"])
                    tok = Q.do("pe", lambda e: e.matmul(bank[:, 0:256], anti, bi, start=False, stop=True), st["b"])
                    m = SM[:, 4 * k:4 * k + 1]
                    mask = cst("mask", 256 * (0, 1, 1, 2)[cb], 256)
                    t = Q.do("dve", lambda e: e.tensor_tensor_reduce(SN[k][:, :], bank[:, 0:256], mask, 1.0, -3e38,
                                                                     ALU.add, ALU.max, m), tok, sn_r[k], sm_r[k])
                    banks.release(b, t)
                    te, t = softmax(SN[k][:, :], PN[k][:, :], 256, 1.0, k, None, pn_r[k], in_max=t)
                    sn_r[k] = [te]
                    if u == 7:
                        nq_r[z], bi_r[z] = [tok], [tok]
                    return t

                def turn(u, k, t):
                    y, cb = u // 4, u % 4
                    p = 64 * y
                    tt, tv = turned(NT[u % 2][:, :, :], PN[k], 2, t, nt_r[u % 2])
                    pn_r[k] = [tt]

                    def values():
                        if u == 0:
                            st["o"] = obanks.claim()
                        oj, bank, w = st["o"]
                        Q.wait("pe", w if u == 0 else [], tv, st["v"])
                        for j in range(2):
                            a = (2 * cb + j) * 128 + p
                            tok = Q.do("pe", lambda e, j=j, a=a: e.matmul(
                                bank[p:p + 64, 128 * cb:128 * cb + 128], NV[z][:, a:a + 64], NT[u % 2][:, j, :],
                                start=(j == 0), stop=(j == 1), skip_group_check=True))
                        nt_r[u % 2] = [tok]
                        if u == 7:
                            nv_r[z] = [tok]
                            src = bank.rearrange("p (c r i) -> p r c i", c=4, r=8)
                            hi = YP[0][:, 0, c, :].rearrange("p (r c i) -> p r c i", r=8, c=4)
                            lo = YP[0][:, 1, c, :].rearrange("p (r c i) -> p r c i", r=8, c=4)
                            y3[c] = halves(hi, lo, src, tok, free=[yp0_r])
                            obanks.release(oj, *y3[c])

                    return values

                return {"n": 8, "there": lambda: "v" in st, "score": score, "turn": turn, "qkv": project}

            pairs = [na_pair(c) for c in range(4)]

            def na_work():
                br = branches(1)
                for c, order in ((1, "qqbbbqqqqq"), (2, "qqbbbqqqqq"), (3, "qqbbbqqqqq")):
                    q = pairs[c]["qkv"]()
                    for w in order:
                        step(q if w == "q" else br, 1)
                        yield
                yield from br

            finish(pairs[0]["qkv"]())
            staged(pairs, na_work(), [1, 2, 1])
            pn.close()
            pa.close()

            start = Q.now()
            banks.only(*range(8))
            GH = sb("GH", [128, DC, T], R, ph)
            GL = sb("GL", [128, DC, T], R, ph)
            gt = [None] * DC
            gx_r[0], gx_r[1], sq_r[0], sq_r[1] = (list(start) for _ in range(4))
            for d in range(DC):
                finish(branch(0, d))
                gt[d] = halves(GH[:, d, :], GL[:, d, :], ACC[:, d, :], acc_t[d], free=[start])
            for c in range(DC):
                b, out, tok = lin([("w2o", (c,), 8)], lambda k: (GH[:, k, :], GL[:, k, :], gt[k]))
                add_x(c, b, out, tok, 0.5)
                mean_part(c, 7)
            ph.close()

        def mean_part(c, n):
            if c == 0 or c >= n:
                return
            a = X[:, 0, :] if c == 1 else SA[:, :]
            sa_t[0] = Q.do("pool", lambda e: e.tensor_tensor(SA[:, :], a, X[:, c, :], ALU.add), xt[c],
                           sa_r[0] + xt[0] if c == 1 else sa_t[0])
            xr[c] += [sa_t[0]]
            if c == 1:
                xr[0] += [sa_t[0]]

        def layer_norm(g, bb, n, done=None):
            b, bank, w = banks.claim()
            now = Q.now()
            Q.do("act", lambda e: e.activation(LC[:, 12:13], vec("eps", 1), ACT.Sqrt), now)
            tp = Q.do("pe", lambda e, bank=bank: e.matmul(bank, ones, SA[:, :], start=True, stop=False), w, sa_t[0])
            sa_r[0] = [tp]
            for c in range(n, DC):
                tp = Q.do("pe", lambda e, bank=bank, c=c: e.matmul(bank, ones, X[:, c, :], start=False, stop=(c == 7)),
                          xt[c])
                xr[c] += [tp]
            tm = Q.do("dve", lambda e, bank=bank: e.tensor_scalar(ST[:, :], bank, 1.0 / D, None, ALU.mult), tp, now)
            banks.release(b, tm)
            b, bank, w = banks.claim()
            bufs = [SA[:, :], RS[:, :], SQ[:, 0, :], SQ[:, 1, :]]
            rd = [[tp], rs_r[0], sq_r[0], sq_r[1]]
            for c in range(DC):
                t = Q.do("dve", lambda e, c=c: e.tensor_tensor(X[:, c, :], X[:, c, :], ST[:, :], ALU.subtract), tm,
                         xt[c], xr[c])
                xt[c], xr[c] = [t], []
            for c in range(DC):
                n = (0, 2, 3, 1, 2, 3, 2, 3)[c]
                S = bufs[n]
                ts = Q.do("act", lambda e, c=c, S=S: e.activation(S, X[:, c, :], ACT.Square), xt[c], rd[n])
                xr[c] = [ts]
                if c == 0:
                    ta = ts
                elif c == 3:
                    td = ts
                elif c < 3:
                    ta = Q.do("pool", lambda e, S=S: e.tensor_tensor(SA[:, :], SA[:, :], S, ALU.add), ts, ta)
                    rd[n] = [ta]
                else:
                    td = Q.do("dve", lambda e, S=S: e.tensor_tensor(RS[:, :], RS[:, :], S, ALU.add), ts, td)
                    rd[n] = [td]
            Q.do("pe", lambda e, bank=bank: e.matmul(bank, ones, SA[:, :], start=True, stop=False), w, ta)
            tp = Q.do("pe", lambda e, bank=bank: e.matmul(bank, ones, RS[:, :], start=False, stop=True), td)
            sa_r[0], sq_r[0], sq_r[1] = [tp], [tp], [tp]
            ta = Q.do("act", lambda e, bank=bank: e.activation(ST[:, :], bank, ACT.Sqrt, bias=vec("eps", 1), scale=1.0 / D),
                      tp, t)
            banks.release(b, ta)
            tr = Q.do("dve", lambda e: e.reciprocal(RS[:, :], ST[:, :]), ta, tp)
            for c in range(DC):
                t = Q.do("dve", lambda e, c=c: e.scalar_tensor_tensor(
                    out=X[:, c, :], in0=X[:, c, :], scalar=vec(g, c), in1=RS[:, :], op0=ALU.mult, op1=ALU.mult),
                    tr, xt[c], xr[c])
                t2 = Q.do("act", lambda e, c=c: e.activation(X[:, c, :], X[:, c, :], ACT.Identity, bias=vec(bb, c)), t)
                xt[c], xr[c] = [t2], []
                if done:
                    done(c)
            rs_r[0] = [t]

        ffn(1, "gfin", 0)
        mixer2()
        dense.close()

        def experts():
            start = Q.now()
            px = ExitStack()
            SL = [sb(f"SL{i}", [128, 2048], F, px) for i in range(NSLOT - 1)]
            SL.append(C[:, CST["bones"]:CST["bones"] + 2048])
            assert CST["bones"] + 2048 <= CST["iota"]
            XNH = sb("XNH", [128, 4, D], R, px)
            XNL = sb("XNL", [128, 4, D], R, px)

            loads = []
            for i in range(8):
                for k in range(8):
                    for e2 in range(2):
                        loads.append((I["wgu"][2 * i + e2, 128 * k:128 * k + 128, :], None))
                for k in range(4):
                    for e2 in range(2):
                        loads.append((I["wdn"][2 * i + e2, 256 * k:256 * k + 256, :].rearrange("(a p) n -> p a n", p=128), 2))
            slots = [None] * len(loads)

            def load(i, *waits):
                src, two = loads[i]
                j = i % NSLOT
                dst = SL[j][:, :] if two is None else SL[j][:, :].rearrange("p (a n) -> p a n", a=2)
                slots[i] = (SL[j], Q.dma("sp", dst, src, d_slot[j], *waits))

            for i in range(NSLOT):
                load(i, start)

            pa = ExitStack()
            XF = sb("XF", [128, 4, D], F, pa)
            LT = sb("LT", [16, T], F, pa)
            WK = sb("WK", [16, T], F, pa)
            M1 = sb("M1", [16, T], F, pa)
            M2 = sb("M2", [16, T], F, pa)
            M3 = sb("M3", [16, T], F, pa)
            ON = sb("ON", [16, T], F, pa)
            T8 = sb("T8", [16, 16], F, pa)
            t_on = Q.do("pool", lambda e: e.memset(ON[:, :], 1.0), start)
            b, bank, w = banks.claim()
            rt = []

            def logit(c, bank=bank, w=w):
                rt[:] = [Q.do("pe", lambda e: e.matmul(bank[0:16, :], WRT[:, c, :], X[:, c, :], start=(c == 0),
                                                       stop=(c == 7)), w if c == 0 else [], xt[c], t_in)]

            layer_norm("l1g", "l1b", 7, done=logit)
            tok = rt[0]
            t = Q.do("dve", lambda e, bank=bank: e.tensor_copy(LT[:, :], bank[0:16, :]), tok, start)
            banks.release(b, t)
            b, bank, w = banks.claim()
            for j in range(4):
                tt = Q.do("pe", lambda e, j=j, bank=bank: e.transpose(bank[:, 16 * j:16 * j + 16],
                                                                     LT[:, 128 * j:128 * j + 128], ident[0:16, 0:16]),
                          w if j == 0 else [], t)
            lg = AF[:, :].rearrange("p (a e) -> p a e", a=4)
            m4 = SM[:, 0:4]
            bc = SM[:, 0:4].unsqueeze(2).to_broadcast([128, 4, 16])
            t0 = Q.do("dve", lambda e, bank=bank: e.tensor_copy(AF[:, :], bank[:, 0:64]), tt, start)
            banks.release(b, t0)
            t = Q.do("dve", lambda e: e.tensor_reduce(m4, lg, AX.X, ALU.max), t0)
            t = Q.do("dve", lambda e: e.tensor_tensor(lg, lg, bc, ALU.subtract), t)
            ta = Q.do("act", lambda e: e.activation(AF[:, :], AF[:, :], ACT.Exp), t)
            t = Q.do("dve", lambda e: e.tensor_reduce(m4, lg, AX.X, ALU.add), ta)
            t = Q.do("dve", lambda e: e.reciprocal(m4, m4), t)
            t_af = Q.do("dve", lambda e: e.tensor_tensor(lg, lg, bc, ALU.mult), t)
            b, bank, w = banks.claim()
            for j in range(4):
                tt = Q.do("pe", lambda e, j=j, bank=bank: e.transpose(bank[0:16, 128 * j:128 * j + 128],
                                                                     AF[:, 16 * j:16 * j + 16], ident),
                          w if j == 0 else [], t_af)
            t = Q.do("dve", lambda e, bank=bank: e.tensor_copy(WK[:, :], bank[0:16, :]), tt)
            banks.release(b, t)
            t1 = Q.do("act", lambda e: e.activation(LT[:, :], WK[:, :], ACT.Copy), t)
            for tc in range(4):
                for half in range(2):
                    b2, bk, w = banks.claim()
                    Q.wait("pe", w, t_in)
                    for j in range(4):
                        c = 4 * half + j
                        t2 = Q.do("pe", lambda e, bk=bk, j=j, c=c, tc=tc: e.transpose(
                            bk[:, 128 * j:128 * j + 128], X[:, c, 128 * tc:128 * tc + 128], ident), xt[c])
                    part = lambda a, tc=tc, half=half: a[:, tc, 512 * half:512 * half + 512]
                    t3 = Q.do("act", lambda e, bk=bk, part=part: e.activation(part(XF), bk, ACT.Copy), t2, start)
                    banks.release(b2, t3)
                    th = Q.do("act", lambda e, part=part: e.activation(part(XNH), part(XF), ACT.Copy), t3)
                    tl = Q.do("pool", lambda e, part=part: e.tensor_tensor(
                        part(XNL), part(XF), part(XNH).bitcast(F), ALU.subtract), t3, th, start)
                    xn_t = [th, tl]
            for i in range(CAP // 8):
                t = Q.do("dve", lambda e: e.max(T8[:, 0:8], WK[:, :]), t)
                if i < CAP // 8 - 1:
                    t = Q.do("dve", lambda e: e.match_replace(out=WK[:, :], in_to_replace=T8[:, 0:8],
                                                              in_values=WK[:, :], imm_value=-1.0), t,
                              t1)
            thr = T8[:, 7:8]
            t = Q.do("dve", lambda e: e.tensor_scalar(M1[:, :], LT[:, :], thr, None, ALU.is_gt, ALU.add,
                                                      accum_out=T8[:, 8:9]), t, t1)
            t2 = Q.do("dve", lambda e: e.tensor_scalar(M2[:, :], LT[:, :], thr, None, ALU.is_equal), t)
            t3 = Q.do("dve", lambda e: e.tensor_scalar(T8[:, 9:10], T8[:, 8:9], -1.0, float(CAP), ALU.mult, ALU.add), t)
            t = Q.do("dve", lambda e: e.tensor_tensor_scan(M3[:, :], ON[:, :], M2[:, :], 0.0, ALU.mult, ALU.add), t2, t_on)
            t = Q.do("dve", lambda e: e.scalar_tensor_tensor(out=M2[:, :], in0=M3[:, :], scalar=T8[:, 9:10],
                                                             in1=M2[:, :], op0=ALU.is_le, op1=ALU.mult), t, t3)
            t = Q.do("dve", lambda e: e.tensor_tensor(M1[:, :], M1[:, :], M2[:, :], ALU.add), t)
            t = Q.do("dve", lambda e: e.tensor_tensor_scan(M3[:, :], ON[:, :], M1[:, :], 0.0, ALU.mult, ALU.add), t)
            t = Q.do("dve", lambda e: e.tensor_tensor(M3[:, :], M3[:, :], M1[:, :], ALU.mult), t)
            b, bank, w = banks.claim()
            for j in range(4):
                tt = Q.do("pe", lambda e, j=j, bank=bank: e.transpose(bank[:, 16 * j:16 * j + 16],
                                                                     M3[:, 128 * j:128 * j + 128], ident[0:16, 0:16]),
                          w if j == 0 else [], t)
            t_po = Q.do("dve", lambda e, bank=bank: e.tensor_copy(PO[:, :], bank[:, 0:64]), tt, start)
            banks.release(b, t_po)
            pa.close()

            start2 = Q.now()
            XS = [sb(f"XS{i}", [128, DC, 256], F, px) for i in range(2)]
            PE = sb("PE", [128, 4, 256], R, px)
            GT = [sb(f"GT{i}", [128, T], F, px) for i in range(2)]
            SG = sb("SG", [128, D], F, px)
            HT = sb("HT", [128, DC, 128], F, px)
            xs_t, xs_r = [[], []], [list(start2), list(start2)]
            pe_r, gt_r, gt_t = list(start2), [list(start2), list(start2)], [None, None]
            one_t = [None]

            def one_hot(q):
                io = cst("iota", 0, 64).unsqueeze(1).unsqueeze(1).to_broadcast([128, 4, 4, CAP])
                po = PO[:, :].rearrange("p (t e) -> p t e", t=4)[:, :, 4 * q:4 * q + 4].unsqueeze(3)
                one_t[0] = Q.do("dve", lambda e: e.tensor_tensor(
                    PE[:, :, :].rearrange("p t (e c) -> p t e c", e=4), io, po.to_broadcast([128, 4, 4, CAP]),
                    ALU.is_equal), t_po, pe_r)

            def gather(q, d):
                z = q % 2
                b, bank, w = banks.claim()
                Q.wait("pe", w, xn_t, one_t[0])
                for tc in range(4):
                    for P in (XNH, XNL):
                        f = lambda e, tc=tc, P=P: e.matmul(
                            bank[:, 0:256], P[:, tc, 128 * d:128 * d + 128], PE[:, tc, :],
                            start=(tc == 0 and P is XNH), stop=(tc == 3 and P is XNL))
                        tok = Q.do("pe", f) if (tc == 3 and P is XNL) else Q.raw("pe", f)
                t = Q.do("dve", lambda e: e.tensor_copy(XS[z][:, d, :], bank[:, 0:256]), tok, xs_r[z])
                banks.release(b, t)
                xs_t[z] = (xs_t[z] if d else []) + [t]
                pe_r[:] = [tok]

            def places(q):
                af = AF[:, :].rearrange("p (t e) -> p t e", t=4)[:, :, 4 * q:4 * q + 4].unsqueeze(3)
                GG = HT[:, :, :].rearrange("p (t a) c -> p t (a c)", t=4)
                split = lambda a: a.rearrange("p t (e c) -> p t e c", e=4)
                t = Q.do("dve", lambda e: e.tensor_tensor(split(GG), split(PE[:, :, :].bitcast(F)),
                                                          af.to_broadcast([128, 4, 4, CAP]), ALU.mult), pe_r, ht_r)
                pe_r[:] = [t]
                for j in range(2):
                    b, bank, w = banks.claim()
                    for tc in range(4):
                        tt = Q.do("pe", lambda e, tc=tc, j=j, bank=bank: e.transpose(
                            bank[:, 128 * tc:128 * tc + 128], GG[:, tc, 128 * j:128 * j + 128], ident),
                            w if tc == 0 else [], t)
                    gt_t[j] = Q.do("act", lambda e, j=j, bank=bank: e.activation(GT[j][:, :], bank, ACT.Copy), tt, gt_r[j])
                    banks.release(b, gt_t[j])
                ht_r[:] = [tt]

            sg_r, ht_r = list(start2), list(start2)
            at = [0]

            def take():
                i = at[0]
                at[0] += 1
                return i, slots[i][0], slots[i][1]

            def drop(i, tok):
                if i + NSLOT < len(loads):
                    load(i + NSLOT, tok)

            for i in range(8):
                hb = [banks.claim() for _ in range(4)]
                if i == 0:
                    one_hot(0)
                    gather(0, 0)
                    gather(0, 1)
                elif i % 2 and i < 7:
                    one_hot(i // 2 + 1)
                z = (i // 2) % 2
                Q.wait("pe", *[h[2] for h in hb])
                for k in range(8):
                    if i == 0 and k + 2 < 8:
                        gather(0, k + 2)
                    if i % 2 and i < 7:
                        gather(i // 2 + 1, k)
                    Q.wait("pe", xs_t[z][k])
                    two = [take(), take()]
                    Q.wait("pe", two[0][2], two[1][2])
                    for n in range(4):
                        for e2 in range(2):
                            s = two[e2][1]
                            tok = Q.do("pe", lambda e, n=n, e2=e2, s=s, k=k, i=i, z=z, bank=hb[n][1]: e.matmul(
                                bank[64 * e2:64 * e2 + 64, :], XS[z][:, k, (2 * (i % 2) + e2) * 64:(2 * (i % 2) + e2) * 64 + 64],
                                s[:, 512 * n:512 * n + 512], start=(k == 0), stop=(k == 7)))
                    drop(two[0][0], tok)
                    drop(two[1][0], tok)
                xs_r[z] = [tok]
                ht_t = []
                for n in range(2):
                    t = Q.do("act", lambda e, n=n, bank=hb[n][1]: e.activation(SG[:, 512 * n:512 * n + 512], bank, ACT.Silu), tok, sg_r)
                    banks.release(hb[n][0], t)
                    t = Q.do("dve", lambda e, n=n, bank=hb[2 + n][1]: e.tensor_tensor(
                        SG[:, 512 * n:512 * n + 512], SG[:, 512 * n:512 * n + 512], bank, ALU.mult), t, tok)
                    banks.release(hb[2 + n][0], t)
                    ht_t.append(t)
                if i % 2 == 0:
                    places(i // 2)
                if i == 0:
                    for c in range(DC):
                        t = Q.do("dve", lambda e, c=c: e.tensor_scalar(X[:, c, :], X[:, c, :], ALPHA, None, ALU.mult),
                                 xt[c], xr[c], start2)
                        xt[c], xr[c] = [t], []
                tts = []
                for half in range(2):
                    tt, tv = turned(HT[:, 4 * half:4 * half + 4, :], SG[:, 512 * half:512 * half + 512], 4,
                                    ht_t[half], ht_r)
                    tts.append(tv)
                sg_r = [tt]
                yb = [banks.claim() for _ in range(2)]
                Q.wait("pe", *[y[2] for y in yb], tts)
                for k in range(4):
                    two = [take(), take()]
                    Q.wait("pe", two[0][2], two[1][2])
                    for a in range(2):
                        for n in range(2):
                            for e2 in range(2):
                                s = two[e2][1]
                                tok = Q.do("pe", lambda e, n=n, e2=e2, s=s, k=k, a=a, bank=yb[n][1]: e.matmul(
                                    bank[64 * e2:64 * e2 + 64, :], HT[:, 2 * k + a, 64 * e2:64 * e2 + 64],
                                    s[:, 1024 * a + 512 * n:1024 * a + 512 * n + 512], start=(k == 0 and a == 0),
                                    stop=(k == 3 and a == 1)))
                    drop(two[0][0], tok)
                    drop(two[1][0], tok)
                ht_r = [tok]
                ty = []
                for n in range(2):
                    t = Q.do("act", lambda e, n=n, bank=yb[n][1]: e.activation(SG[:, 512 * n:512 * n + 512], bank, ACT.Copy), tok, sg_r)
                    banks.release(yb[n][0], t)
                    ty.append(t)
                for d in range(DC):
                    b, bank, w = banks.claim()
                    tok = Q.do("pe", lambda e, d=d, bank=bank, i=i: e.matmul(bank, SG[:, 128 * d:128 * d + 128], GT[i % 2][:, :],
                                                                            start=True, stop=True), w, ty, gt_t[i % 2])
                    add_x(d, b, bank, tok)
                    if i == 7:
                        mean_part(d, 5)
                sg_r, gt_r[i % 2] = [tok], [tok]
            px.close()

        experts()
        outs = []

        def store(c):
            outs.append(Q.dma("sp", OUT[c], X[:, c, :], d_out, xt[c]))

        layer_norm("l2g", "l2b", 5, done=store)
        Q.wait("sp", outs[-1])


        engines = (("sync", "sp"), ("gpsimd", "pool"), ("scalar", "act"), ("vector", "dve"), ("tensor", "pe"))
        with nc.Block() as block:
            def body(key):
                def run(e):
                    for f in Q.q[key]:
                        f(e)
                return run
            block.sync(body("sp"))
            block.gpsimd(body("pool"))
            block.scalar(body("act"))
            block.vector(body("dve"))
            block.tensor(body("pe"))
    return rec
def _consts():
    c = np.zeros((128, NCST), np.float32)
    i = np.arange(128)

    def put(n, a):
        c[:, CST[n]:CST[n] + a.shape[1]] = a

    put("ident", np.eye(128, dtype=np.float32))
    put("ones", np.ones((128, 128), np.float32))
    put("bones", (i[:, None] // 64 == i[None, :] // 64).astype(np.float32))
    put("anti", np.eye(128, dtype=np.float32)[::-1])
    put("tri", (i[:, None] >= i[None, :]).astype(np.float32))
    put("nmask", np.where(i[:, None] < i[None, :], 0.0, -1e30).astype(np.float32))
    sw = np.zeros((128, 128), np.float32)
    sw[i[1::2], i[0::2]] = -1.0
    sw[i[0::2], i[1::2]] = 1.0
    put("swap", sw)
    t = np.arange(T)
    half = 32
    inv = (np.float32(10000.0) ** (-np.arange(0, half, 2, dtype=np.float32) / np.float32(half))).astype(np.float32)
    ang = np.concatenate([(t // 64).astype(np.float32)[:, None] * inv, (t % 64).astype(np.float32)[:, None] * inv], 1)
    ang = ang[:, (i % 64) // 2].T
    put("cos", np.cos(ang).astype(np.float32))
    put("sin", np.sin(ang).astype(np.float32))
    for n, cb in enumerate((0, 1, 3)):
        bs = min(max(cb * 16 - 8, 0), 32)
        col = cb * 16 + i % 16
        st = np.clip(col - 8, 0, 48)
        kc = bs + np.arange(256) % 32
        m = (kc[None, :] >= st[:, None]) & (kc[None, :] < st[:, None] + 16)
        c[:, CST["mask"] + 256 * n:CST["mask"] + 256 * n + 256] = np.where(m, 0.0, -1e30)
    put("iota", np.tile(np.arange(1, 65, dtype=np.float32), (128, 1)))
    return c


def _tiles(w):
    k, n = w.shape
    return np.ascontiguousarray(w.reshape(k // 128, 128, n // 128, 128).transpose(2, 1, 0, 3))


def _layout(a):
    f = {k: np.asarray(v) for k, v in a.items()}
    col = lambda v: np.ascontiguousarray(v.reshape(-1, 128).T)
    vec = np.zeros((128, NVEC), np.float32)

    def put(n, v):
        vec[:, VEC[n]:VEC[n] + v.shape[1]] = v

    put("gmix", col(f["norm_mix_g"]))
    put("gffn", col(f["norm_ffn_g"]))
    put("gfin", col(f["final_g"]))
    put("cw", col(f["a_conv_w"]))
    put("cb", col(f["a_conv_b"]))
    put("br", col(f["a_b_r"]))
    put("bi", col(f["a_b_i"]))
    put("lam", col(f["a_lambda"]))
    put("bg", col(f["b_gate_2"]))
    put("qg", np.concatenate([f["gqa_q_gain_2"]] * 2, 1).T)
    put("kg", np.concatenate([f["gqa_k_gain_2"]] * 2, 1).T)
    put("l1g", col(f["ln1_g_2"]))
    put("l1b", col(f["ln1_b_2"]))
    put("l2g", col(f["ln2_g_2"]))
    put("l2b", col(f["ln2_b_2"]))
    vec[:, VEC["eps"]] = RMS_EPS
    vec[:, VEC["eps"] + 1] = LN_EPS
    rows = lambda m: np.ascontiguousarray(m.T.reshape(-1, 128, m.shape[0]).transpose(1, 0, 2))
    heads = np.array([0, 4, 1, 5, 2, 6, 3, 7])
    order = (heads[:, None] * 64 + np.arange(64)).ravel()
    w2 = f["w_in_2"][0]
    w2 = np.concatenate([w2[:, :1536], w2[:, 1536 + order], w2[:, 2048:]], 1)
    wb = f["w_branch_2"][0].copy()
    wb[1] = wb[1][order]
    wr, wi = f["a_w_r"][0], f["a_w_i"][0]
    wri = np.stack([np.stack([_tiles(w[n]) for w in (wr, wi)]) for n in range(4)])
    wri = np.ascontiguousarray(wri.transpose(0, 3, 1, 2, 4, 5).reshape(4, 128, 8, 128))
    wd = f["ffn_w_down"]
    rpb = np.zeros(16 + 8 * 465 + 32, np.float32)
    rpb[16:16 + 3720] = f["na_rpb_2"].reshape(-1)
    return {
        "x": rows(f["x"][0]),
        "mem": rows(f["mem_2"][0]),
        "vec": vec,
        "cst": _consts(),
        "win": _tiles(f["a_w_in"][0]),
        "wri": wri,
        "wout": _tiles(f["a_w_out"][0]),
        "wg": np.stack([_tiles(w) for w in f["ffn_w_gate"]]),
        "wu": np.stack([_tiles(w) for w in f["ffn_w_up"]]),
        "wd": np.stack([np.stack([_tiles(w[:1408]), _tiles(w[1408:])]) for w in wd]),
        "wqkv": _tiles(f["b_w_qkv"][0]),
        "wbo": _tiles(f["b_w_out"][0]),
        "w2": _tiles(w2),
        "wmkv": _tiles(f["w_mem_kv_2"][0]),
        "wbr": np.stack([_tiles(w) for w in wb]),
        "w2o": _tiles(f["w_out_2"][0]),
        "rpb": rpb,
        "wrt": np.ascontiguousarray(f["w_router_2"][0].reshape(8, 128, 16).transpose(1, 0, 2)),
        "wgu": np.ascontiguousarray(f["w_gate_up_2"][0]),
        "wdn": np.ascontiguousarray(f["w_down_2"][0]),
    }


def _build(nc, arrays, plan):
    aps = {n: nc.dram_tensor(f"in_{n}_dram", a.shape, mybir.dt.from_np(a.dtype), kind="ExternalInput").ap()
           for n, a in arrays.items()}
    out = nc.dram_tensor("out_dram", (DC, 128, T), F, kind="ExternalOutput").ap()
    return program(nc, aps, out, plan)


def kernel(**inputs):
    import concourse.bacc as _bacc
    from concourse.bass_utils import run_bass_kernel_spmd as _run

    arrays = _layout(inputs)
    plan = _build(_bacc.Bacc("TRN2", target_bir_lowering=False, num_devices=1), arrays, None)
    nc = _bacc.Bacc("TRN2", target_bir_lowering=False, num_devices=1)
    _build(nc, arrays, plan)
    r = _run(nc, [{f"in_{n}_dram": a for n, a in arrays.items()}], core_ids=[0])
    got = r.results[0]["out_dram"]
    return np.ascontiguousarray(got.reshape(D, T).T)[None]
```
